# Optimizing a Trainium2 kernel written in Bass

```python
import jax, jax.numpy as jnp
from jax import lax
import numpy as np
import math
import jax
import jax.numpy as jnp

D_MODEL = 1024
BATCH = 1
SEQ = 512
DEPTH = 2

HEAD_DIM = 64
ROT_DIM = HEAD_DIM // 4
ROPE_THETA = 500000.0
A_HEADS = (D_MODEL // 2) // (2 * HEAD_DIM)
B_HEADS = (D_MODEL // 2) // HEAD_DIM
KV_LORA = D_MODEL // 4
IDX_HEADS = 4
IDX_DIM = 64
TOPK_MAX = 256
QBLOCK = 128
C_WIDTH = D_MODEL // 2
CONV_W = 3
POOL_WINDOWS = (2, 4, 8, 16)
POOL_WIDTH = D_MODEL // 2
POOL_GROUP = POOL_WIDTH // len(POOL_WINDOWS)
MEM_LEN = 256
X_HEADS = 4
X_HEAD_DIM = D_MODEL // 8
D_FF = 4 * D_MODEL
EPS = 1e-6
N_EVEN = (DEPTH + 1) // 2
N_ODD = DEPTH // 2
EVEN_SPLITS = (A_HEADS * 2 * HEAD_DIM, A_HEADS * 2 * HEAD_DIM, A_HEADS * 2 * HEAD_DIM,
               B_HEADS * HEAD_DIM, KV_LORA, IDX_HEADS * IDX_DIM, IDX_DIM, IDX_HEADS)
EVEN_IN = sum(EVEN_SPLITS)
ODD_SPLITS = (C_WIDTH, C_WIDTH, C_WIDTH, POOL_WIDTH)
ODD_IN = sum(ODD_SPLITS)


def rmsnorm(x, g):
    xf = x.astype(jnp.float32)
    y = xf * lax.rsqrt(jnp.mean(xf * xf, axis=-1, keepdims=True) + EPS)
    return (y * g.astype(jnp.float32)).astype(x.dtype)

def _split(a, sizes):
    return jnp.split(a, np.cumsum(sizes)[:-1].tolist(), axis=-1)

def rope_tables(positions):
    inv = ROPE_THETA ** (-jnp.arange(0, ROT_DIM, 2, dtype=jnp.float32) / ROT_DIM)
    ang = positions.astype(jnp.float32)[..., None] * inv
    return jnp.cos(ang)[:, :, None, :], jnp.sin(ang)[:, :, None, :]

def rope(x, cos, sin):
    half = ROT_DIM // 2
    xr, xp = x[..., :ROT_DIM], x[..., ROT_DIM:]
    x1, x2 = xr[..., :half], xr[..., half:]
    rot = jnp.concatenate([x1 * cos - x2 * sin, x2 * cos + x1 * sin], axis=-1)
    return jnp.concatenate([rot.astype(x.dtype), xp], axis=-1)

def even_mixer(h, cos, sin, w_in, gq_a, gk_a, lam, lam_init, g_sub_a,
               g_kv_b, w_kv_up_b, gq_b, gk_b, g_kidx, w_out, k_sel):
    B, S, _ = h.shape
    nb = S // QBLOCK

    def to_blocks(a):
        return jnp.moveaxis(a.reshape((B, nb, QBLOCK) + a.shape[2:]), 1, 0)

    def from_blocks(o):
        return jnp.moveaxis(o, 0, 1).reshape((B, S) + o.shape[3:])

    qa, ka, va, qb, ckv, qi, ki, wi = _split(h @ w_in, EVEN_SPLITS)

    qa = rope(rmsnorm(qa.reshape(B, S, 2 * A_HEADS, HEAD_DIM), gq_a), cos, sin)
    qa = qa.reshape(B, S, A_HEADS, 2, HEAD_DIM)
    ka = rope(rmsnorm(ka.reshape(B, S, 2 * A_HEADS, HEAD_DIM), gk_a), cos, sin)
    ka = ka.reshape(B, S, A_HEADS, 2, HEAD_DIM)
    va = va.reshape(B, S, A_HEADS, 2 * HEAD_DIM)

    kb, vb = jnp.split(rmsnorm(ckv, g_kv_b) @ w_kv_up_b, 2, axis=-1)
    qb = rope(rmsnorm(qb.reshape(B, S, B_HEADS, HEAD_DIM), gq_b), cos, sin)
    kb = rope(rmsnorm(kb.reshape(B, S, B_HEADS, HEAD_DIM), gk_b), cos, sin)
    vb = vb.reshape(B, S, B_HEADS, HEAD_DIM)
    qi = rope(qi.reshape(B, S, IDX_HEADS, IDX_DIM), cos, sin)
    ki = rope(rmsnorm(ki, g_kidx)[:, :, None, :], cos, sin)[:, :, 0, :]
    wi = wi.astype(jnp.float32) * (IDX_HEADS ** -0.5 * IDX_DIM ** -0.5)

    kpos = jnp.arange(S)
    scale = HEAD_DIM ** -0.5

    def a_block(args):
        q, t0 = args
        qpos = t0 + jnp.arange(QBLOCK)
        causal = kpos[None, :] <= qpos[:, None]
        logits = jnp.einsum('bqhcd,bkhcd->bhcqk', q, ka).astype(jnp.float32) * scale
        p = jax.nn.softmax(jnp.where(causal, logits, -jnp.inf), axis=-1)
        attn = p[:, :, 0] - lam * p[:, :, 1]
        return jnp.einsum('bhqk,bkhe->bqhe', attn.astype(va.dtype), va)

    def b_block(args):
        q, qidx, widx, t0 = args
        qpos = t0 + jnp.arange(QBLOCK)
        causal = kpos[None, :] <= qpos[:, None]
        isc = jax.nn.relu(jnp.einsum('bqhd,bkd->bqhk', qidx, ki).astype(jnp.float32))
        isc = jnp.einsum('bqhk,bqh->bqk', isc, widx)
        isc = jnp.where(causal[None], isc, -jnp.inf)
        _, idx = lax.top_k(isc, k_sel)
        k_g = jax.vmap(lambda a, i: a[i])(kb, idx)
        v_g = jax.vmap(lambda a, i: a[i])(vb, idx)
        logits = jnp.einsum('bqhd,bqkhd->bhqk', q, k_g).astype(jnp.float32) * scale
        valid = (idx <= qpos[None, :, None])[:, None]
        p = jax.nn.softmax(jnp.where(valid, logits, -jnp.inf), axis=-1)
        return jnp.einsum('bhqk,bqkhd->bqhd', p.astype(vb.dtype), v_g)

    starts = jnp.arange(nb, dtype=jnp.int32) * QBLOCK
    out_a = from_blocks(lax.map(a_block, (to_blocks(qa), starts)))
    out_a = rmsnorm(out_a, g_sub_a) * (1.0 - lam_init)
    out_b = from_blocks(lax.map(b_block, (to_blocks(qb), to_blocks(qi), to_blocks(wi), starts)))
    y = jnp.concatenate([out_a.reshape(B, S, -1), out_b.reshape(B, S, -1)], axis=-1)
    return y @ w_out

def pool_mixer(z, w_pool, pool_scale):
    B, S, _ = z.shape
    zf = z.astype(jnp.float32).reshape(B, S, len(POOL_WINDOWS), POOL_GROUP)
    csp = jnp.pad(jnp.cumsum(zf, axis=1), ((0, 0), (1, 0), (0, 0), (0, 0)))
    t = jnp.arange(S)
    outs = []
    for g, w in enumerate(POOL_WINDOWS):
        lo = jnp.maximum(t + 1 - w, 0)
        win_sum = csp[:, 1:, g] - csp[:, lo, g]
        cnt = jnp.minimum(t + 1, w).astype(jnp.float32)
        outs.append(win_sum / cnt[None, :, None] - zf[:, :, g])
    pooled = jnp.stack(outs, axis=2).astype(z.dtype)
    y = jnp.einsum('bsgc,gcd->bsgd', pooled, w_pool).reshape(B, S, POOL_WIDTH)
    return y * pool_scale

def odd_mixer(h, w_in, conv_w, w_pool, pool_scale, w_out):
    gb, gc, hc, zd = _split(h @ w_in, ODD_SPLITS)
    u = gc * hc
    conv = lax.conv_general_dilated(
        u, conv_w[:, None, :].astype(u.dtype), window_strides=(1,),
        padding=[(CONV_W - 1, 0)], dimension_numbers=('NWC', 'WIO', 'NWC'),
        feature_group_count=C_WIDTH)
    yc = gb * conv
    yd = pool_mixer(zd, w_pool, pool_scale)
    return jnp.concatenate([yc, yd], axis=-1) @ w_out

def cross_attn(h, m, wq, wkv, gq, gk, wo):
    B, S, _ = h.shape
    q = rmsnorm((h @ wq).reshape(B, S, X_HEADS, X_HEAD_DIM), gq)
    k, v = jnp.split(m @ wkv, 2, axis=-1)
    k = rmsnorm(k.reshape(B, -1, X_HEADS, X_HEAD_DIM), gk)
    v = v.reshape(B, -1, X_HEADS, X_HEAD_DIM)
    logits = jnp.einsum('bqhd,bkhd->bhqk', q, k).astype(jnp.float32) * X_HEAD_DIM ** -0.5
    p = jax.nn.softmax(logits, axis=-1)
    o = jnp.einsum('bhqk,bkhd->bqhd', p.astype(v.dtype), v).reshape(B, S, -1)
    return o @ wo

def mlp(h, w_up, w_down):
    return jnp.square(jax.nn.relu(h @ w_up)) @ w_down

def first_inputs(seed: int = 0) -> dict:
    key = jax.random.key(seed)
    ks = iter(jax.random.split(key, 48))

    def nrm(shape, scale):
        return scale * jax.random.normal(next(ks), shape, jnp.float32)

    def gain(shape):
        return 1.0 + 0.05 * jax.random.normal(next(ks), shape, jnp.float32)

    d = D_MODEL
    return {
        'x': nrm((BATCH, SEQ, d), 1.0),
        'mem': nrm((BATCH, MEM_LEN, d), 1.0),
        'positions': jnp.tile(jnp.arange(SEQ, dtype=jnp.int32)[None, :], (BATCH, 1)),
        'g_mix': gain((DEPTH, d)),
        'g_xattn': gain((DEPTH, d)),
        'g_mem': gain((DEPTH, d)),
        'g_mlp': gain((DEPTH, d)),
        'wq_x': nrm((DEPTH, d, X_HEADS * X_HEAD_DIM), d ** -0.5),
        'wkv_x': nrm((DEPTH, d, 2 * X_HEADS * X_HEAD_DIM), d ** -0.5),
        'gq_x': gain((DEPTH, X_HEAD_DIM)),
        'gk_x': gain((DEPTH, X_HEAD_DIM)),
        'wo_x': nrm((DEPTH, X_HEADS * X_HEAD_DIM, d), (X_HEADS * X_HEAD_DIM) ** -0.5),
        'w_up': nrm((DEPTH, d, D_FF), d ** -0.5),
        'w_down': nrm((DEPTH, D_FF, d), D_FF ** -0.5),
        'w_in_e': nrm((N_EVEN, d, EVEN_IN), d ** -0.5),
        'gq_a': gain((N_EVEN, HEAD_DIM)),
        'gk_a': gain((N_EVEN, HEAD_DIM)),
        'lam_q1': nrm((N_EVEN, HEAD_DIM), 0.1),
        'lam_k1': nrm((N_EVEN, HEAD_DIM), 0.1),
        'lam_q2': nrm((N_EVEN, HEAD_DIM), 0.1),
        'lam_k2': nrm((N_EVEN, HEAD_DIM), 0.1),
        'g_sub_a': gain((N_EVEN, 2 * HEAD_DIM)),
        'g_kv_b': gain((N_EVEN, KV_LORA)),
        'w_kv_up_b': nrm((N_EVEN, KV_LORA, 2 * B_HEADS * HEAD_DIM), KV_LORA ** -0.5),
        'gq_b': gain((N_EVEN, HEAD_DIM)),
        'gk_b': gain((N_EVEN, HEAD_DIM)),
        'g_kidx': gain((N_EVEN, IDX_DIM)),
        'w_out_e': nrm((N_EVEN, d, d), d ** -0.5),
        'w_in_o': nrm((N_ODD, d, ODD_IN), d ** -0.5),
        'conv_w': nrm((N_ODD, CONV_W, C_WIDTH), CONV_W ** -0.5),
        'w_pool': nrm((N_ODD, len(POOL_WINDOWS), POOL_GROUP, POOL_GROUP), POOL_GROUP ** -0.5),
        'pool_scale': gain((N_ODD, POOL_WIDTH)),
        'w_out_o': nrm((N_ODD, d, d), d ** -0.5),
    }

def first_block(x, mem, positions, g_mix, g_xattn, g_mem, g_mlp, wq_x, wkv_x, gq_x, gk_x,
              wo_x, w_up, w_down, w_in_e, gq_a, gk_a, lam_q1, lam_k1, lam_q2, lam_k2,
              g_sub_a, g_kv_b, w_kv_up_b, gq_b, gk_b, g_kidx, w_out_e, w_in_o, conv_w,
              w_pool, pool_scale, w_out_o):
    S = x.shape[1]
    k_sel = min(TOPK_MAX, S // 4)
    cos, sin = rope_tables(positions)
    for i in range(DEPTH):
        j = i // 2
        h = rmsnorm(x, g_mix[i])
        if i % 2 == 0:
            lam_init = 0.8 - 0.6 * float(np.exp(-0.3 * i))
            f32 = jnp.float32
            lam = (jnp.exp(jnp.sum(lam_q1[j].astype(f32) * lam_k1[j].astype(f32)))
                   - jnp.exp(jnp.sum(lam_q2[j].astype(f32) * lam_k2[j].astype(f32)))
                   + lam_init)
            mix = even_mixer(h, cos, sin, w_in_e[j], gq_a[j], gk_a[j], lam, lam_init,
                             g_sub_a[j], g_kv_b[j], w_kv_up_b[j], gq_b[j], gk_b[j],
                             g_kidx[j], w_out_e[j], k_sel)
        else:
            mix = odd_mixer(h, w_in_o[j], conv_w[j], w_pool[j], pool_scale[j], w_out_o[j])
        x = x + mix
        x = x + cross_attn(rmsnorm(x, g_xattn[i]), rmsnorm(mem, g_mem[i]),
                           wq_x[i], wkv_x[i], gq_x[i], gk_x[i], wo_x[i])
        x = x + mlp(rmsnorm(x, g_mlp[i]), w_up[i], w_down[i])
    return x


DEPTH_2 = 1

MIX_WIDTH = D_MODEL
MLSTM_WIDTH = MIX_WIDTH // 2
ATTN_WIDTH = MIX_WIDTH - MLSTM_WIDTH
MLSTM_HEADS = 4
MLSTM_HEAD_DIM = MLSTM_WIDTH // MLSTM_HEADS
MLSTM_QKV_BLOCK = 4
MLSTM_CONV = 5
MLSTM_CHUNK = 64
ATTN_HEAD_DIM = 64
ATTN_HEADS = ATTN_WIDTH // ATTN_HEAD_DIM
DILATED_PATTERNS = ((128, 1), (512, 4), (2048, 16))
ATTN_BLOCK = 64
REL_BUCKETS = 32
REL_MAX_DIST = 1024
N_EXPERTS = 16
EC_CAPACITY_FACTOR = 2
D_FF_EXPERT = 2 * D_MODEL
NORM_EPS = 1e-6
N_MOD = 6
PROJ_WIDTHS = (MLSTM_WIDTH, MLSTM_WIDTH, MLSTM_HEADS, MLSTM_HEADS, MLSTM_HEADS, MLSTM_HEADS,
               ATTN_WIDTH, ATTN_WIDTH, ATTN_WIDTH)
PROJ_TOTAL = sum(PROJ_WIDTHS)


def rms_norm(x, g):
    xf = x.astype(jnp.float32)
    y = xf * lax.rsqrt(jnp.mean(xf * xf, axis=-1, keepdims=True) + NORM_EPS)
    return (y * g.astype(jnp.float32)).astype(x.dtype)

def t5_bucket(rel):
    half = REL_BUCKETS // 2
    exact = half // 2
    n = jnp.abs(rel)
    log_ratio = jnp.log(jnp.maximum(n, 1).astype(jnp.float32) / exact) / math.log(REL_MAX_DIST / exact)
    large = jnp.minimum(exact + (log_ratio * (half - exact)).astype(jnp.int32), half - 1)
    return jnp.where(rel > 0, half, 0) + jnp.where(n < exact, n, large)

def dilated_window_attention(q, k, v, rel_bias, window, dilation):
    B, S, H, E = q.shape
    half = window // (2 * dilation)
    L = S // dilation
    nb = -(-L // ATTN_BLOCK)
    pad = nb * ATTN_BLOCK - L

    def phases(t):
        return t.reshape(B, L, dilation, H, E).transpose(0, 2, 3, 1, 4).reshape(B * dilation, H, L, E)

    qb = jnp.pad(phases(q), ((0, 0), (0, 0), (0, pad), (0, 0))).reshape(B * dilation, H, nb, ATTN_BLOCK, E)

    def key_blocks(t):
        tp = jnp.pad(phases(t), ((0, 0), (0, 0), (ATTN_BLOCK, pad + ATTN_BLOCK), (0, 0)))
        tp = tp.reshape(B * dilation, H, nb + 2, ATTN_BLOCK, E)
        return jnp.concatenate([tp[:, :, 0:nb], tp[:, :, 1:nb + 1], tp[:, :, 2:nb + 2]], axis=3)

    kb, vb = key_blocks(k), key_blocks(v)
    qi = jnp.arange(ATTN_BLOCK)[:, None]
    kj = jnp.arange(3 * ATTN_BLOCK)[None, :] - ATTN_BLOCK
    rel = kj - qi
    key_pos = jnp.arange(nb)[:, None] * ATTN_BLOCK + kj
    valid = (jnp.abs(rel) <= half)[None] & ((key_pos >= 0) & (key_pos < L))[:, None, :]
    bias = rel_bias[t5_bucket(rel * dilation)].transpose(2, 0, 1).astype(jnp.float32)
    logits = jnp.einsum('nhcqe,nhcke->nhcqk', qb, kb).astype(jnp.float32) / math.sqrt(E) + bias[:, None]
    logits = jnp.where(valid, logits, -jnp.inf)
    lse = jax.nn.logsumexp(logits, axis=-1)
    p = jnp.exp(logits - lse[..., None]).astype(v.dtype)
    o = jnp.einsum('nhcqk,nhcke->nhcqe', p, vb)
    o = o.reshape(B * dilation, H, nb * ATTN_BLOCK, E)[:, :, :L]
    o = o.reshape(B, dilation, H, L, E).transpose(0, 3, 1, 2, 4).reshape(B, S, H, E)
    lse = lse.reshape(B * dilation, H, nb * ATTN_BLOCK)[:, :, :L]
    lse = lse.reshape(B, dilation, H, L).transpose(0, 3, 1, 2).reshape(B, S, H)
    return o, lse

def dilated_attention_mixer(a_q, a_k, a_v, q_norm_g, k_norm_g, rel_bias):
    B, S, _ = a_q.shape
    heads = lambda t: t.reshape(B, S, ATTN_HEADS, ATTN_HEAD_DIM)
    q = rms_norm(heads(a_q), q_norm_g)
    k = rms_norm(heads(a_k), k_norm_g)
    v = heads(a_v)
    outs, lses = zip(*[dilated_window_attention(q, k, v, rel_bias, w, d) for w, d in DILATED_PATTERNS])
    weights = jax.nn.softmax(jnp.stack(lses), axis=0)
    o = jnp.sum(weights[..., None] * jnp.stack(outs).astype(jnp.float32), axis=0)
    return o.reshape(B, S, ATTN_WIDTH).astype(a_q.dtype)

def mlstm_chunkwise(q, k, v, i_pre, log_f):
    B, H, S, E = q.shape
    NC = S // MLSTM_CHUNK
    ch = lambda t: t.reshape((B, H, NC, MLSTM_CHUNK) + t.shape[3:])
    q, k, v, i_pre, log_f = ch(q), ch(k), ch(v), ch(i_pre), ch(log_f)
    b = jnp.cumsum(log_f, axis=-1)
    g = b[..., -1]
    a = g[..., None] - b + i_pre

    def step(carry, xs):
        C, n, m = carry
        kc, vc, ac, gc = xs
        m_new = jnp.maximum(gc + m, jnp.max(ac, axis=-1))
        w = jnp.exp(ac - m_new[..., None])
        decay = jnp.exp(gc + m - m_new)
        C_new = decay[..., None, None] * C + jnp.einsum('bhl,bhld,bhle->bhde', w, kc, vc)
        n_new = decay[..., None] * n + jnp.einsum('bhl,bhld->bhd', w, kc)
        return (C_new, n_new, m_new), (C, n, m)

    init = (jnp.zeros((B, H, E, E), jnp.float32), jnp.zeros((B, H, E), jnp.float32), jnp.zeros((B, H), jnp.float32))
    xs = tuple(jnp.moveaxis(t, 2, 0) for t in (k, v, a, g))
    _, (C_prev, n_prev, m_prev) = lax.scan(step, init, xs)
    C_prev = jnp.moveaxis(C_prev, 0, 2)
    n_prev = jnp.moveaxis(n_prev, 0, 2)
    m_prev = jnp.moveaxis(m_prev, 0, 2)

    lower = jnp.tril(jnp.ones((MLSTM_CHUNK, MLSTM_CHUNK), dtype=bool))
    D = jnp.where(lower, b[..., :, None] - b[..., None, :] + i_pre[..., None, :], -jnp.inf)
    inter = b + m_prev[..., None]
    m_t = jnp.maximum(inter, jnp.max(D, axis=-1))
    w_intra = jnp.exp(D - m_t[..., None]) * jnp.einsum('bhcte,bhcje->bhctj', q, k)
    w_inter = jnp.exp(inter - m_t)
    num = w_inter[..., None] * jnp.einsum('bhcte,bhced->bhctd', q, C_prev) + jnp.einsum('bhctj,bhcjd->bhctd', w_intra, v)
    den = w_inter * jnp.einsum('bhcte,bhce->bhct', q, n_prev) + jnp.sum(w_intra, axis=-1)
    h = num / jnp.maximum(jnp.abs(den), jnp.exp(-m_t))[..., None]
    return h.reshape(B, H, S, E)

def mlstm_mixer(x_m, o_pre, i_fw, f_fw, i_bw, f_bw, conv_w, conv_b, w_q_blk, w_k_blk, w_v_blk,
                b_igate, b_fgate, out_norm_g, skip):
    B, S, _ = x_m.shape
    xc = lax.conv_general_dilated(x_m, conv_w[:, None, :], window_strides=(1,),
                                  padding=((MLSTM_CONV // 2, MLSTM_CONV // 2),),
                                  dimension_numbers=('NWC', 'WIO', 'NWC'),
                                  feature_group_count=MLSTM_WIDTH) + conv_b
    xc = jax.nn.silu(xc)

    def blockdiag(t, w):
        y = jnp.einsum('bsgi,gij->bsgj', t.reshape(B, S, -1, MLSTM_QKV_BLOCK), w)
        return y.reshape(B, S, MLSTM_HEADS, MLSTM_HEAD_DIM).transpose(0, 2, 1, 3).astype(jnp.float32)

    q = blockdiag(xc, w_q_blk)
    k = blockdiag(xc, w_k_blk) / math.sqrt(MLSTM_HEAD_DIM)
    v = blockdiag(x_m, w_v_blk)
    gate = lambda t, bias: (t.astype(jnp.float32) + bias.astype(jnp.float32)).transpose(0, 2, 1)
    i_f, logf_f = gate(i_fw, b_igate[0]), jax.nn.log_sigmoid(gate(f_fw, b_fgate[0]))
    i_b, logf_b = gate(i_bw, b_igate[1]), jax.nn.log_sigmoid(gate(f_bw, b_fgate[1]))
    flip = lambda t: jnp.flip(t, axis=2)
    h_fwd = mlstm_chunkwise(q, k, v, i_f, logf_f)
    h_bwd = flip(mlstm_chunkwise(flip(q), flip(k), flip(v), flip(i_b), flip(logf_b)))
    h = (h_fwd + h_bwd).transpose(0, 2, 1, 3)
    h = h * lax.rsqrt(jnp.mean(h * h, axis=-1, keepdims=True) + NORM_EPS)
    h = h * out_norm_g.astype(jnp.float32).reshape(MLSTM_HEADS, MLSTM_HEAD_DIM)
    h = h.reshape(B, S, MLSTM_WIDTH).astype(x_m.dtype) + skip * xc
    return h * jax.nn.sigmoid(o_pre)

def expert_choice_ffn(h, w_router, b_router, w_gate, w_up, w_down):
    B, S, D = h.shape
    cap = (EC_CAPACITY_FACTOR * S) // N_EXPERTS
    logits = (h @ w_router + b_router).astype(jnp.float32)
    affinity = jax.nn.softmax(logits, axis=-1)
    gates, idx = lax.top_k(affinity.transpose(0, 2, 1), cap)
    bidx = jnp.arange(B)[:, None, None]
    xin = h[bidx, idx]
    hid = jax.nn.silu(jnp.einsum('becd,edf->becf', xin, w_gate)) * jnp.einsum('becd,edf->becf', xin, w_up)
    y = jnp.einsum('becf,efd->becd', hid, w_down) * gates[..., None].astype(h.dtype)
    return jnp.zeros_like(h).at[bidx, idx].add(y)

def second_inputs(seed: int = 0) -> dict:
    key = jax.random.key(seed)
    ks = jax.random.split(key, 26)
    f32 = jnp.float32
    nrm = lambda k, shape, scale: scale * jax.random.normal(k, shape, f32)
    L = DEPTH_2
    H = MLSTM_HEADS
    nblk = MLSTM_WIDTH // MLSTM_QKV_BLOCK
    return {
        "x": nrm(ks[0], (BATCH, SEQ, D_MODEL), 1.0),
        "c": nrm(ks[1], (BATCH, D_MODEL), 1.0),
        "w_ada": nrm(ks[2], (L, D_MODEL, N_MOD * D_MODEL), 0.5 * D_MODEL ** -0.5),
        "b_ada": nrm(ks[3], (L, N_MOD * D_MODEL), 0.02),
        "norm1_g": 1.0 + nrm(ks[4], (L, D_MODEL), 0.02),
        "w_in": nrm(ks[5], (L, D_MODEL, PROJ_TOTAL), D_MODEL ** -0.5),
        "conv_w": nrm(ks[6], (L, MLSTM_CONV, MLSTM_WIDTH), MLSTM_CONV ** -0.5),
        "conv_b": nrm(ks[7], (L, MLSTM_WIDTH), 0.02),
        "w_q_blk": nrm(ks[8], (L, nblk, MLSTM_QKV_BLOCK, MLSTM_QKV_BLOCK), MLSTM_QKV_BLOCK ** -0.5),
        "w_k_blk": nrm(ks[9], (L, nblk, MLSTM_QKV_BLOCK, MLSTM_QKV_BLOCK), MLSTM_QKV_BLOCK ** -0.5),
        "w_v_blk": nrm(ks[10], (L, nblk, MLSTM_QKV_BLOCK, MLSTM_QKV_BLOCK), MLSTM_QKV_BLOCK ** -0.5),
        "b_igate": nrm(ks[11], (L, 2, H), 0.1),
        "b_fgate": jnp.linspace(3.0, 6.0, H, dtype=f32)[None, None, :] + nrm(ks[12], (L, 2, H), 0.1),
        "mlstm_norm_g": 1.0 + nrm(ks[13], (L, MLSTM_WIDTH), 0.02),
        "mlstm_skip": 1.0 + nrm(ks[14], (L, MLSTM_WIDTH), 0.02),
        "q_norm_g": 1.0 + nrm(ks[15], (L, ATTN_HEAD_DIM), 0.02),
        "k_norm_g": 1.0 + nrm(ks[16], (L, ATTN_HEAD_DIM), 0.02),
        "rel_bias": nrm(ks[17], (REL_BUCKETS, ATTN_HEADS), 0.5),
        "w_out": nrm(ks[18], (L, MIX_WIDTH, D_MODEL), MIX_WIDTH ** -0.5),
        "norm2_g": 1.0 + nrm(ks[19], (L, D_MODEL), 0.02),
        "w_router": nrm(ks[20], (L, D_MODEL, N_EXPERTS), D_MODEL ** -0.5),
        "b_router": nrm(ks[21], (L, N_EXPERTS), 0.01),
        "w_gate": nrm(ks[22], (L, N_EXPERTS, D_MODEL, D_FF_EXPERT), D_MODEL ** -0.5),
        "w_up": nrm(ks[23], (L, N_EXPERTS, D_MODEL, D_FF_EXPERT), D_MODEL ** -0.5),
        "w_down": nrm(ks[24], (L, N_EXPERTS, D_FF_EXPERT, D_MODEL), D_FF_EXPERT ** -0.5),
    }

def second_block(x, c, w_ada, b_ada, norm1_g, w_in, conv_w, conv_b, w_q_blk, w_k_blk, w_v_blk,
              b_igate, b_fgate, mlstm_norm_g, mlstm_skip, q_norm_g, k_norm_g, rel_bias, w_out,
              norm2_g, w_router, b_router, w_gate, w_up, w_down):
    split_points = [int(s) for s in np.cumsum(PROJ_WIDTHS)[:-1]]
    for l in range(DEPTH_2):
        mod = jax.nn.silu(c) @ w_ada[l] + b_ada[l]
        shift1, scale1, gate1, shift2, scale2, gate2 = jnp.split(mod[:, None, :], N_MOD, axis=-1)

        h = rms_norm(x, norm1_g[l]) * (1.0 + scale1) + shift1
        proj = h @ w_in[l]
        x_m, o_pre, i_fw, f_fw, i_bw, f_bw, a_q, a_k, a_v = jnp.split(proj, split_points, axis=-1)
        y_mlstm = mlstm_mixer(x_m, o_pre, i_fw, f_fw, i_bw, f_bw, conv_w[l], conv_b[l], w_q_blk[l],
                              w_k_blk[l], w_v_blk[l], b_igate[l], b_fgate[l], mlstm_norm_g[l], mlstm_skip[l])
        y_attn = dilated_attention_mixer(a_q, a_k, a_v, q_norm_g[l], k_norm_g[l], rel_bias)
        mix = jnp.concatenate([y_mlstm, y_attn], axis=-1) @ w_out[l]
        x = x + gate1 * mix

        h2 = rms_norm(x, norm2_g[l]) * (1.0 + scale2) + shift2
        x = x + gate2 * expert_choice_ffn(h2, w_router[l], b_router[l], w_gate[l], w_up[l], w_down[l])
    return x


def setup_inputs(seed=0):
    out = dict(first_inputs(seed))
    for name, value in second_inputs(seed + 1).items():
        if name != "x":
            out[name + "_2"] = value
    return out


def reference(
    x, mem, positions, g_mix, g_xattn, g_mem, g_mlp, wq_x, wkv_x, gq_x, gk_x, wo_x, w_up,
    w_down, w_in_e, gq_a, gk_a, lam_q1, lam_k1, lam_q2, lam_k2, g_sub_a, g_kv_b, w_kv_up_b,
    gq_b, gk_b, g_kidx, w_out_e, w_in_o, conv_w, w_pool, pool_scale, w_out_o, c_2, w_ada_2,
    b_ada_2, norm1_g_2, w_in_2, conv_w_2, conv_b_2, w_q_blk_2, w_k_blk_2, w_v_blk_2, b_igate_2,
    b_fgate_2, mlstm_norm_g_2, mlstm_skip_2, q_norm_g_2, k_norm_g_2, rel_bias_2, w_out_2,
    norm2_g_2, w_router_2, b_router_2, w_gate_2, w_up_2, w_down_2,
):
    x = first_block(
        x, mem, positions, g_mix, g_xattn, g_mem, g_mlp, wq_x, wkv_x, gq_x, gk_x, wo_x, w_up,
        w_down, w_in_e, gq_a, gk_a, lam_q1, lam_k1, lam_q2, lam_k2, g_sub_a, g_kv_b, w_kv_up_b,
        gq_b, gk_b, g_kidx, w_out_e, w_in_o, conv_w, w_pool, pool_scale, w_out_o,
    )
    return second_block(
        x, c_2, w_ada_2, b_ada_2, norm1_g_2, w_in_2, conv_w_2, conv_b_2, w_q_blk_2, w_k_blk_2,
        w_v_blk_2, b_igate_2, b_fgate_2, mlstm_norm_g_2, mlstm_skip_2, q_norm_g_2, k_norm_g_2,
        rel_bias_2, w_out_2, norm2_g_2, w_router_2, b_router_2, w_gate_2, w_up_2, w_down_2,
    )


_drawn_inputs = setup_inputs


def setup_inputs(seed=0):
    import zlib

    import numpy as np

    out = dict(_drawn_inputs(seed))
    spreads = {}
    factors = {'g_xattn': 8.0,
     'g_mem': 5.953,
     'gq_x': 8.0,
     'gk_x': 8.0,
     'g_kv_b': 5.274,
     'gq_b': 8.0,
     'gk_b': 7.635,
     'g_kidx': 3.253,
     'pool_scale': 3.425,
     'b_ada_2': 6.75,
     'norm1_g_2': 8.0,
     'conv_b_2': 8.0,
     'b_igate_2': 171.256,
     'b_fgate_2': 3.873,
     'mlstm_norm_g_2': 64.0,
     'mlstm_skip_2': 8.0,
     'q_norm_g_2': 8.0,
     'k_norm_g_2': 8.0,
     'rel_bias_2': 8.0,
     'norm2_g_2': 8.0,
     'b_router_2': 22.88}
    for name, (base, spread) in spreads.items():
        noise = np.random.default_rng([zlib.crc32(name.encode()), seed]).standard_normal(out[name].shape)
        drawn = base * np.exp(spread * noise) if base else spread * noise
        out[name] = jnp.asarray(drawn.astype(out[name].dtype))
    for name, factor in factors.items():
        out[name] = (out[name] * factor).astype(out[name].dtype)
    return out
```

```python
from contextlib import ExitStack

import numpy as np
import concourse.bass as bass
from concourse import mybir

F32 = mybir.dt.float32
I32 = mybir.dt.int32
ACT = mybir.ActivationFunctionType
ALU = mybir.AluOpType
AX = mybir.AxisListType

P = 128
SEQ = 512
NT = SEQ // P
D = 1024
KD = D // P
BANK = 512
RING = 4
EPS = 1e-6
NEG = -1e30
MEM = 256
FF = 4096
EXPERTS = 16
CAP = 64
FE = 2048


class Counter:

    def __init__(self, g, name):
        self.g, self.name, self.base = g, name, g.totals.setdefault(name, 0)
        self.sem = g.sems[name] if name in g.sems else g.sems.setdefault(name, g.sem(name))

    def up(self):
        self.g.totals[self.name] += 1
        return self.sem

    def at(self, n):
        return self.sem, self.base + n


class Program:

    def __init__(self, nc, t, ctx):
        self.nc, self.t, self.ctx = nc, t, ctx
        self.sems, self.totals = {}, {}
        self.ring = self.sb("ring", [P, RING, KD * BANK])
        self.landed = [self.sem(f"weights_landed_{s}") for s in range(RING)]
        self.tiles_done = self.sem("tiles_done")
        self.tiles = 0
        self.done_at = []
        self.groups = []
        self.issued = 0
        self.taken = 0
        self.dve_sem = self.sem("dve_chain")
        self.act_sem = self.sem("act_chain")
        self.pool_sem = self.sem("pool_chain")
        self.dve_n = self.act_n = self.pool_n = 0
        self.psum = ctx.enter_context(nc.psum_tensor("banks", [P, 8, BANK], F32))

    def sb(self, name, shape, dt=F32, ctx=None):
        return (ctx or self.ctx).enter_context(self.nc.sbuf_tensor(name, shape, dt))

    def sem(self, name):
        return self.ctx.enter_context(self.nc.semaphore(name))

    def counter(self, name):
        return Counter(self, name)

    def vlink(self, ins):
        self.dve_n += 1
        ins.then_inc(self.dve_sem, 1)
        self.nc.vector.wait_ge(self.dve_sem, self.dve_n)

    def alink(self, ins):
        self.act_n += 1
        ins.then_inc(self.act_sem, 1)
        self.nc.scalar.wait_ge(self.act_sem, self.act_n)

    def plink(self, ins):
        self.pool_n += 1
        ins.then_inc(self.pool_sem, 1)
        self.nc.gpsimd.wait_ge(self.pool_sem, self.pool_n)

    def prefetch(self, sp, consumed):
        while self.issued < min(consumed + RING, len(self.groups)):
            g = self.issued
            if g >= RING:
                sp.wait_ge(self.tiles_done, self.done_at[g - RING])
            src, kc, n = self.groups[g]
            dst = self.slot(g, kc, n)
            sp.dma_start(dst, src).then_inc(self.landed[g % RING], 16)
            self.issued += 1

    def slot(self, g, kc, n):
        return self.ring[:, g % RING, 0:kc * n].rearrange("p (k n) -> p k n", k=kc)


def weight_plan(t):
    out = []

    def add(w, c0, c1, k0=0, k1=None):
        k1 = w.shape[0] // P if k1 is None else k1
        v = w.rearrange("(k p) n -> p k n", p=P)
        out.append((v[:, k0:k1, c0:c1], k1 - k0, c1 - c0))

    def blocks(w, step=BANK):
        for c in range(0, w.shape[1], step):
            add(w, c, min(c + step, w.shape[1]))

    for l in range(2):
        blocks(t["wkv_x"][l])
        if l == 0:
            blocks(t["w_in_e"][0])
            blocks(t["w_kv_up_b"][0])
            blocks(t["w_out_e"][0])
        else:
            blocks(t["w_in_o"][0])
            blocks(t["w_out_o"][0])
        blocks(t["wq_x"][l])
        blocks(t["wo_x"][l])
        blocks(t["w_up"][l])
        for c in range(0, D, BANK):
            for k in range(0, FF // P, KD):
                add(t["w_down"][l], c, c + BANK, k, k + KD)
    blocks(t["w_ada_2"][0])
    for c0, c1 in ((0, 512), (512, 1024), (1040, 1552), (1552, 2064), (2064, 2576)):
        add(t["w_in_2"][0], c0, c1)
    blocks(t["w_out_2"][0])
    return out


def project(g, name, groups, act, evac, cols=False, ntok=SEQ, kgroups=1, engines="v"):
    nc = g.nc
    free = {e: g.counter(f"bank_free_{e}") for e in engines}
    first = g.taken
    plan = g.groups[first:first + groups]

    def tiles(n):
        return (n + P - 1) // P if cols else ntok // P

    base = []
    for _, _, n in plan:
        base.append(g.tiles)
        g.tiles += tiles(n)
        g.done_at.append(g.tiles)

    units = [(b, m) for b in range(groups // kgroups) for m in range(tiles(plan[b * kgroups][2]))]
    who = [engines[u % len(engines)] for u in range(len(units))]
    turn = [sum(w == who[u] for w in who[:u + 1]) for u in range(len(units))]

    with nc.Block() as block:

        @block.sync
        def _(sp):
            g.prefetch(sp, first + groups)

        @block.tensor
        def _(pe):
            u0 = 0
            for b in range(groups // kgroups):
                for kg in range(kgroups):
                    gi = first + b * kgroups + kg
                    _, kc, n = g.groups[gi]
                    w = g.slot(gi, kc, n)
                    pe.wait_ge(g.landed[gi % RING], 16 * (gi // RING + 1))
                    for m in range(tiles(n)):
                        u = u0 + m
                        if kg == 0 and u >= 8:
                            pe.wait_ge(*free[who[u - 8]].at(turn[u - 8]))
                        for k in range(kc):
                            ka = kg * kc + k
                            if cols:
                                a, z = m * P, min(m * P + P, n)
                                o = g.psum[0:z - a, u % 8, 0:ntok]
                                mm = nc.tensor.matmul(o, w[:, k, a:z], act[:, ka, 0:ntok],
                                                      start=(ka == 0), stop=(ka == kc * kgroups - 1))
                            else:
                                mm = nc.tensor.matmul(g.psum[:, u % 8, 0:n], act[:, ka, m * P:m * P + P], w[:, k, :],
                                                      start=(ka == 0), stop=(ka == kc * kgroups - 1))
                        mm.then_inc(g.tiles_done, 1)
                u0 += tiles(n)

        def evacuate(eng, e):
            for u, (b, m) in enumerate(units):
                if who[u] != e:
                    continue
                n = plan[b * kgroups][2]
                eng.wait_ge(g.tiles_done, base[b * kgroups + kgroups - 1] + m + 1)
                rows = min(P, n - m * P) if cols else P
                width = ntok if cols else n
                evac(eng, b, m, g.psum[0:rows, u % 8, 0:width], n).then_inc(free[e].up(), 1)

        if "v" in engines:
            @block.vector
            def _(dve):
                evacuate(nc.vector, "v")

        if "a" in engines:
            @block.scalar
            def _(act_eng):
                evacuate(nc.scalar, "a")
    g.taken = first + groups


def copy(eng, nc, out, in_):
    if eng is nc.scalar:
        return nc.scalar.activation(out, in_, ACT.Copy)
    return eng.tensor_copy(out, in_)


def newton_rstd(g, rstd, mean, tmp):
    nc = g.nc
    g.vlink(nc.vector.tensor_tensor(tmp, rstd, rstd, ALU.mult))
    g.vlink(nc.vector.tensor_tensor(tmp, tmp, mean, ALU.mult))
    g.vlink(nc.vector.tensor_scalar(tmp, tmp, -0.5, 1.5, ALU.mult, ALU.add))
    g.vlink(nc.vector.tensor_tensor(rstd, rstd, tmp, ALU.mult))


def norm_transpose(g, name, rows, nt, out, gain_col=None, gain_row=None, shift_row=None, keep=None):
    nc = g.nc
    squared, inverse, rooted = (g.counter(s) for s in ("squared", "inverse", "rooted"))
    ready, turned, moved = (g.counter(s) for s in ("rows_ready", "bank_turned", "bank_moved"))
    with ExitStack() as ctx:
        normed = keep if keep is not None else g.sb(name + "_normed", [P, nt, D], ctx=ctx)
        square = g.sb(name + "_square", [P, D], ctx=ctx)
        st = g.sb(name + "_stats", [P, 4, nt], ctx=ctx)
        total, mean, rstd, tmp = (st[:, i, :] for i in range(4))
        with nc.Block() as block:

            @block.sync
            def _(sp):
                g.prefetch(sp, g.taken)

            @block.scalar
            def _(act):
                for t in range(nt):
                    g.alink(nc.scalar.activation(square[:], rows[:, t, :], ACT.Square, accum_out=total[:, t:t + 1]))
                nc.scalar.activation(square[:, 0:nt], total, ACT.Copy).then_inc(squared.up(), 1)
                act.wait_ge(*inverse.at(1))
                nc.scalar.activation(rstd, tmp, ACT.Sqrt).then_inc(rooted.up(), 1)

            @block.vector
            def _(dve):
                dve.wait_ge(*squared.at(1))
                g.vlink(nc.vector.tensor_scalar(mean, total, 1.0 / D, EPS, ALU.mult, ALU.add))
                nc.vector.reciprocal(tmp, mean).then_inc(inverse.up(), 1)
                dve.wait_ge(*rooted.at(1))
                newton_rstd(g, rstd, mean, tmp)
                for t in range(nt):
                    ins = nc.vector.tensor_scalar(normed[:, t, :], rows[:, t, :], rstd[:, t:t + 1], None, ALU.mult)
                    if gain_row is not None:
                        g.vlink(ins)
                        g.vlink(nc.vector.tensor_tensor(normed[:, t, :], normed[:, t, :], gain_row, ALU.mult))
                        ins = nc.vector.tensor_tensor(normed[:, t, :], normed[:, t, :], shift_row, ALU.add)
                    ins.then_inc(ready.up(), 1)
                for k in range(KD):
                    dve.wait_ge(*turned.at(k + 1))
                    if gain_col is not None:
                        nc.vector.tensor_scalar(out[:, k, 0:nt * P], g.psum[:, k, 0:nt * P], gain_col[:, k:k + 1],
                                                None, ALU.mult).then_inc(moved.up(), 1)
                    else:
                        nc.vector.tensor_copy(out[:, k, 0:nt * P], g.psum[:, k, 0:nt * P]).then_inc(moved.up(), 1)

            @block.tensor
            def _(pe):
                pe.wait_ge(*ready.at(nt))
                for k in range(KD):
                    for t in range(nt):
                        mm = nc.tensor.transpose(g.psum[:, k, t * P:t * P + P], normed[:, t, k * P:k * P + P],
                                                 g.ident[:])
                    mm.then_inc(turned.up(), 1)


def transpose_rows(g, name, jobs, engines="v"):
    nc = g.nc
    turned, moved = g.counter("bank_turned"), g.counter("bank_moved")
    with nc.Block() as block:

        @block.sync
        def _(sp):
            g.prefetch(sp, g.taken)

        @block.tensor
        def _(pe):
            for j, (out, tiles) in enumerate(jobs):
                if j >= 8:
                    pe.wait_ge(*moved.at(j - 7))
                for i, tile in enumerate(tiles):
                    c = tile.shape[1]
                    mm = nc.tensor.transpose(g.psum[0:c, j % 8, i * P:i * P + P], tile, g.ident[:])
                mm.then_inc(turned.up(), 1)

        @block.vector
        def _(dve):
            for j, (out, tiles) in enumerate(jobs):
                dve.wait_ge(*turned.at(j + 1))
                nc.vector.tensor_copy(out, g.psum[0:tiles[0].shape[1], j % 8, 0:len(tiles) * P]).then_inc(moved.up(), 1)


def head_norm(g, name, items):
    nc = g.nc
    squared, freed, inverse, rooted = (g.counter(s) for s in ("squared", "square_read", "inverse", "rooted"))
    most = max(x.shape[1] * x.shape[2] for x, _ in items)
    n = sum(x.shape[1] for x, _ in items)
    with ExitStack() as ctx:
        square = g.sb(name + "_square", [P, most], ctx=ctx)
        st = g.sb(name + "_stats", [P, 4, n], ctx=ctx)
        total, mean, rstd, tmp = (st[:, i, :] for i in range(4))
        with nc.Block() as block:

            @block.sync
            def _(sp):
                g.prefetch(sp, g.taken)

            @block.scalar
            def _(act):
                for i, (x, _) in enumerate(items):
                    if i:
                        act.wait_ge(*freed.at(i))
                    sq = square[:, 0:x.shape[1] * x.shape[2]].rearrange("p (a b) -> p a b", b=x.shape[2])
                    nc.scalar.activation(sq, x, ACT.Square).then_inc(squared.up(), 1)
                act.wait_ge(*inverse.at(1))
                nc.scalar.activation(rstd, tmp, ACT.Sqrt).then_inc(rooted.up(), 1)

            @block.vector
            def _(dve):
                at = 0
                for i, (x, _) in enumerate(items):
                    a, w = x.shape[1], x.shape[2]
                    dve.wait_ge(*squared.at(i + 1))
                    sq = square[:, 0:a * w].rearrange("p (a b) -> p a b", b=w)
                    ins = nc.vector.tensor_reduce(total[:, at:at + a], sq, AX.X, ALU.add)
                    g.vlink(ins)
                    g.vlink(nc.vector.tensor_scalar(mean[:, at:at + a], total[:, at:at + a], 1.0 / w, EPS,
                                                    ALU.mult, ALU.add))
                    nc.vector.reciprocal(tmp[:, at:at + a], mean[:, at:at + a]).then_inc(
                        (inverse if i == len(items) - 1 else freed).up(), 1)
                    at += a
                dve.wait_ge(*rooted.at(1))
                newton_rstd(g, rstd, mean, tmp)
                at = 0
                for x, gain in items:
                    a, w = x.shape[1], x.shape[2]
                    r = rstd[:, at:at + a].unsqueeze(2).to_broadcast([P, a, w])
                    g.vlink(nc.vector.tensor_tensor(x, x, r, ALU.mult))
                    if gain is not None:
                        gb = gain.unsqueeze(1).to_broadcast([P, a, w])
                        g.vlink(nc.vector.tensor_tensor(x, x, gb, ALU.mult))
                    at += a


def attend(g, name, units, comps, width, out_evac, mask_scale):
    nc = g.nc
    U = len(units)
    names = ("scores", "peak", "probs", "mixed", "turned", "copied", "out", "out_read")
    s_scores, s_peak, s_probs, s_mixed, s_turned, s_copied, s_out, s_read = (g.counter(s) for s in names)
    B = 2
    with ExitStack() as ctx:
        logits = g.sb(name + "_logits", [P, B, comps, BANK], ctx=ctx)
        probs = g.sb(name + "_probs", [P, B, comps, BANK], ctx=ctx)
        probsT = g.sb(name + "_probsT", [P, B, BANK], ctx=ctx)
        st = g.sb(name + "_stats", [P, 4, 4, comps], ctx=ctx)

        with nc.Block() as block:

            @block.sync
            def _(sp):
                g.prefetch(sp, g.taken)

            @block.tensor
            def _(pe):
                def scores(i):
                    un = units[i]
                    if i >= B:
                        pe.wait_ge(*s_peak.at(i - B + 1))
                    for c in range(comps):
                        mm = nc.tensor.matmul(g.psum[:, (i % B) * 2 + c, 0:un["nk"]], un["q"][c], un["k"][c],
                                              start=True, stop=True)
                    mm.then_inc(s_scores.up(), 1)

                def turn(i):
                    un = units[i]
                    pe.wait_ge(*(s_mixed if comps == 2 else s_probs).at(i + 1))
                    if i >= B:
                        pe.wait_ge(*s_copied.at(i - B + 1))
                    for j in range(un["nk"] // P):
                        mm = nc.tensor.transpose(g.psum[:, 4 + i % B, j * P:j * P + P],
                                                 probs[:, i % B, 0, j * P:j * P + P], g.ident[:])
                    mm.then_inc(s_turned.up(), 1)

                def values(i):
                    un = units[i]
                    pe.wait_ge(*s_copied.at(i + 1))
                    if i >= B:
                        pe.wait_ge(*s_read.at(i - B + 1))
                    n = un["nk"] // P
                    for j in range(n):
                        mm = nc.tensor.matmul(g.psum[:, 6 + i % B, 0:width], probsT[:, i % B, j * P:j * P + P],
                                              un["v"][j], start=(j == 0), stop=(j == n - 1))
                    mm.then_inc(s_out.up(), 1)

                for i in range(U + 2):
                    if i < U:
                        scores(i)
                    if 1 <= i <= U:
                        turn(i - 1)
                    if i >= 2:
                        values(i - 2)

            @block.vector
            def _(dve):
                def peak(i):
                    un = units[i]
                    dve.wait_ge(*s_scores.at(i + 1))
                    if i >= B:
                        dve.wait_ge(*s_probs.at(i - B + 1))
                    for c in range(comps):
                        ins = nc.vector.tensor_tensor_reduce(
                            logits[:, i % B, c, 0:un["nk"]], g.psum[:, (i % B) * 2 + c, 0:un["nk"]], un["bias"],
                            mask_scale, NEG * 10, ALU.add, ALU.max, st[:, i % 4, 0, c:c + 1])
                    g.vlink(ins)
                    nc.vector.tensor_scalar(st[:, i % 4, 1, :], st[:, i % 4, 0, :], -1.0, None,
                                            ALU.mult).then_inc(s_peak.up(), 1)

                def mix(i):
                    un = units[i]
                    dve.wait_ge(*s_probs.at(i + 1))
                    g.vlink(nc.vector.reciprocal(st[:, i % 4, 3, :], st[:, i % 4, 2, :]))
                    if comps == 2:
                        g.vlink(nc.vector.tensor_scalar(st[:, i % 4, 3, 1:2], st[:, i % 4, 3, 1:2], g.neg_lam[:, 0:1],
                                                        None, ALU.mult))
                        p0, p1 = (probs[:, i % B, c, 0:un["nk"]] for c in range(2))
                        g.vlink(nc.vector.tensor_scalar(p0, p0, st[:, i % 4, 3, 0:1], None, ALU.mult))
                        nc.vector.scalar_tensor_tensor(p0, p1, st[:, i % 4, 3, 1:2], p0, ALU.mult,
                                                       ALU.add).then_inc(s_mixed.up(), 1)

                def finish(i):
                    dve.wait_ge(*s_out.at(i + 1))
                    out_evac(units[i], g.psum[:, 6 + i % B, 0:width], st[:, i % 4, 3, 0:1]).then_inc(s_read.up(), 1)

                for i in range(U + 2):
                    if i < U:
                        peak(i)
                    if 1 <= i <= U:
                        mix(i - 1)
                    if i >= 2:
                        finish(i - 2)

            @block.scalar
            def _(act):
                def exponent(i):
                    un = units[i]
                    act.wait_ge(*s_peak.at(i + 1))
                    if i >= B:
                        act.wait_ge(*s_turned.at(i - B + 1))
                    if i >= 4:
                        act.wait_ge(*s_read.at(i - 3))
                    for c in range(comps):
                        ins = nc.scalar.activation(probs[:, i % B, c, 0:un["nk"]], logits[:, i % B, c, 0:un["nk"]],
                                                   ACT.Exp, bias=st[:, i % 4, 1, c:c + 1],
                                                   accum_out=st[:, i % 4, 2, c:c + 1])
                    ins.then_inc(s_probs.up(), 1)

                def copy_turned(i):
                    un = units[i]
                    act.wait_ge(*s_turned.at(i + 1))
                    if i >= B:
                        act.wait_ge(*s_out.at(i - B + 1))
                    nc.scalar.activation(probsT[:, i % B, 0:un["nk"]], g.psum[:, 4 + i % B, 0:un["nk"]],
                                         ACT.Copy).then_inc(s_copied.up(), 1)

                for i in range(U + 1):
                    if i < U:
                        exponent(i)
                    if i >= 1:
                        copy_turned(i - 1)


COLS = dict(g_mix=0, g_xattn=16, g_mem=32, g_mlp=48, conv_w=64, pool_scale=76, conv_w_2=80, conv_b_2=100)
COL_ROWS = 104
ROW_GAINS = (("gq_a", 64), ("gk_a", 64), ("gq_b", 64), ("gk_b", 64), ("g_kidx", 64), ("g_sub_a", 128), ("g_kv_b", 256),
             ("gq_x", 256), ("gk_x", 256), ("q_norm_g_2", 64), ("k_norm_g_2", 64))


def spread(w, n):
    return bass.AP(w.tensor, w.offset, [[0, P], [1, n]])


def constants(g):
    nc, t = g.nc, g.t
    g.x = g.sb("x_rows", [P, NT, D])
    g.hT = g.sb("hT", [P, KD, SEQ])
    g.ident = g.sb("ident", [P, P])
    g.causal = g.sb("causal", [P, SEQ])
    g.zeros = g.sb("zeros", [P, MEM])
    g.cols = g.sb("cols", [P, COL_ROWS])
    g.rowg = g.sb("row_gains", [P, sum(n for _, n in ROW_GAINS)])
    g.cos, g.sin = g.sb("cos", [P, NT, 8]), g.sb("sin", [P, NT, 8])
    g.neg_lam = g.sb("neg_lam", [P, 1])
    g.gain = {}
    at = 0
    for name, n in ROW_GAINS:
        g.gain[name] = g.rowg[:, at:at + n]
        at += n
    loaded, x_loaded, made = g.sem("constants_loaded"), g.sem("x_loaded"), g.counter("tables_made")
    turned, zeroed = g.counter("cols_turned"), g.counter("constants_zeroed")
    reduced, sines, expo = g.counter("angles_reduced"), g.counter("sines"), g.counter("lambda_exp")
    inv = (np.float32(500000.0) ** (-np.arange(0, 16, 2, dtype=np.float32) / np.float32(16))).astype(np.float32)
    c1, c2 = 6.28125, 0.0019350051879882812
    c3 = 2 * np.pi - c1 - c2
    with ExitStack() as ctx:
        colrows = g.sb("col_rows", [COL_ROWS, P], ctx=ctx)
        pos = g.sb("positions", [P, NT], I32, ctx=ctx)
        posf = g.sb("positions_f", [P, NT], ctx=ctx)
        freq = g.sb("frequencies", [P, 8], ctx=ctx)
        ang, turns, rest = (g.sb(n, [P, NT, 8], ctx=ctx) for n in ("angle", "turns", "rest"))
        lamv = g.sb("lambda_vectors", [P, 4, 64], ctx=ctx)
        lams = g.sb("lambda_sums", [P, 4], ctx=ctx)
        junk = g.sb("lambda_products", [P, 64], ctx=ctx)
        loads = [
            (colrows[0:16], t["g_mix"].rearrange("l (k p) -> (l k) p", p=P)),
            (colrows[16:32], t["g_xattn"].rearrange("l (k p) -> (l k) p", p=P)),
            (colrows[32:48], t["g_mem"].rearrange("l (k p) -> (l k) p", p=P)),
            (colrows[48:64], t["g_mlp"].rearrange("l (k p) -> (l k) p", p=P)),
            (colrows[64:76], t["conv_w"][0].rearrange("j (k p) -> (j k) p", p=P)),
            (colrows[76:80], t["pool_scale"].rearrange("l (k p) -> (l k) p", p=P)),
            (colrows[80:100], t["conv_w_2"][0].rearrange("j (k p) -> (j k) p", p=P)),
            (colrows[100:104], t["conv_b_2"].rearrange("l (k p) -> (l k) p", p=P)),
            (pos[:], t["positions"][0].rearrange("(t p) -> p t", p=P)),
        ]
        loads += [(g.gain[name], spread(t[name], n)) for name, n in ROW_GAINS]
        loads += [(lamv[:, i, :], spread(t[n], 64)) for i, n in enumerate(("lam_q1", "lam_k1", "lam_q2", "lam_k2"))]
        with nc.Block() as block:

            @block.sync
            def _(sp):
                sp.dma_start(g.x[:], t["x"][0].rearrange("(t p) d -> p t d", p=P)).then_inc(x_loaded, 16)
                with nc.allow_non_contiguous_dma(reason="512 positions, one per partition and tile"):
                    for out, src in loads:
                        sp.dma_start(out, src).then_inc(loaded, 16)
                g.prefetch(sp, 0)
                sp.wait_ge(x_loaded, 16)
                sp.wait_ge(loaded, 16 * len(loads))

            @block.gpsimd
            def _(pool):
                nc.gpsimd.memset(g.zeros[:], 0.0).then_inc(zeroed.up(), 1)
                nc.gpsimd.memset(g.ident[:], 0.0).then_inc(zeroed.up(), 1)
                nc.gpsimd.memset(g.causal[:], 0.0).then_inc(zeroed.up(), 1)
                for i in range(8):
                    nc.gpsimd.memset(freq[:, i:i + 1], float(inv[i])).then_inc(zeroed.up(), 1)
                pool.wait_ge(*zeroed.at(11))
                nc.gpsimd.affine_select(out=g.ident[:], in_=g.ident[:], compare_op=ALU.not_equal, fill=1.0, base=0,
                                        pattern=[[-1, P]], channel_multiplier=1).then_inc(made.up(), 1)
                nc.gpsimd.affine_select(out=g.causal[:], in_=g.causal[:], compare_op=ALU.is_ge, fill=NEG,
                                        base=SEQ - P, pattern=[[-1, SEQ]], channel_multiplier=1).then_inc(made.up(), 1)

            @block.tensor
            def _(pe):
                pe.wait_ge(*made.at(2))
                pe.wait_ge(loaded, 16 * len(loads))
                nc.tensor.transpose(g.psum[:, 0, 0:COL_ROWS], colrows[:], g.ident[0:COL_ROWS, 0:COL_ROWS]).then_inc(
                    turned.up(), 1)

            @block.vector
            def _(dve):
                dve.wait_ge(loaded, 16 * len(loads))
                dve.wait_ge(*zeroed.at(11))
                g.vlink(nc.vector.tensor_copy(posf[:], pos[:]))
                f = freq[:].unsqueeze(1).to_broadcast([P, NT, 8])
                g.vlink(nc.vector.tensor_tensor(ang[:], posf[:].unsqueeze(2).to_broadcast([P, NT, 8]), f, ALU.mult))
                g.vlink(nc.vector.tensor_scalar(turns[:], ang[:], float(1 / (2 * np.pi)), 12582912.0,
                                                ALU.mult, ALU.add))
                g.vlink(nc.vector.tensor_scalar(turns[:], turns[:], -12582912.0, None, ALU.add))
                for c in (c1, c2, c3):
                    g.vlink(nc.vector.scalar_tensor_tensor(ang[:], turns[:], -float(c), ang[:], ALU.mult, ALU.add))
                g.vlink(nc.vector.tensor_scalar(ang[:], ang[:], 3.1415925, -3.1415925, ALU.min, ALU.max))
                g.vlink(nc.vector.scalar_tensor_tensor(rest[:], ang[:], -1.0, ang[:], ALU.mult, ALU.max))
                nc.vector.tensor_scalar(rest[:], rest[:], -1.0, float(np.pi / 2), ALU.mult, ALU.add).then_inc(
                    reduced.up(), 1)
                for i in range(2):
                    ins = nc.vector.tensor_tensor_reduce(junk[:], lamv[:, 2 * i, :], lamv[:, 2 * i + 1, :], 1.0, 0.0,
                                                         ALU.mult, ALU.add, lams[:, i:i + 1])
                    g.vlink(ins)
                nc.vector.tensor_copy(junk[:, 0:2], lams[:, 0:2]).then_inc(reduced.up(), 1)
                dve.wait_ge(*turned.at(1))
                nc.vector.tensor_copy(g.cols[:], g.psum[:, 0, 0:COL_ROWS])
                dve.wait_ge(*expo.at(1))
                nc.vector.scalar_tensor_tensor(g.neg_lam[:], lams[:, 3:4], -0.2, lams[:, 2:3], ALU.add, ALU.subtract)

            @block.scalar
            def _(act):
                act.wait_ge(*reduced.at(2))
                nc.scalar.activation(g.sin[:], ang[:], ACT.Sin)
                nc.scalar.activation(g.cos[:], rest[:], ACT.Sin).then_inc(sines.up(), 1)
                nc.scalar.activation(lams[:, 2:4], junk[:, 0:2], ACT.Exp).then_inc(expo.up(), 1)


def rope(g, name, items):
    nc = g.nc
    with ExitStack() as ctx:
        tmp = [g.sb(f"{name}_tmp{i}", [P, NT * 8 * 8], ctx=ctx) for i in range(4)]
        with nc.Block() as block:

            @block.sync
            def _(sp):
                g.prefetch(sp, g.taken)

            @block.vector
            def _(dve):
                for x in items:
                    h = x.shape[2]
                    for t in range(NT):
                        x1, x2 = x[:, t, :, 0:8], x[:, t, :, 8:16]
                        c = g.cos[:, t, :].unsqueeze(1).to_broadcast([P, h, 8])
                        s = g.sin[:, t, :].unsqueeze(1).to_broadcast([P, h, 8])
                        o = 64 * t
                        v = [a[:, o:o + h * 8].rearrange("p (h d) -> p h d", d=8) for a in tmp]
                        nc.vector.tensor_tensor(v[0], x1, c, ALU.mult)
                        nc.vector.tensor_tensor(v[1], x2, s, ALU.mult)
                        nc.vector.tensor_tensor(v[2], x2, c, ALU.mult)
                        g.vlink(nc.vector.tensor_tensor(v[3], x1, s, ALU.mult))
                        nc.vector.tensor_tensor(x1, v[0], v[1], ALU.subtract)
                        g.vlink(nc.vector.tensor_tensor(x2, v[2], v[3], ALU.add))


def heads(x, w):
    return x.rearrange("p t (h d) -> p (t h) d", d=w)


def add_to_x(g):
    def evac(eng, b, m, ps, n):
        xs = g.x[:, m, b * BANK:b * BANK + n]
        return eng.tensor_tensor(xs, ps, xs, ALU.add)
    return evac


def col(g, name, l, k=KD):
    return g.cols[:, COLS[name] + l * k:COLS[name] + (l + 1) * k]


def memory_keys(g, l, kT, v):
    nc, t = g.nc, g.t
    with ExitStack() as ctx:
        mem = g.sb(f"mem{l}", [P, 2, D], ctx=ctx)
        krow = g.sb(f"mem_keys{l}", [P, 2, BANK], ctx=ctx)
        s = g.sem(f"mem_loaded{l}")
        with nc.Block() as block:

            @block.sync
            def _(sp):
                sp.dma_start(mem[:], t["mem"][0].rearrange("(t p) d -> p t d", p=P)).then_inc(s, 16)
                g.prefetch(sp, g.taken)
                sp.wait_ge(s, 16)

        norm_transpose(g, f"mem_norm{l}", mem[:], 2, g.hT, gain_col=col(g, "g_mem", l))
        project(g, f"mem_kv{l}", 2, g.hT, lambda eng, b, m, ps, n: copy(eng, nc, (krow, v)[b][:, m, :], ps),
                ntok=MEM, engines="va")
        head_norm(g, f"mem_knorm{l}", [(heads(krow[:], P), g.gain["gk_x"][:, l * P:l * P + P])])
        transpose_rows(g, f"mem_kT{l}", [(kT[:, h, :], [krow[:, i, h * P:h * P + P] for i in range(2)])
                                         for h in range(4)])


def cross_attention(g, l, kT, v):
    nc = g.nc
    norm_transpose(g, f"x_norm{l}", g.x[:], NT, g.hT, gain_col=col(g, "g_xattn", l))
    with ExitStack() as ctx:
        q = g.sb(f"x_q{l}", [P, NT, BANK], ctx=ctx)
        y = g.sb(f"x_y{l}", [P, NT, BANK], ctx=ctx)
        project(g, f"x_qproj{l}", 1, g.hT, lambda eng, b, m, ps, n: copy(eng, nc, q[:, m, :], ps), engines="va")
        head_norm(g, f"x_qnorm{l}", [(heads(q[:], P), g.gain["gq_x"][:, l * P:l * P + P])])
        transpose_rows(g, f"x_qT{l}", [(g.hT[:, h, :], [q[:, i, h * P:h * P + P] for i in range(NT)])
                                       for h in range(4)])
        units = [dict(q=[g.hT[:, h, i * P:i * P + P]], k=[kT[:, h, :]], nk=MEM, bias=g.zeros[:],
                      v=[v[:, j, h * P:h * P + P] for j in range(2)], out=y[:, i, h * P:h * P + P])
                 for h in range(4) for i in range(NT)]
        attend(g, f"x_att{l}", units, 1, P,
               lambda un, ps, r: nc.vector.tensor_scalar(un["out"], ps, r, None, ALU.mult), float(P) ** -0.5)
        transpose_rows(g, f"x_yT{l}", [(g.hT[:, h, :], [y[:, i, h * P:h * P + P] for i in range(NT)])
                                       for h in range(4)])
        project(g, f"x_out{l}", 2, g.hT, add_to_x(g))


def mlp(g, l):
    nc = g.nc
    norm_transpose(g, f"m_norm{l}", g.x[:], NT, g.hT, gain_col=col(g, "g_mlp", l))
    with ExitStack() as ctx:
        u = g.sb(f"m_u{l}", [P, FF // P, SEQ], ctx=ctx)

        def squared_relu(eng, b, m, ps, n):
            o = u[:, b * 4 + m, :]
            if eng is nc.scalar:
                g.alink(nc.scalar.activation(o, ps, ACT.Relu))
                return nc.scalar.activation(o, o, ACT.Square)
            g.vlink(nc.vector.tensor_scalar(o, ps, 0.0, None, ALU.max))
            return nc.vector.tensor_tensor(o, o, o, ALU.mult)

        project(g, f"m_up{l}", FF // BANK, g.hT, squared_relu, cols=True, engines="va")
        project(g, f"m_down{l}", 8, u, add_to_x(g), kgroups=4)


def index_select(g, qiT, kiT, wi, bias, scratch, topk=P):
    nc = g.nc
    scored, relued, read = g.counter("scores"), g.counter("scores_relu"), g.counter("relu_read")
    tiles = range(1, NT)
    units = [(i, h) for i in tiles for h in range(4)]
    with ExitStack() as ctx:
        isc, work, eq, run = (scratch[0][:, i, :] for i in range(4))
        rel = scratch[1]
        top = g.sb("index_top", [P, 8], ctx=ctx)
        cnt = g.sb("index_count", [P, 1], ctx=ctx)
        with nc.Block() as block:

            @block.sync
            def _(sp):
                g.prefetch(sp, g.taken)

            @block.tensor
            def _(pe):
                for u, (i, h) in enumerate(units):
                    p0, nk = 64 * (h % 2), (i + 1) * P
                    if u >= 8:
                        pe.wait_ge(*relued.at(u - 7))
                    nc.tensor.matmul(g.psum[:, u % 8, 0:nk], qiT[p0:p0 + 64, h // 2, i * P:i * P + P],
                                     kiT[p0:p0 + 64, 0:nk], start=True, stop=True).then_inc(scored.up(), 1)

            @block.scalar
            def _(act):
                for u, (i, h) in enumerate(units):
                    nk = (i + 1) * P
                    act.wait_ge(*scored.at(u + 1))
                    if u >= 2:
                        act.wait_ge(*read.at(u - 1))
                    nc.scalar.activation(rel[:, u % 2, 0:nk], g.psum[:, u % 8, 0:nk], ACT.Relu).then_inc(relued.up(), 1)

            @block.vector
            def _(dve):
                at = 0
                for u, (i, h) in enumerate(units):
                    nk = (i + 1) * P
                    dve.wait_ge(*relued.at(u + 1))
                    s, r = isc[:, 0:nk], rel[:, u % 2, 0:nk]
                    w = wi[:, i, h:h + 1]
                    if h == 0:
                        ins = nc.vector.tensor_scalar(s, r, w, None, ALU.mult)
                    else:
                        ins = nc.vector.scalar_tensor_tensor(s, r, w, s, ALU.mult, ALU.add)
                    ins.then_inc(read.up(), 1)
                    dve.wait_ge(*read.at(u + 1))
                    if h < 3:
                        continue
                    g.vlink(nc.vector.tensor_tensor(s, s, g.causal[:, (NT - 1 - i) * P:SEQ], ALU.add))
                    src, wk = s, work[:, 0:nk]
                    for r8 in range(topk // 8):
                        g.vlink(nc.vector.max(top[:], src))
                        if r8 < topk // 8 - 1:
                            g.vlink(nc.vector.match_replace(wk, top[:], src, -3e38))
                            src = wk
                    thr = top[:, 7:8]
                    g.vlink(nc.vector.tensor_scalar(wk, s, thr, None, ALU.is_gt, ALU.add, cnt[:]))
                    g.vlink(nc.vector.tensor_scalar(eq[:, 0:nk], s, thr, None, ALU.is_equal))
                    g.vlink(nc.vector.tensor_scalar(cnt[:], cnt[:], -1.0, float(topk), ALU.mult, ALU.add))
                    g.vlink(nc.vector.tensor_tensor_scan(run[:, 0:nk], eq[:, 0:nk], eq[:, 0:nk], 0.0, ALU.add,
                                                         ALU.bypass))
                    g.vlink(nc.vector.scalar_tensor_tensor(eq[:, 0:nk], run[:, 0:nk], cnt[:], eq[:, 0:nk],
                                                           ALU.is_le, ALU.mult))
                    g.vlink(nc.vector.tensor_tensor(wk, wk, eq[:, 0:nk], ALU.add))
                    b = bias[:, at:at + nk]
                    g.vlink(nc.vector.tensor_scalar(wk, wk, -NEG, NEG, ALU.mult, ALU.add))
                    g.vlink(nc.vector.tensor_tensor(b, wk, g.causal[:, (NT - 1 - i) * P:SEQ], ALU.min))
                    at += nk


def even_mixer(g):
    nc = g.nc
    norm_transpose(g, "e_norm", g.x[:], NT, g.hT, gain_col=col(g, "g_mix", 0))
    with ExitStack() as ctx:
        va, vb, qb, kb = (g.sb("e_" + n, [P, NT, BANK], ctx=ctx) for n in ("va", "vb", "qb", "kb"))
        bias = g.sb("e_bias", [P, 1152], ctx=ctx)
        QTb, KTb = g.sb("e_QTb", [P, 4, SEQ], ctx=ctx), g.sb("e_KTb", [P, 4, SEQ], ctx=ctx)
        QTa, KTa = g.hT[:, 0:4, :], g.hT[:, 4:8, :]
        with ExitStack() as c2:
            qa, ka, cq = (g.sb("e_" + n, [P, NT, BANK], ctx=c2) for n in ("qa", "ka", "cq"))
            kw = g.sb("e_kw", [P, NT, 68], ctx=c2)
            dest = [qa[:], ka[:], va[:], qb[:], cq[:], kw[:]]
            project(g, "e_in", 6, g.hT, lambda eng, b, m, ps, n: copy(eng, nc, dest[b][:, m, :], ps), engines="va")
            head_norm(g, "e_kvnorm", [(cq[:, :, 0:256], g.gain["g_kv_b"])])
            with ExitStack() as c3:
                ckT = g.sb("e_ckT", [P, 2, SEQ], ctx=c3)
                transpose_rows(g, "e_ckT_t", [(ckT[:, k, :], [cq[:, i, k * P:k * P + P] for i in range(NT)])
                                              for k in range(2)])
                project(g, "e_kvup", 2, ckT, lambda eng, b, m, ps, n: copy(eng, nc, (kb, vb)[b][:, m, :], ps),
                        engines="va")
            head_norm(g, "e_hnorm", [(heads(qa[:], 64), g.gain["gq_a"]), (heads(ka[:], 64), g.gain["gk_a"]),
                                     (heads(qb[:], 64), g.gain["gq_b"]), (heads(kb[:], 64), g.gain["gk_b"]),
                                     (kw[:, :, 0:64], g.gain["g_kidx"])])

            def split(x):
                return x.rearrange("p t (h d) -> p t h d", d=64)

            rope(g, "e_rope", [split(qa[:]), split(ka[:]), split(qb[:]), split(kb[:]),
                               split(cq[:, :, 256:512]), kw[:, :, 0:64].unsqueeze(2)])
            with ExitStack() as c3:
                ki2 = g.sb("e_ki2", [P, NT, P], ctx=c3)
                wi = g.sb("e_wi", [P, NT, 4], ctx=c3)
                qiT, kiT = g.sb("e_qiT", [P, 2, SEQ], ctx=c3), g.sb("e_kiT", [P, SEQ], ctx=c3)
                with nc.Block() as block:

                    @block.vector
                    def _(dve):
                        nc.vector.tensor_copy(ki2[:, :, 0:64], kw[:, :, 0:64])
                        nc.vector.tensor_copy(ki2[:, :, 64:128], kw[:, :, 0:64])
                        nc.vector.tensor_scalar(wi[:], kw[:, :, 64:68], 4 ** -0.5 * 64 ** -0.5, None, ALU.mult)

                jobs = [(dst[:, k, :], [src[:, i, k * P:k * P + P] for i in range(NT)])
                        for dst, src in ((QTa, qa), (KTa, ka), (QTb, qb), (KTb, kb)) for k in range(4)]
                jobs += [(qiT[:, k, :], [cq[:, i, 256 + k * P:384 + k * P] for i in range(NT)]) for k in range(2)]
                jobs += [(kiT[:], [ki2[:, i, :] for i in range(NT)])]
                transpose_rows(g, "e_T", jobs)
                index_select(g, qiT, kiT, wi, bias, (qa, ka))
        with ExitStack() as c2:
            ya, yb = (g.sb("e_" + n, [P, NT, BANK], ctx=c2) for n in ("ya", "yb"))

            def causal(i):
                return g.causal[:, (NT - 1 - i) * P:SEQ]

            units = [dict(q=[QTa[64 * c:64 * c + 64, h, i * P:i * P + P] for c in range(2)],
                          k=[KTa[64 * c:64 * c + 64, h, 0:(i + 1) * P] for c in range(2)], nk=(i + 1) * P,
                          bias=causal(i), v=[va[:, j, h * P:h * P + P] for j in range(i + 1)],
                          out=ya[:, i, h * P:h * P + P]) for h in range(4) for i in range(NT)]
            attend(g, "e_attA", units, 2, P, lambda un, ps, r: nc.vector.tensor_copy(un["out"], ps), 64 ** -0.5)
            offs = [0, 0, 256, 640]
            units = [dict(q=[QTb[64 * (h % 2):64 * (h % 2) + 64, h // 2, i * P:i * P + P]],
                          k=[KTb[64 * (h % 2):64 * (h % 2) + 64, h // 2, 0:(i + 1) * P]], nk=(i + 1) * P,
                          bias=causal(0) if i == 0 else bias[:, offs[i]:offs[i] + (i + 1) * P],
                          v=[vb[:, j, h * 64:h * 64 + 64] for j in range(i + 1)],
                          out=yb[:, i, h * 64:h * 64 + 64]) for h in range(8) for i in range(NT)]
            attend(g, "e_attB", units, 1, 64,
                   lambda un, ps, r: nc.vector.tensor_scalar(un["out"], ps, r, None, ALU.mult), 64 ** -0.5)
            gs = g.sb("e_gsub", [P, P], ctx=c2)
            with nc.Block() as block:

                @block.vector
                def _(dve):
                    nc.vector.tensor_scalar(gs[:], g.gain["g_sub_a"], 0.8, None, ALU.mult)

            head_norm(g, "e_onorm", [(heads(ya[:], P), gs[:])])
            transpose_rows(g, "e_yT", [(g.hT[:, 4 * s + k, :], [(ya, yb)[s][:, i, k * P:k * P + P]
                                                               for i in range(NT)]) for s in range(2)
                                       for k in range(4)])
            project(g, "e_out", 2, g.hT, add_to_x(g))


def odd_mixer(g):
    nc, t = g.nc, g.t
    norm_transpose(g, "o_norm", g.x[:], NT, g.hT, gain_col=col(g, "g_mix", 1))
    with ExitStack() as ctx:
        gb, u, z, cv, sm = (g.sb("o_" + n, [P, NT, SEQ], ctx=ctx) for n in ("gb", "u", "z", "conv", "sums"))
        wp = g.sb("o_wpool", [P, 4, P], ctx=ctx)
        rc = g.sb("o_rcount", [P, 16], ctx=ctx)

        def evac(eng, b, m, ps, n):
            if b == 2:
                if m == 0:
                    g.vlink(nc.vector.tensor_copy(rc[:, 0:1], g.zeros[:, 0:1]))
                return eng.tensor_tensor(u[:, m, :], ps, u[:, m, :], ALU.mult)
            return eng.tensor_copy({0: gb, 1: u, 3: z}[b][:, m, :], ps)

        project(g, "o_in", 4, g.hT, evac, cols=True)
        wl = g.sem("w_pool_loaded")
        cnt, pooled, mixed = (g.counter(n) for n in ("counts", "pooled", "pool_mixed"))
        yT = g.hT
        with nc.Block() as block:

            @block.sync
            def _(sp):
                sp.dma_start(wp[:], t["w_pool"][0].rearrange("g c d -> c g d")).then_inc(wl, 16)
                g.prefetch(sp, g.taken)

            @block.gpsimd
            def _(pool):
                for i in range(16):
                    nc.gpsimd.memset(rc[:, i:i + 1], 1.0 / (i + 1)).then_inc(cnt.up(), 1)

            @block.vector
            def _(dve):
                dve.wait_ge(*cnt.at(16))
                for m in range(4):
                    w = 2 ** (m + 1)
                    src, s = z[:, m, :], 1
                    bufs = [sm[:, m, :], cv[:, m, :]]
                    k = 0
                    while s < w:
                        dst = bufs[k % 2]
                        nc.vector.tensor_copy(dst[:, 0:s], src[:, 0:s])
                        g.vlink(nc.vector.tensor_tensor(dst[:, s:SEQ], src[:, s:SEQ], src[:, 0:SEQ - s], ALU.add))
                        src, s, k = dst, 2 * s, k + 1
                    o = bufs[k % 2]
                    g.vlink(nc.vector.tensor_tensor(o[:, 0:w], src[:, 0:w], rc[:, 0:w], ALU.mult))
                    g.vlink(nc.vector.tensor_tensor(o[:, 0:w], o[:, 0:w], z[:, m, 0:w], ALU.subtract))
                    g.vlink(nc.vector.scalar_tensor_tensor(o[:, w:SEQ], src[:, w:SEQ], 1.0 / w, z[:, m, w:SEQ],
                                                           ALU.mult, ALU.subtract))
                    nc.vector.tensor_copy(z[:, m, :], o).then_inc(pooled.up(), 1)
                dve.wait_ge(*pooled.at(4))
                for m in range(4):
                    c, um = cv[:, m, :], u[:, m, :]
                    w = [g.cols[:, COLS["conv_w"] + 4 * j + m:COLS["conv_w"] + 4 * j + m + 1] for j in range(3)]
                    g.vlink(nc.vector.tensor_scalar(c, um, w[2], None, ALU.mult))
                    for j in (1, 0):
                        d = 2 - j
                        g.vlink(nc.vector.scalar_tensor_tensor(c[:, d:SEQ], um[:, 0:SEQ - d], w[j], c[:, d:SEQ],
                                                               ALU.mult, ALU.add))
                    nc.vector.tensor_tensor(yT[:, m, :], gb[:, m, :], c, ALU.mult)
                for m in range(4):
                    dve.wait_ge(*mixed.at(m + 1))
                    ps = g.cols[:, COLS["pool_scale"] + m:COLS["pool_scale"] + m + 1]
                    nc.vector.tensor_scalar(yT[:, 4 + m, :], g.psum[:, m, :], ps, None, ALU.mult)

            @block.tensor
            def _(pe):
                pe.wait_ge(wl, 16)
                for m in range(4):
                    pe.wait_ge(*pooled.at(m + 1))
                    nc.tensor.matmul(g.psum[:, m, :], wp[:, m, :], z[:, m, :], start=True, stop=True).then_inc(
                        mixed.up(), 1)

        project(g, "o_out", 2, g.hT, add_to_x(g))


def first_block(g):
    for l in range(2):
        with ExitStack() as ctx:
            kT, v = g.sb(f"x_kT{l}", [P, 4, MEM], ctx=ctx), g.sb(f"x_v{l}", [P, 2, BANK], ctx=ctx)
            memory_keys(g, l, kT, v)
            if l == 0:
                even_mixer(g)
            else:
                odd_mixer(g)
            cross_attention(g, l, kT, v)
        mlp(g, l)


def shape_constants():
    dist = np.arange(1024) - 511
    n = np.abs(dist)
    half, exact = 16, 8
    ratio = np.log(np.maximum(n, 1).astype(np.float32) / exact) / np.float32(np.log(1024 / exact))
    large = np.minimum(exact + (ratio * (half - exact)).astype(np.int32), half - 1)
    bucket = np.where(dist > 0, half, 0) + np.where(n < exact, n, large)
    hot = (bucket[None, :] == np.arange(32)[:, None]).astype(np.float32)
    count = sum(((n % d == 0) & (n <= 64 * d)).astype(np.float64) for d in (1, 4, 16))
    logs = np.where(count > 0, 8 * np.log(np.maximum(count, 1)), NEG).astype(np.float32)
    return {"bucket_hot": hot, "window_logs": logs}


def modulation(g, mod):
    nc, t = g.nc, g.t
    loaded, silued, wide = g.sem("modulation_loaded"), g.counter("c_silu"), g.counter("c_wide")
    with ExitStack() as ctx:
        c, cs = g.sb("c_col", [P, KD], ctx=ctx), g.sb("c_silu", [P, KD], ctx=ctx)
        cw = g.sb("c_wide", [P, KD, P], ctx=ctx)
        gains = g.sb("norm_rows", [P, 2, D], ctx=ctx)
        with nc.Block() as block:

            @block.sync
            def _(sp):
                with nc.allow_non_contiguous_dma(reason="1024 values, one per partition and chunk"):
                    sp.dma_start(c[:], t["c_2"][0].rearrange("(k p) -> p k", p=P)).then_inc(loaded, 16)
                sp.dma_start(mod[:], spread(t["b_ada_2"], 6 * D)).then_inc(loaded, 16)
                sp.dma_start(gains[:, 0, :], spread(t["norm1_g_2"], D)).then_inc(loaded, 16)
                sp.dma_start(gains[:, 1, :], spread(t["norm2_g_2"], D)).then_inc(loaded, 16)
                g.prefetch(sp, g.taken)
                sp.wait_ge(loaded, 64)

            @block.scalar
            def _(act):
                act.wait_ge(loaded, 64)
                nc.scalar.activation(cs[:], c[:], ACT.Silu).then_inc(silued.up(), 1)

            @block.vector
            def _(dve):
                dve.wait_ge(*silued.at(1))
                nc.vector.tensor_copy(cw[:], cs[:].unsqueeze(2).to_broadcast([P, KD, P])).then_inc(wide.up(), 1)

        def add_bias(eng, b, m, ps, n):
            o = mod[:, b * BANK:b * BANK + n]
            return eng.tensor_tensor(o, ps, o, ALU.add)

        project(g, "ada", 12, cw, add_bias, ntok=P)
        with nc.Block() as block:

            @block.vector
            def _(dve):
                for i in range(2):
                    o = mod[:, (3 * i + 1) * D:(3 * i + 2) * D]
                    nc.vector.scalar_tensor_tensor(o, o, 1.0, gains[:, i, :], ALU.add, ALU.mult)


def gate_rows(g, xT, aT, enT, mrow):
    nc, t = g.nc, g.t
    loaded = g.sem("gates_loaded")
    packed, gated, logf, exped, lned, scanned, turned = (g.counter("gate_" + n) for n in (
        "packed", "gated", "logf", "exped", "lned", "scanned", "turned"))
    first = t["w_in_2"][0][:, 1024:1040].rearrange("(k p) n -> p k n", p=P)
    with ExitStack() as ctx:
        w, wp = g.sb("gate_w", [P, KD, 16], ctx=ctx), g.sb("gate_wp", [P, KD, P], ctx=ctx)
        bias = g.sb("gate_bias", [P, 1], ctx=ctx)
        pre = g.sb("gate_pre", [P, SEQ], ctx=ctx)
        f, e, cum, a, nm = (g.sb("gate_" + n, [64, SEQ], ctx=ctx) for n in ("f", "e", "cum", "a", "nm"))
        zeroed = g.counter("gate_zeroed")
        with nc.Block() as block:

            @block.sync
            def _(sp):
                sp.wait_ge(*zeroed.at(1))
                sp.dma_start(w[:], first).then_inc(loaded, 16)
                with nc.allow_non_contiguous_dma(reason="four biases of four bytes each"):
                    for i, (name, d) in enumerate((("b_igate_2", 0), ("b_igate_2", 1), ("b_fgate_2", 0),
                                                   ("b_fgate_2", 1))):
                        sp.dma_start(bias[32 * i:32 * i + 4, :],
                                     t[name][0, d].rearrange("(h o) -> h o", o=1)).then_inc(loaded, 16)
                g.prefetch(sp, g.taken)

            @block.vector
            def _(dve):
                g.vlink(nc.vector.memset(wp[:], 0.0))
                nc.vector.memset(bias[:], 0.0).then_inc(zeroed.up(), 1)
                dve.wait_ge(loaded, 80)
                for i, c in enumerate((0, 8, 4, 12)):
                    ins = nc.vector.tensor_copy(wp[:, :, 32 * i:32 * i + 4], w[:, :, c:c + 4])
                ins.then_inc(packed.up(), 1)
                dve.wait_ge(*gated.at(1))
                g.vlink(nc.vector.tensor_scalar(pre[:], g.psum[:, 0, :], bias[:, 0:1], None, ALU.add))
                g.vlink(nc.vector.tensor_copy(f[:], pre[64:128, :]))
                nc.vector.scalar_tensor_tensor(e[:], f[:], -1.0, f[:], ALU.mult, ALU.max).then_inc(logf.up(), 1)
                dve.wait_ge(*lned.at(1))
                g.vlink(nc.vector.scalar_tensor_tensor(f[:], f[:], 0.0, e[:], ALU.min, ALU.subtract))
                g.vlink(nc.vector.tensor_tensor_scan(cum[0:32, :], f[0:32, :], f[0:32, :], 0.0, ALU.add, ALU.bypass))
                g.vlink(nc.vector.tensor_tensor_scan(cum[32:64, ::-1], f[32:64, ::-1], f[32:64, ::-1], 0.0, ALU.add,
                                                     ALU.bypass))
                g.vlink(nc.vector.tensor_tensor(a[:], pre[0:64, :], cum[:], ALU.subtract))
                g.vlink(nc.vector.tensor_tensor_scan(mrow[0:32, :], a[0:32, :], a[0:32, :], 0.0, ALU.max, ALU.bypass))
                g.vlink(nc.vector.tensor_tensor_scan(mrow[32:64, ::-1], a[32:64, ::-1], a[32:64, ::-1], 0.0, ALU.max,
                                                     ALU.bypass))
                nc.vector.scalar_tensor_tensor(nm[:], cum[:], -1.0, mrow[:], ALU.mult, ALU.subtract).then_inc(
                    scanned.up(), 1)
                dve.wait_ge(*turned.at(1))
                nc.vector.tensor_copy(aT[:], g.psum[:, 1, 0:4 * 64].rearrange("p (t h) -> p t h", t=4))

            @block.scalar
            def _(act):
                act.wait_ge(*logf.at(1))
                g.alink(nc.scalar.activation(e[:], e[:], ACT.Exp, scale=-1.0))
                nc.scalar.activation(e[:], e[:], ACT.Ln, bias=1.0).then_inc(lned.up(), 1)
                act.wait_ge(*turned.at(2))
                nc.scalar.activation(enT[:], g.psum[:, 2, 0:4 * 64].rearrange("p (t h) -> p t h", t=4), ACT.Exp)

            @block.tensor
            def _(pe):
                pe.wait_ge(*packed.at(1))
                for k in range(KD):
                    mm = nc.tensor.matmul(g.psum[:, 0, :], wp[:, k, :], xT[:, k, :], start=(k == 0), stop=(k == KD - 1))
                mm.then_inc(gated.up(), 1)
                pe.wait_ge(*scanned.at(1))
                for bank, src in ((1, a), (2, nm)):
                    for i in range(4):
                        mm = nc.tensor.transpose(g.psum[:, bank, i * 64:i * 64 + 64], src[:, i * P:i * P + P],
                                                 g.ident[0:64, 0:64])
                    mm.then_inc(turned.up(), 1)


def mlstm_inputs(g, xmT, xcT, qT, kT, v):
    nc, t = g.nc, g.t
    loaded = g.sem("blocks_loaded")
    built, summed, silued, made, moved = (g.counter("mx_" + n) for n in ("built", "summed", "silued", "made", "moved"))
    with ExitStack() as ctx:
        wl = g.sb("block_w", [P, 3, 4, 4], ctx=ctx)
        bd = g.sb("block_diag", [P, 3, 4, P], ctx=ctx)
        with nc.Block() as block:

            @block.sync
            def _(sp):
                for i, n in enumerate(("w_q_blk_2", "w_k_blk_2", "w_v_blk_2")):
                    sp.dma_start(wl[:, i], t[n][0].rearrange("(h g) i j -> (g i) h j", h=4)).then_inc(loaded, 16)
                g.prefetch(sp, g.taken)

            @block.gpsimd
            def _(pool):
                pool.wait_ge(loaded, 48)
                for i in range(3):
                    for h in range(4):
                        o = bd[:, i, h].rearrange("p (b j) -> p b j", j=4)
                        src = wl[:, i, h].unsqueeze(1).to_broadcast([P, 32, 4])
                        g.plink(nc.gpsimd.affine_select(out=o, in_=src, compare_op=ALU.is_ge, fill=0.0, base=0,
                                                        pattern=[[-4, 32], [0, 4]], channel_multiplier=1))
                        nc.gpsimd.affine_select(out=o, in_=o, compare_op=ALU.is_ge, fill=0.0, base=3,
                                                pattern=[[4, 32], [0, 4]], channel_multiplier=-1).then_inc(
                            built.up(), 1)

            @block.vector
            def _(dve):
                for m in range(4):
                    x, c = xmT[:, m, :], xcT[:, m, :]
                    w = [g.cols[:, COLS["conv_w_2"] + 4 * j + m:COLS["conv_w_2"] + 4 * j + m + 1] for j in range(5)]
                    g.vlink(nc.vector.tensor_scalar(c, x, w[2], None, ALU.mult))
                    for j in (0, 1, 3, 4):
                        d = j - 2
                        co, xi = (c[:, -d:SEQ], x[:, 0:SEQ + d]) if d < 0 else (c[:, 0:SEQ - d], x[:, d:SEQ])
                        ins = nc.vector.scalar_tensor_tensor(co, xi, w[j], co, ALU.mult, ALU.add)
                        if j < 4:
                            g.vlink(ins)
                    ins.then_inc(summed.up(), 1)
                g.vlink(nc.vector.memset(v[:, :, :, P:P + 1], 1.0))
                for u in range(12):
                    dve.wait_ge(*made.at(u + 1))
                    h, ps = u // 3, g.psum[:, u % 8, :]
                    if u % 3 == 0:
                        ins = nc.vector.tensor_copy(qT[:, h, :], ps)
                    elif u % 3 == 1:
                        ins = nc.vector.tensor_scalar(kT[:, h, :], ps, float(P) ** -0.5, None, ALU.mult)
                    else:
                        ins = nc.vector.tensor_copy(v[:, :, h, 0:P], ps.rearrange("p (t e) -> p t e", e=P))
                    ins.then_inc(moved.up(), 1)

            @block.scalar
            def _(act):
                for m in range(4):
                    act.wait_ge(*summed.at(m + 1))
                    b = COLS["conv_b_2"] + m
                    nc.scalar.activation(xcT[:, m, :], xcT[:, m, :], ACT.Silu, bias=g.cols[:, b:b + 1]).then_inc(
                        silued.up(), 1)

            @block.tensor
            def _(pe):
                pe.wait_ge(*built.at(12))
                for u in range(12):
                    h, what = u // 3, u % 3
                    if u >= 8:
                        pe.wait_ge(*moved.at(u - 7))
                    pe.wait_ge(*silued.at(h + 1))
                    if what < 2:
                        mm = nc.tensor.matmul(g.psum[:, u % 8, :], bd[:, what, h, :], xcT[:, h, :], start=True,
                                              stop=True)
                    else:
                        for j in range(4):
                            mm = nc.tensor.matmul(g.psum[:, u % 8, j * P:j * P + P], xmT[:, h, j * P:j * P + P],
                                                  bd[:, 2, h, :], start=True, stop=True)
                    mm.then_inc(made.up(), 1)


def mlstm_scan(g, qT, kT, v, aT, enT, mrow, spare, hr):
    nc = g.nc
    s_s, s_m, s_diff, s_exp, s_w, s_mask, s_num, s_fin = (g.counter("ml_" + n) for n in (
        "scores", "mrow", "diff", "exp", "weighted", "masked", "num", "finished"))
    units = [(h, d) for h in range(4) for d in range(2)]

    def span(d, j):
        return (j * P, SEQ) if d == 0 else (0, (j + 1) * P)

    with ExitStack() as ctx:
        e = g.sb("ml_e", [P, 3, SEQ], ctx=ctx)
        w = [spare, g.sb("ml_w", [P, NT, SEQ], ctx=ctx)]
        den = g.sb("ml_den", [P, 2, NT], ctx=ctx)
        with nc.Block() as block:

            @block.sync
            def _(sp):
                g.prefetch(sp, g.taken)

            @block.tensor
            def _(pe):
                def numerator(n):
                    h, d = units[n]
                    pe.wait_ge(*s_mask.at(4 * n + 4))
                    if n >= 1:
                        pe.wait_ge(*s_fin.at(n))
                    for tt in range(NT):
                        js = range(0, tt + 1) if d == 0 else range(tt, NT)
                        o = g.psum[:, 6 + tt // 2, (tt % 2) * 256:(tt % 2) * 256 + P + 1]
                        for j in js:
                            mm = nc.tensor.matmul(o, w[n % 2][:, j, tt * P:tt * P + P], v[:, j, h, :],
                                                  start=(j == js[0]), stop=(j == js[-1]))
                    mm.then_inc(s_num.up(), 1)

                for n, (h, d) in enumerate(units):
                    if d == 0:
                        if n:
                            pe.wait_ge(*s_w.at(4 * n))
                        for j in range(NT):
                            mm = nc.tensor.matmul(g.psum[:, j, :], kT[:, h, j * P:j * P + P], qT[:, h, :],
                                                  start=True, stop=True)
                        mm.then_inc(s_s.up(), 1)
                    r = 32 * d + h
                    if n >= 2:
                        pe.wait_ge(*s_diff.at(4 * (n - 1)))
                    nc.tensor.matmul(g.psum[:, 4 + n % 2, :], g.ident[0:64, r:r + 1].to_broadcast([64, P]), mrow[:],
                                     start=True, stop=True).then_inc(s_m.up(), 1)
                    if n:
                        numerator(n - 1)
                numerator(len(units) - 1)

            @block.vector
            def _(dve):
                def difference(s):
                    n, j = s // 4, s % 4
                    h, d = units[n]
                    a, z = span(d, j)
                    dve.wait_ge(*s_m.at(n + 1))
                    if s >= 3:
                        dve.wait_ge(*s_w.at(s - 2))
                    r = 32 * d + h
                    nc.vector.tensor_scalar(e[:, s % 3, a:z], g.psum[:, 4 + n % 2, a:z], aT[:, j, r:r + 1], 0.0,
                                            ALU.subtract, ALU.max).then_inc(s_diff.up(), 1)

                def weigh(s):
                    n, j = s // 4, s % 4
                    h, d = units[n]
                    a, z = span(d, j)
                    dve.wait_ge(*s_exp.at(s + 1))
                    dve.wait_ge(*s_s.at(h + 1))
                    if n >= 2:
                        dve.wait_ge(*s_num.at(n - 1))
                    nc.vector.tensor_tensor(w[n % 2][:, j, a:z], e[:, s % 3, a:z], g.psum[:, j, a:z],
                                            ALU.mult).then_inc(s_w.up(), 1)

                def finish(n):
                    h, d = units[n]
                    r = 32 * d + h
                    dve.wait_ge(*s_num.at(n + 1))
                    sums = [g.psum[:, 6 + tt // 2, (tt % 2) * 256 + P:(tt % 2) * 256 + P + 1] for tt in range(NT)]
                    for tt in range(NT):
                        ins = nc.vector.scalar_tensor_tensor(den[:, 0, tt:tt + 1], sums[tt], -1.0,
                                                             enT[:, tt, r:r + 1], ALU.mult, ALU.max)
                    g.vlink(ins)
                    for tt in range(NT):
                        ins = nc.vector.tensor_tensor(den[:, 0, tt:tt + 1], sums[tt], den[:, 0, tt:tt + 1], ALU.max)
                    g.vlink(ins)
                    g.vlink(nc.vector.reciprocal(den[:, 1, :], den[:, 0, :]))
                    for tt in range(NT):
                        c = (tt % 2) * 256
                        o, num = hr[:, tt, h * P:h * P + P], g.psum[:, 6 + tt // 2, c:c + P]
                        if d == 0:
                            ins = nc.vector.tensor_scalar(o, num, den[:, 1, tt:tt + 1], None, ALU.mult)
                        else:
                            ins = nc.vector.scalar_tensor_tensor(o, num, den[:, 1, tt:tt + 1], o, ALU.mult, ALU.add)
                    ins.then_inc(s_fin.up(), 1)
                    dve.wait_ge(*s_fin.at(n + 1))

                for s in range(4 * len(units) + 1):
                    new_head = s % 8 == 0
                    if s >= 1 and new_head:
                        weigh(s - 1)
                    if s < 4 * len(units):
                        difference(s)
                    if s >= 1 and not new_head:
                        weigh(s - 1)
                    if s % 4 == 0 and s >= 8:
                        finish(s // 4 - 2)
                finish(len(units) - 1)

            @block.scalar
            def _(act):
                for s in range(4 * len(units)):
                    a, z = span(units[s // 4][1], s % 4)
                    act.wait_ge(*s_diff.at(s + 1))
                    nc.scalar.activation(e[:, s % 3, a:z], e[:, s % 3, a:z], ACT.Exp, scale=-1.0).then_inc(
                        s_exp.up(), 1)

            @block.gpsimd
            def _(pool):
                for s in range(4 * len(units)):
                    n, j = s // 4, s % 4
                    pool.wait_ge(*s_w.at(s + 1))
                    b = w[n % 2][:, j, j * P:j * P + P]
                    sign = 1 if units[n][1] == 0 else -1
                    nc.gpsimd.affine_select(out=b, in_=b, compare_op=ALU.is_ge, fill=0.0, base=0,
                                            pattern=[[sign, P]], channel_multiplier=-sign).then_inc(s_mask.up(), 1)


def mlstm(g, xmT, o, hr):
    nc, t = g.nc, g.t
    with ExitStack() as ctx:
        xcT = g.sb("xcT", [P, 4, SEQ], ctx=ctx)
        with ExitStack() as c2:
            aT, enT = g.sb("aT", [P, NT, 64], ctx=c2), g.sb("enT", [P, NT, 64], ctx=c2)
            mrow = g.sb("mrow", [64, SEQ], ctx=c2)
            gate_rows(g, g.hT, aT, enT, mrow)
            v = g.sb("ml_v", [P, NT, 4, P + 1], ctx=c2)
            qT, kT = g.hT[:, 0:4, :], g.hT[:, 4:8, :]
            mlstm_inputs(g, xmT, xcT, qT, kT, v)
            mlstm_scan(g, qT, kT, v, aT, enT, mrow, xmT, hr)
        head_norm(g, "ml_norm", [(heads(hr[:], P), None)])
        xc = g.sb("xc_rows", [P, NT, BANK], ctx=ctx)
        transpose_rows(g, "ml_xc", [(xc[:, i, :], [xcT[:, m, i * P:i * P + P] for m in range(4)])
                                    for i in range(NT)])
        rows = g.sb("ml_rows", [P, 2, BANK], ctx=ctx)
        loaded, gated = g.sem("ml_rows_loaded"), g.counter("sigmoid")
        with nc.Block() as block:

            @block.sync
            def _(sp):
                sp.dma_start(rows[:, 0, :], spread(t["mlstm_norm_g_2"], BANK)).then_inc(loaded, 16)
                sp.dma_start(rows[:, 1, :], spread(t["mlstm_skip_2"], BANK)).then_inc(loaded, 16)
                g.prefetch(sp, g.taken)

            @block.scalar
            def _(act):
                nc.scalar.activation(o, o, ACT.Sigmoid).then_inc(gated.up(), 1)

            @block.vector
            def _(dve):
                dve.wait_ge(loaded, 32)
                gain, skip = (rows[:, i, :].unsqueeze(1).to_broadcast([P, NT, BANK]) for i in range(2))
                nc.vector.tensor_tensor(xc[:], xc[:], skip, ALU.mult)
                g.vlink(nc.vector.tensor_tensor(hr[:], hr[:], gain, ALU.mult))
                g.vlink(nc.vector.tensor_tensor(hr[:], hr[:], xc[:], ALU.add))
                dve.wait_ge(*gated.at(1))
                nc.vector.tensor_tensor(hr[:], hr[:], o, ALU.mult)


def distance_bias(g, bias):
    nc, t = g.nc, g.t
    scratch = nc.dram_tensor("distance_scratch", (8, P, 1024), F32, kind="Internal").ap()
    loaded = g.sem("distance_loaded")
    written = [g.sem(f"distance_written_{i}") for i in range(2)]
    back = g.sem("distance_back")
    spread_, added = g.counter("distance_spread"), g.counter("distance_added")
    with ExitStack() as ctx:
        hot, rb = g.sb("bucket_hot", [32, 1024], ctx=ctx), g.sb("rel_bias", [32, 8], ctx=ctx)
        logs = g.sb("window_logs", [P, 1024], ctx=ctx)
        wide = g.sb("distance_wide", [P, 2, 1024], ctx=ctx)
        with nc.Block() as block:

            @block.sync
            def _(sp):
                sp.dma_start(hot[:], t["bucket_hot"]).then_inc(loaded, 16)
                sp.dma_start(rb[:], t["rel_bias_2"]).then_inc(loaded, 16)
                sp.dma_start(logs[:], spread(t["window_logs"], 1024)).then_inc(loaded, 16)
                g.prefetch(sp, g.taken)
                for h in range(8):
                    sp.wait_ge(*added.at(2 * h + 2))
                    sp.dma_start(scratch[h], wide[:, h % 2, :]).then_inc(written[h % 2], 16)
                    sp.wait_ge(written[h % 2], 16 * (h // 2 + 1))
                    src = bass.AP(scratch.tensor, scratch[h].offset + 127, [[1023, P], [1, 896]])
                    sp.dma_start(bias[:, h, :], src).then_inc(back, 16)
                sp.wait_ge(back, 16 * 8)

            @block.tensor
            def _(pe):
                pe.wait_ge(loaded, 48)
                for u in range(16):
                    if u >= 8:
                        pe.wait_ge(*added.at(u - 7))
                    h, c = u // 2, u % 2
                    nc.tensor.matmul(g.psum[:, u % 8, :], rb[:, h:h + 1].to_broadcast([32, P]),
                                     hot[:, c * BANK:c * BANK + BANK], start=True, stop=True).then_inc(
                        spread_.up(), 1)

            @block.vector
            def _(dve):
                for u in range(16):
                    h, c = u // 2, u % 2
                    dve.wait_ge(*spread_.at(u + 1))
                    if h >= 2:
                        dve.wait_ge(written[h % 2], 16 * (h // 2))
                    nc.vector.scalar_tensor_tensor(wide[:, h % 2, c * BANK:c * BANK + BANK], g.psum[:, u % 8, :], 8.0,
                                                   logs[:, c * BANK:c * BANK + BANK], ALU.mult, ALU.add).then_inc(
                        added.up(), 1)


def route(g, h2, xin, slots_gated):
    nc, t = g.nc, g.t
    E = EXPERTS
    loaded = g.sem("router_loaded")
    s_log, s_pk, s_exp, s_aff, s_turn, s_pos, s_back, s_hot, s_gat, s_read, s_gh, s_gt, s_mv = (
        g.counter("route_" + n) for n in ("logits", "peak", "exp", "affinity", "turned", "positions", "back", "hot",
                                         "gathered", "gather_read", "gated", "gated_turned", "gated_moved"))
    with ExitStack() as ctx:
        wr, br = g.sb("w_router", [P, KD, E], ctx=ctx), g.sb("b_router", [P, E], ctx=ctx)
        hot = g.sb("slot_hot", [P, NT, E * CAP], ctx=ctx)
        aff = g.sb("affinity", [P, NT, E], ctx=ctx)
        st = g.sb("route_stats", [P, 3, NT], ctx=ctx)
        A, wk, eq, run = (g.sb("route_" + n, [E, SEQ], ctx=ctx) for n in ("a", "work", "equal", "running"))
        top, cnt = g.sb("route_top", [E, 8], ctx=ctx), g.sb("route_count", [E, 1], ctx=ctx)
        pos = g.sb("route_pos", [P, NT, E], ctx=ctx)
        slot = g.sb("slot_numbers", [P, CAP], ctx=ctx)
        numbered = g.counter("route_numbered")
        with nc.Block() as block:

            @block.sync
            def _(sp):
                sp.dma_start(wr[:], t["w_router_2"][0].rearrange("(k p) e -> p k e", p=P)).then_inc(loaded, 16)
                sp.dma_start(br[:], spread(t["b_router_2"], E)).then_inc(loaded, 16)

            @block.gpsimd
            def _(pool):
                nc.gpsimd.iota(slot[:], [[1, CAP]], base=0, channel_multiplier=0,
                               allow_small_or_imprecise_dtypes=True).then_inc(numbered.up(), 1)

            @block.tensor
            def _(pe):
                pe.wait_ge(loaded, 32)
                for i in range(NT):
                    for k in range(KD):
                        mm = nc.tensor.matmul(g.psum[:, i, 0:E], g.hT[:, k, i * P:i * P + P], wr[:, k, :],
                                              start=(k == 0), stop=(k == KD - 1))
                mm.then_inc(s_log.up(), 1)
                pe.wait_ge(*s_aff.at(1))
                for i in range(NT):
                    mm = nc.tensor.transpose(g.psum[0:E, 4, i * P:i * P + P], aff[:, i, :], g.ident[:])
                mm.then_inc(s_turn.up(), 1)
                pe.wait_ge(*s_pos.at(1))
                for i in range(NT):
                    mm = nc.tensor.transpose(g.psum[:, 5, i * E:i * E + E], run[:, i * P:i * P + P],
                                             g.ident[0:E, 0:E])
                mm.then_inc(s_back.up(), 1)
                pe.wait_ge(*s_hot.at(1))
                for u in range(16):
                    k, c = u // 2, u % 2
                    if u >= 6:
                        pe.wait_ge(*s_read.at(u - 5))
                    for i in range(NT):
                        mm = nc.tensor.matmul(g.psum[:, u % 6, :], h2[:, i, k * P:k * P + P],
                                              hot[:, i, c * BANK:c * BANK + BANK], start=(i == 0), stop=(i == NT - 1))
                    mm.then_inc(s_gat.up(), 1)
                pe.wait_ge(*s_gh.at(1))
                for u in range(8):
                    if u >= 2:
                        pe.wait_ge(*s_mv.at(u - 1))
                    for i in range(NT):
                        mm = nc.tensor.transpose(g.psum[:, 6 + u % 2, i * P:i * P + P], hot[:, i, u * P:u * P + P],
                                                 g.ident[:])
                    mm.then_inc(s_gt.up(), 1)

            @block.scalar
            def _(act):
                act.wait_ge(*s_pk.at(1))
                for i in range(NT):
                    ins = nc.scalar.activation(aff[:, i, :], aff[:, i, :], ACT.Exp, bias=st[:, 1, i:i + 1],
                                               accum_out=st[:, 2, i:i + 1])
                g.alink(ins)
                nc.scalar.activation(br[:, 0:1], br[:, 0:1], ACT.Copy).then_inc(s_exp.up(), 1)

            @block.vector
            def _(dve):
                dve.wait_ge(*s_log.at(1))
                for i in range(NT):
                    ins = nc.vector.tensor_tensor_reduce(aff[:, i, :], g.psum[:, i, 0:E], br[:], 1.0, NEG * 10,
                                                         ALU.add, ALU.max, st[:, 0, i:i + 1])
                g.vlink(ins)
                nc.vector.tensor_scalar(st[:, 1, :], st[:, 0, :], -1.0, None, ALU.mult).then_inc(s_pk.up(), 1)
                dve.wait_ge(*s_exp.at(1))
                g.vlink(nc.vector.reciprocal(st[:, 0, :], st[:, 2, :]))
                r = st[:, 0, :].unsqueeze(2).to_broadcast([P, NT, E])
                nc.vector.tensor_tensor(aff[:], aff[:], r, ALU.mult).then_inc(s_aff.up(), 1)
                dve.wait_ge(*s_turn.at(1))
                g.vlink(nc.vector.tensor_copy(A[:], g.psum[0:E, 4, :]))
                src = A[:]
                for r8 in range(CAP // 8):
                    g.vlink(nc.vector.max(top[:], src))
                    if r8 < CAP // 8 - 1:
                        g.vlink(nc.vector.match_replace(wk[:], top[:], src, -1.0))
                        src = wk[:]
                thr = top[:, 7:8]
                g.vlink(nc.vector.tensor_scalar(wk[:], A[:], thr, None, ALU.is_gt, ALU.add, cnt[:]))
                g.vlink(nc.vector.tensor_scalar(eq[:], A[:], thr, None, ALU.is_equal))
                g.vlink(nc.vector.tensor_scalar(cnt[:], cnt[:], -1.0, float(CAP), ALU.mult, ALU.add))
                g.vlink(nc.vector.tensor_tensor_scan(run[:], eq[:], eq[:], 0.0, ALU.add, ALU.bypass))
                g.vlink(nc.vector.scalar_tensor_tensor(eq[:], run[:], cnt[:], eq[:], ALU.is_le, ALU.mult))
                g.vlink(nc.vector.tensor_tensor(wk[:], wk[:], eq[:], ALU.add))
                g.vlink(nc.vector.tensor_tensor_scan(eq[:], wk[:], wk[:], 0.0, ALU.add, ALU.bypass))
                g.vlink(nc.vector.tensor_tensor(eq[:], eq[:], wk[:], ALU.mult))
                nc.vector.tensor_scalar(run[:], eq[:], -1.0, None, ALU.add).then_inc(s_pos.up(), 1)
                dve.wait_ge(*s_back.at(1))
                g.vlink(nc.vector.tensor_copy(pos[:], g.psum[:, 5, 0:NT * E].rearrange("p (t e) -> p t e", e=E)))
                dve.wait_ge(*numbered.at(1))
                for i in range(NT):
                    o = hot[:, i, :].rearrange("p (e s) -> p e s", s=CAP)
                    ins = nc.vector.tensor_tensor(o, slot[:].unsqueeze(1).to_broadcast([P, E, CAP]),
                                                  pos[:, i, :].unsqueeze(2).to_broadcast([P, E, CAP]), ALU.is_equal)
                ins.then_inc(s_hot.up(), 1)
                for u in range(16):
                    k, c = u // 2, u % 2
                    dve.wait_ge(*s_gat.at(u + 1))
                    nc.vector.tensor_copy(xin[:, k, c * BANK:c * BANK + BANK], g.psum[:, u % 6, :]).then_inc(
                        s_read.up(), 1)
                for i in range(NT):
                    o = hot[:, i, :].rearrange("p (e s) -> p e s", s=CAP)
                    ins = nc.vector.tensor_tensor(o, o, aff[:, i, :].unsqueeze(2).to_broadcast([P, E, CAP]), ALU.mult)
                ins.then_inc(s_gh.up(), 1)
                for u in range(8):
                    dve.wait_ge(*s_gt.at(u + 1))
                    nc.vector.tensor_copy(slots_gated[:, u, :], g.psum[:, 6 + u % 2, :]).then_inc(s_mv.up(), 1)


def experts(g, xin, y, spare):
    nc, t = g.nc, g.t
    pairs, nf = EXPERTS // 2, FE // BANK
    per = 4 * nf + 8
    base, g0 = g.tiles, g.taken
    wg, wu, wd = (t[n].rearrange("a e (k p) n -> (a e) p k n", p=P) for n in ("w_gate_2", "w_up_2", "w_down_2"))
    s_hid, s_turn, s_copy, s_y = (g.counter("ex_" + n) for n in ("hidden", "turned", "copied", "y"))

    def slot_of(j):
        return (g0 + j) % RING

    def landed_at(j):
        return 16 * ((g0 + j) // RING + 1)

    with ExitStack() as ctx:
        xc = g.sb("ex_x", [P, KD, P], ctx=ctx)
        hT = spare[:, 0:FE].rearrange("p (f s) -> p f s", s=P)
        hid, act_g = (spare[:, a:a + 2 * BANK].rearrange("p (b n) -> p b n", b=2) for a in (FE, FE + 2 * BANK))

        with nc.Block() as block:

            @block.gpsimd
            def _(pool):
                for q in range(8):
                    nc.gpsimd.memset(hid[:, 0, q:q + 1], 0.0).then_inc((s_hid, s_y, s_turn, s_copy)[q // 2].up(), 1)

        s_x, s_silu, s_hid, s_turn, s_copy, s_y = (g.counter("ex_" + n) for n in (
            "x", "silu", "hidden", "turned", "copied", "y"))
        with nc.Block() as block:

            @block.sync
            def _(sp):
                with sp.Fori(0, pairs) as i:
                    for j in range(per):
                        sp.wait_ge(g.tiles_done, i * per + (base + j + 1 - RING))
                        if j < 4 * nf:
                            b, what, e = j // 4, (j // 2) % 2, j % 2
                            src = (wg, wu)[what][i * 2 + e, :, :, b * BANK:b * BANK + BANK]
                        else:
                            jj = j - 4 * nf
                            b, kg, e = jj // 4, (jj // 2) % 2, jj % 2
                            src = wd[i * 2 + e, :, kg * KD:kg * KD + KD, b * BANK:b * BANK + BANK]
                        dst = g.ring[:, slot_of(j), :].rearrange("p (k n) -> p k n", k=KD)
                        sp.dma_start(dst, src).then_inc(g.landed[slot_of(j)], 16)

            @block.tensor
            def _(pe):
                def pair_of_groups(i, j, bank, lhs, start, stop):
                    ws = [g.ring[:, slot_of(j + e), :].rearrange("p (k n) -> p k n", k=KD) for e in range(2)]
                    for e in range(2):
                        pe.wait_ge(g.landed[slot_of(j + e)], i * (16 * per // RING) + landed_at(j + e))
                    for k in range(KD):
                        for e in range(2):
                            mm = nc.tensor.matmul(g.psum[64 * e:64 * e + 64, bank, :], lhs(k)[:, 64 * e:64 * e + 64],
                                                  ws[e][:, k, :], start=(start and k == 0), stop=(stop and k == KD - 1))
                            if k == KD - 1:
                                mm.then_inc(g.tiles_done, 1)

                def turn(i, b):
                    pe.wait_ge(s_hid.sem, i * nf + (s_hid.base + b + 1))
                    pe.wait_ge(s_copy.sem, i * nf + (s_copy.base + b - 1))
                    for c in range(4):
                        mm = nc.tensor.transpose(g.psum[:, 4 + b % 2, c * P:c * P + P], hid[:, b % 2, c * P:c * P + P],
                                                 g.ident[:])
                    mm.then_inc(s_turn.up(), 1)

                with pe.Fori(0, pairs) as i:
                    pe.wait_ge(s_x.sem, i + (s_x.base + 1))
                    for b in range(nf):
                        pe.wait_ge(s_hid.sem, i * nf + (s_hid.base + b - 1))
                        pair_of_groups(i, 4 * b, (b % 2) * 2, lambda k: xc[:, k, :], True, True)
                        pair_of_groups(i, 4 * b + 2, (b % 2) * 2 + 1, lambda k: xc[:, k, :], True, True)
                        if b:
                            turn(i, b - 1)
                    turn(i, nf - 1)
                    pe.wait_ge(s_copy.sem, i * nf + (s_copy.base + nf))
                    for b in range(2):
                        pe.wait_ge(s_y.sem, i * 2 + (s_y.base + b - 1))
                        for kg in range(2):
                            pair_of_groups(i, 4 * nf + 4 * b + 2 * kg, 6 + b, lambda k: hT[:, kg * KD + k, :],
                                           kg == 0, kg == 1)

            @block.scalar
            def _(act):
                def copied(i, b):
                    act.wait_ge(s_turn.sem, i * nf + (s_turn.base + b + 1))
                    nc.scalar.activation(hT[:, 4 * b:4 * b + 4, :],
                                         g.psum[:, 4 + b % 2, :].rearrange("p (c s) -> p c s", c=4),
                                         ACT.Copy).then_inc(s_copy.up(), 1)

                with act.Fori(0, pairs) as i:
                    for b in range(nf):
                        act.wait_ge(g.tiles_done, i * per + (base + 4 * b + 2))
                        act.wait_ge(s_hid.sem, i * nf + (s_hid.base + b - 1))
                        nc.scalar.activation(act_g[:, b % 2, :], g.psum[:, (b % 2) * 2, :], ACT.Silu).then_inc(
                            s_silu.up(), 1)
                        if b:
                            copied(i, b - 1)
                    copied(i, nf - 1)

            @block.vector
            def _(dve):
                with dve.Fori(0, pairs) as i:
                    dve.wait_ge(s_turn.sem, i * nf + s_turn.base)
                    nc.vector.tensor_copy(xc[:], xin[:, :, bass.ds(i * P, P)]).then_inc(s_x.up(), 1)
                    for b in range(nf):
                        dve.wait_ge(s_silu.sem, i * nf + (s_silu.base + b + 1))
                        dve.wait_ge(g.tiles_done, i * per + (base + 4 * b + 4))
                        dve.wait_ge(s_turn.sem, i * nf + (s_turn.base + b - 1))
                        nc.vector.tensor_tensor(hid[:, b % 2, :], g.psum[:, (b % 2) * 2 + 1, :], act_g[:, b % 2, :],
                                                ALU.mult).then_inc(s_hid.up(), 1)
                    for b in range(2):
                        dve.wait_ge(g.tiles_done, i * per + (base + 4 * nf + 4 * b + 4))
                        nc.vector.tensor_copy(y[:, bass.ds(i, 1), b * BANK:b * BANK + BANK],
                                              g.psum[:, 6 + b, :].unsqueeze(1)).then_inc(s_y.up(), 1)


def combine(g, slots_gated, y, gate2, out):
    nc = g.nc
    summed, read, added = g.counter("combine_summed"), g.counter("combine_read"), g.counter("combine_added")
    done = g.sem("out_written")
    rows = out[0].rearrange("(t p) d -> p t d", p=P)
    with ExitStack() as ctx:
        tmp = g.sb("combine_tmp", [P, 2, BANK], ctx=ctx)
        with nc.Block() as block:

            @block.tensor
            def _(pe):
                for u in range(2 * NT):
                    i, c = u // 2, u % 2
                    for e in range(EXPERTS // 2):
                        mm = nc.tensor.matmul(g.psum[:, u, :], slots_gated[:, e, i * P:i * P + P],
                                              y[:, e, c * BANK:c * BANK + BANK], start=(e == 0),
                                              stop=(e == EXPERTS // 2 - 1))
                    mm.then_inc(summed.up(), 1)

            @block.vector
            def _(dve):
                for u in range(2 * NT):
                    i, c = u // 2, u % 2
                    dve.wait_ge(*summed.at(u + 1))
                    g.vlink(nc.vector.tensor_tensor(tmp[:, u % 2, :], g.psum[:, u, :], gate2[:, c * BANK:c * BANK + BANK],
                                                    ALU.mult))
                    xs = g.x[:, i, c * BANK:c * BANK + BANK]
                    nc.vector.tensor_tensor(xs, tmp[:, u % 2, :], xs, ALU.add).then_inc(added.up(), 1)

            @block.sync
            def _(sp):
                for i in range(NT):
                    sp.wait_ge(*added.at(2 * i + 2))
                    sp.dma_start(rows[:, i, :], g.x[:, i, :]).then_inc(done, 16)
                sp.wait_ge(done, 16 * NT)


def second_block(g, out):
    nc = g.nc
    mod = g.sb("mod", [P, 6 * D])
    shift1, gain1, gate1, shift2, gain2, gate2 = (mod[:, i * D:i * D + D] for i in range(6))
    modulation(g, mod)
    norm_transpose(g, "s_norm", g.x[:], NT, g.hT, gain_row=gain1, shift_row=shift1)
    with ExitStack() as ctx:
        aq, ak, av, hr = (g.sb("s_" + n, [P, NT, BANK], ctx=ctx) for n in ("aq", "ak", "av", "hr"))
        with ExitStack() as c2:
            xmT = g.sb("s_xmT", [P, NT, SEQ], ctx=c2)
            o = mod[:, 0:2 * D].rearrange("p (t n) -> p t n", t=NT)
            project(g, "s_xm", 1, g.hT, lambda eng, b, m, ps, n: copy(eng, nc, xmT[:, m, :], ps), cols=True,
                    engines="va")
            dest = [o, aq, ak, av]
            project(g, "s_rows", 4, g.hT, lambda eng, b, m, ps, n: copy(eng, nc, dest[b][:, m, :], ps), engines="va")
            mlstm(g, xmT, o, hr)
        bias = g.sb("s_bias", [P, 8, 896], ctx=ctx)
        distance_bias(g, bias)
        head_norm(g, "s_qk", [(heads(aq[:], 64), g.gain["q_norm_g_2"]), (heads(ak[:], 64), g.gain["k_norm_g_2"])])
        QT, KT = g.hT[:, 0:4, :], g.hT[:, 4:8, :]
        transpose_rows(g, "s_T", [(dst[:, k, :], [src[:, i, k * P:k * P + P] for i in range(NT)])
                                  for dst, src in ((QT, aq), (KT, ak)) for k in range(4)])
        ya = aq
        units = [dict(q=[QT[64 * (h % 2):64 * (h % 2) + 64, h // 2, i * P:i * P + P]],
                      k=[KT[64 * (h % 2):64 * (h % 2) + 64, h // 2, :]], nk=SEQ,
                      bias=bias[:, h, 384 - P * i:896 - P * i], v=[av[:, j, h * 64:h * 64 + 64] for j in range(NT)],
                      out=ya[:, i, h * 64:h * 64 + 64]) for h in range(8) for i in range(NT)]
        attend(g, "s_att", units, 1, 64,
               lambda un, ps, r: nc.vector.tensor_scalar(un["out"], ps, r, None, ALU.mult), 0.125)
        transpose_rows(g, "s_yT", [(g.hT[:, 4 * s + k, :], [(hr, ya)[s][:, i, k * P:k * P + P] for i in range(NT)])
                                   for s in range(2) for k in range(4)])
        tmp = g.sb("s_tmp", [P, 2, BANK], ctx=ctx)

        def gated_add(eng, b, m, ps, n):
            g.vlink(eng.tensor_tensor(tmp[:, m % 2, :], ps, gate1[:, b * BANK:b * BANK + BANK], ALU.mult))
            xs = g.x[:, m, b * BANK:b * BANK + BANK]
            return eng.tensor_tensor(xs, tmp[:, m % 2, :], xs, ALU.add)

        project(g, "s_out", 2, g.hT, gated_add)
    with ExitStack() as ctx:
        xin = g.sb("xin", [P, KD, EXPERTS * CAP], ctx=ctx)
        with ExitStack() as c2:
            h2 = g.sb("h2_rows", [P, NT, D], ctx=c2)
            norm_transpose(g, "r_norm", g.x[:], NT, g.hT, gain_row=gain2, shift_row=shift2, keep=h2)
            route(g, h2, xin, g.hT)
        y = g.sb("expert_rows", [P, EXPERTS // 2, D], ctx=ctx)
        experts(g, xin, y, mod[:, 0:4 * D])
        combine(g, g.hT, y, gate2, out)


def build(nc, t, out):
    with ExitStack() as ctx:
        g = Program(nc, t, ctx)
        g.groups = weight_plan(t)
        constants(g)
        first_block(g)
        second_block(g, out)


_INS = ['x', 'mem', 'positions', 'g_mix', 'g_xattn', 'g_mem', 'g_mlp', 'wq_x', 'wkv_x', 'gq_x', 'gk_x', 'wo_x', 'w_up',
        'w_down', 'w_in_e', 'gq_a', 'gk_a', 'lam_q1', 'lam_k1', 'lam_q2', 'lam_k2', 'g_sub_a', 'g_kv_b', 'w_kv_up_b',
        'gq_b', 'gk_b', 'g_kidx', 'w_out_e', 'w_in_o', 'conv_w', 'w_pool', 'pool_scale', 'w_out_o', 'c_2', 'w_ada_2',
        'b_ada_2', 'norm1_g_2', 'w_in_2', 'conv_w_2', 'conv_b_2', 'w_q_blk_2', 'w_k_blk_2', 'w_v_blk_2', 'b_igate_2',
        'b_fgate_2', 'mlstm_norm_g_2', 'mlstm_skip_2', 'q_norm_g_2', 'k_norm_g_2', 'rel_bias_2', 'w_out_2',
        'norm2_g_2', 'w_router_2', 'b_router_2', 'w_gate_2', 'w_up_2', 'w_down_2']


def kernel(**inputs):
    import numpy as _np
    import concourse.bacc as _bacc
    from concourse import mybir as _mybir
    from concourse.bass_utils import run_bass_kernel_spmd as _run

    nc = _bacc.Bacc("TRN2", target_bir_lowering=False, num_devices=1)
    arrays, t = {}, {}
    for name in _INS:
        a = _np.ascontiguousarray(inputs[name])
        arrays[f"in_{name}"] = a
        t[name] = nc.dram_tensor(f"in_{name}", a.shape, _mybir.dt.from_np(a.dtype), kind="ExternalInput").ap()
    out = nc.dram_tensor("out", (1, SEQ, D), _mybir.dt.float32, kind="ExternalOutput").ap()
    for name, value in shape_constants().items():
        arrays[f"in_{name}"] = value
        t[name] = nc.dram_tensor(f"in_{name}", value.shape, _mybir.dt.float32, kind="ExternalInput").ap()
    build(nc, t, out)
    r = _run(nc, [arrays], core_ids=[0])
    return r.results[0]["out"]
```

```python
from contextlib import ExitStack

import numpy as np
import concourse.bass as bass
from concourse import mybir

F32 = mybir.dt.float32
I32 = mybir.dt.int32
ACT = mybir.ActivationFunctionType
ALU = mybir.AluOpType
AX = mybir.AxisListType

P = 128
SEQ = 512
NT = SEQ // P
D = 1024
KD = D // P
BANK = 512
RING = 4
EPS = 1e-6
NEG = -1e30
MEM = 256
FF = 4096
EXPERTS = 16
CAP = 64
FE = 2048


class Counter:

    def __init__(self, g, name):
        self.g, self.name, self.base = g, name, g.totals.setdefault(name, 0)
        self.sem = g.sems[name] if name in g.sems else g.sems.setdefault(name, g.sem(name))

    def up(self):
        self.g.totals[self.name] += 1
        return self.sem

    def at(self, n):
        return self.sem, self.base + n


class Program:

    def __init__(self, nc, t, ctx):
        self.nc, self.t, self.ctx = nc, t, ctx
        self.sems, self.totals = {}, {}
        self.ring = self.sb("ring", [P, RING, KD * BANK])
        self.landed = [self.sem(f"weights_landed_{s}") for s in range(RING)]
        self.tiles_done = self.sem("tiles_done")
        self.tiles = 0
        self.done_at = []
        self.groups = []
        self.issued = 0
        self.taken = 0
        self.dve_sem = self.sem("dve_chain")
        self.act_sem = self.sem("act_chain")
        self.pool_sem = self.sem("pool_chain")
        self.dve_n = self.act_n = self.pool_n = 0
        self.psum = ctx.enter_context(nc.psum_tensor("banks", [P, 8, BANK], F32))

    def sb(self, name, shape, dt=F32, ctx=None):
        return (ctx or self.ctx).enter_context(self.nc.sbuf_tensor(name, shape, dt))

    def sem(self, name):
        return self.ctx.enter_context(self.nc.semaphore(name))

    def counter(self, name):
        return Counter(self, name)

    def vlink(self, ins):
        self.dve_n += 1
        ins.then_inc(self.dve_sem, 1)
        self.nc.vector.wait_ge(self.dve_sem, self.dve_n)

    def vmark(self, ins):
        self.dve_n += 1
        ins.then_inc(self.dve_sem, 1)
        return self.dve_n

    def alink(self, ins):
        self.act_n += 1
        ins.then_inc(self.act_sem, 1)
        self.nc.scalar.wait_ge(self.act_sem, self.act_n)

    def plink(self, ins):
        self.pool_n += 1
        ins.then_inc(self.pool_sem, 1)
        self.nc.gpsimd.wait_ge(self.pool_sem, self.pool_n)

    def prefetch(self, sp, consumed):
        while self.issued < min(consumed + RING, len(self.groups)):
            g = self.issued
            if g >= RING:
                sp.wait_ge(self.tiles_done, self.done_at[g - RING])
            src, kc, n = self.groups[g]
            dst = self.slot(g, kc, n)
            sp.dma_start(dst, src).then_inc(self.landed[g % RING], 16)
            self.issued += 1

    def slot(self, g, kc, n):
        return self.ring[:, g % RING, 0:kc * n].rearrange("p (k n) -> p k n", k=kc)


def weight_plan(t):
    out = []

    def add(w, c0, c1, k0=0, k1=None):
        k1 = w.shape[0] // P if k1 is None else k1
        v = w.rearrange("(k p) n -> p k n", p=P)
        out.append((v[:, k0:k1, c0:c1], k1 - k0, c1 - c0))

    def blocks(w, step=BANK):
        for c in range(0, w.shape[1], step):
            add(w, c, min(c + step, w.shape[1]))

    for l in range(2):
        blocks(t["wkv_x"][l])
        if l == 0:
            for c in (2560, 2048, 0, 512, 1024, 1536):
                add(t["w_in_e"][0], c, min(c + BANK, t["w_in_e"].shape[2]))
            blocks(t["w_kv_up_b"][0])
            blocks(t["w_out_e"][0])
        else:
            blocks(t["w_in_o"][0])
            blocks(t["w_out_o"][0])
        blocks(t["wq_x"][l])
        blocks(t["wo_x"][l])
        blocks(t["w_up"][l])
        for c in range(0, D, BANK):
            for k in range(0, FF // P, KD):
                add(t["w_down"][l], c, c + BANK, k, k + KD)
    for c0, c1 in ((0, 512), (512, 1024), (1040, 1552), (1552, 2064), (2064, 2576)):
        add(t["w_in_2"][0], c0, c1)
    blocks(t["w_out_2"][0])
    return out


def project(g, name, groups, act, evac, cols=False, ntok=SEQ, kgroups=1, engines="v", beside=None):
    nc = g.nc
    free = {e: g.counter(f"bank_free_{e}") for e in engines}
    first = g.taken
    plan = g.groups[first:first + groups]

    def tiles(n):
        return (n + P - 1) // P if cols else ntok // P

    base = []
    for _, _, n in plan:
        base.append(g.tiles)
        g.tiles += tiles(n)
        g.done_at.append(g.tiles)

    units = [(b, m) for b in range(groups // kgroups) for m in range(tiles(plan[b * kgroups][2]))]
    who = [engines[u % len(engines)] for u in range(len(units))]
    turn = [sum(w == who[u] for w in who[:u + 1]) for u in range(len(units))]

    with nc.Block() as block:

        @block.sync
        def _(sp):
            g.prefetch(sp, first + groups)

        @block.tensor
        def _(pe):
            if beside:
                beside[0](pe)
            u0 = 0
            for b in range(groups // kgroups):
                src = act[b] if isinstance(act, list) else act
                for kg in range(kgroups):
                    gi = first + b * kgroups + kg
                    _, kc, n = g.groups[gi]
                    w = g.slot(gi, kc, n)
                    pe.wait_ge(g.landed[gi % RING], 16 * (gi // RING + 1))
                    for m in range(tiles(n)):
                        u = u0 + m
                        if kg == 0 and u >= 8:
                            pe.wait_ge(*free[who[u - 8]].at(turn[u - 8]))
                        for k in range(kc):
                            ka = kg * kc + k
                            if cols:
                                a, z = m * P, min(m * P + P, n)
                                o = g.psum[0:z - a, u % 8, 0:ntok]
                                mm = nc.tensor.matmul(o, w[:, k, a:z], src[:, ka, 0:ntok],
                                                      start=(ka == 0), stop=(ka == kc * kgroups - 1))
                            else:
                                mm = nc.tensor.matmul(g.psum[:, u % 8, 0:n], src[:, ka, m * P:m * P + P], w[:, k, :],
                                                      start=(ka == 0), stop=(ka == kc * kgroups - 1))
                        mm.then_inc(g.tiles_done, 1)
                u0 += tiles(n)

        def evacuate(eng, e):
            for u, (b, m) in enumerate(units):
                if who[u] != e:
                    continue
                n = plan[b * kgroups][2]
                eng.wait_ge(g.tiles_done, base[b * kgroups + kgroups - 1] + m + 1)
                rows = min(P, n - m * P) if cols else P
                width = ntok if cols else n
                evac(eng, b, m, g.psum[0:rows, u % 8, 0:width], n).then_inc(free[e].up(), 1)

        if "v" in engines:
            @block.vector
            def _(dve):
                evacuate(nc.vector, "v")

        if "a" in engines:
            @block.scalar
            def _(act_eng):
                if beside:
                    beside[1](act_eng)
                evacuate(nc.scalar, "a")
        if beside:
            @block.vector
            def _(dve):
                beside[2](dve)

            if len(beside) > 3:
                @block.gpsimd
                def _(pool):
                    beside[3](pool)

    g.taken = first + groups


def copy(eng, nc, out, in_):
    if eng is nc.scalar:
        return nc.scalar.activation(out, in_, ACT.Copy)
    return eng.tensor_copy(out, in_)


def newton_rstd(g, rstd, mean, tmp):
    nc = g.nc
    g.vlink(nc.vector.tensor_tensor(tmp, rstd, rstd, ALU.mult))
    g.vlink(nc.vector.tensor_tensor(tmp, tmp, mean, ALU.mult))
    g.vlink(nc.vector.tensor_scalar(tmp, tmp, -0.5, 1.5, ALU.mult, ALU.add))
    g.vlink(nc.vector.tensor_tensor(rstd, rstd, tmp, ALU.mult))


def norm_transpose(g, name, rows, nt, out, gain_col=None, gain_row=None, shift_row=None, keep=None):
    nc = g.nc
    squared, inverse, rooted = (g.counter(s) for s in ("squared", "inverse", "rooted"))
    ready, turned, moved = (g.counter(s) for s in ("rows_ready", "bank_turned", "bank_moved"))
    with ExitStack() as ctx:
        by_row = gain_row is not None
        if by_row:
            normed = keep if keep is not None else g.sb(name + "_normed", [P, nt, D], ctx=ctx)
        else:
            scaling = g.sb(name + "_scaling", [P, nt, P], ctx=ctx)
        square = g.sb(name + "_square", [P, 2, D], ctx=ctx)
        st = g.sb(name + "_stats", [P, 4, nt], ctx=ctx)
        total, mean, rstd, tmp = (st[:, i, :] for i in range(4))
        with nc.Block() as block:

            @block.sync
            def _(sp):
                g.prefetch(sp, g.taken)

            @block.scalar
            def _(act):
                for t in range(nt // 2):
                    g.alink(nc.scalar.activation(square[:, 0, :], rows[:, t, :], ACT.Square,
                                                 accum_out=total[:, t:t + 1]))
                nc.scalar.activation(square[:, 0, 0:1], total[:, 0:1], ACT.Copy).then_inc(squared.up(), 1)
                act.wait_ge(*inverse.at(1))
                nc.scalar.activation(rstd, tmp, ACT.Sqrt).then_inc(rooted.up(), 1)

            @block.vector
            def _(dve):
                for t in range(nt // 2, nt):
                    g.vlink(nc.vector.tensor_tensor_reduce(square[:, 1, :], rows[:, t, :], rows[:, t, :], 1.0, 0.0,
                                                           ALU.mult, ALU.add, total[:, t:t + 1]))
                dve.wait_ge(*squared.at(1))
                g.vlink(nc.vector.tensor_scalar(mean, total, 1.0 / D, EPS, ALU.mult, ALU.add))
                nc.vector.reciprocal(tmp, mean).then_inc(inverse.up(), 1)
                dve.wait_ge(*rooted.at(1))
                newton_rstd(g, rstd, mean, tmp)
                for t in range(nt):
                    if by_row:
                        g.vlink(nc.vector.scalar_tensor_tensor(normed[:, t, :], rows[:, t, :], rstd[:, t:t + 1],
                                                               gain_row, ALU.mult, ALU.mult))
                        ins = nc.vector.tensor_tensor(normed[:, t, :], normed[:, t, :], shift_row, ALU.add)
                    else:
                        ins = nc.vector.tensor_scalar(scaling[:, t, :], g.ident[:], rstd[:, t:t + 1], None, ALU.mult)
                    ins.then_inc(ready.up(), 1)
                for k in range(KD):
                    dve.wait_ge(*turned.at(k + 1))
                    if gain_col is not None:
                        nc.vector.tensor_scalar(out[:, k, 0:nt * P], g.psum[:, k, 0:nt * P], gain_col[:, k:k + 1],
                                                None, ALU.mult).then_inc(moved.up(), 1)
                    else:
                        nc.vector.tensor_copy(out[:, k, 0:nt * P], g.psum[:, k, 0:nt * P]).then_inc(moved.up(), 1)

            @block.tensor
            def _(pe):
                pe.wait_ge(*ready.at(nt))
                for k in range(KD):
                    for t in range(nt):
                        o, cols = g.psum[:, k, t * P:t * P + P], slice(k * P, k * P + P)
                        if by_row:
                            mm = nc.tensor.transpose(o, normed[:, t, cols], g.ident[:])
                        else:
                            mm = nc.tensor.matmul(o, rows[:, t, cols], scaling[:, t, :], start=True, stop=True)
                    mm.then_inc(turned.up(), 1)


def transpose_rows(g, name, jobs):
    nc = g.nc
    turned, moved = g.counter("bank_turned"), [g.counter("bank_moved"), g.counter("bank_moved_by_act")]
    with nc.Block() as block:

        @block.sync
        def _(sp):
            g.prefetch(sp, g.taken)

        @block.tensor
        def _(pe):
            for j, (out, tiles) in enumerate(jobs):
                if j >= 8:
                    pe.wait_ge(*moved[j % 2].at((j - 8) // 2 + 1))
                for i, tile in enumerate(tiles):
                    c = tile.shape[1]
                    mm = nc.tensor.transpose(g.psum[0:c, j % 8, i * P:i * P + P], tile, g.ident[:])
                mm.then_inc(turned.up(), 1)

        def move(eng, which):
            for j, (out, tiles) in enumerate(jobs):
                if j % 2 == which:
                    eng.wait_ge(*turned.at(j + 1))
                    src = g.psum[0:tiles[0].shape[1], j % 8, 0:len(tiles) * P]
                    copy(eng, nc, out, src).then_inc(moved[which].up(), 1)

        @block.vector
        def _(dve):
            move(nc.vector, 0)

        @block.scalar
        def _(act):
            move(nc.scalar, 1)


def head_norm(g, name, items):
    nc = g.nc
    squared, freed, inverse, rooted = (g.counter(s) for s in ("squared", "square_read", "inverse", "rooted"))
    most = max(x.shape[1] * x.shape[2] for x, _ in items)
    n = sum(x.shape[1] for x, _ in items)
    with ExitStack() as ctx:
        square = g.sb(name + "_square", [P, most], ctx=ctx)
        st = g.sb(name + "_stats", [P, 4, n], ctx=ctx)
        total, mean, rstd, tmp = (st[:, i, :] for i in range(4))
        with nc.Block() as block:

            @block.sync
            def _(sp):
                g.prefetch(sp, g.taken)

            @block.scalar
            def _(act):
                for i, (x, _) in enumerate(items):
                    if i:
                        act.wait_ge(*freed.at(i))
                    sq = square[:, 0:x.shape[1] * x.shape[2]].rearrange("p (a b) -> p a b", b=x.shape[2])
                    nc.scalar.activation(sq, x, ACT.Square).then_inc(squared.up(), 1)
                act.wait_ge(*inverse.at(1))
                nc.scalar.activation(rstd, tmp, ACT.Sqrt).then_inc(rooted.up(), 1)

            @block.vector
            def _(dve):
                at = 0
                for i, (x, _) in enumerate(items):
                    a, w = x.shape[1], x.shape[2]
                    dve.wait_ge(*squared.at(i + 1))
                    sq = square[:, 0:a * w].rearrange("p (a b) -> p a b", b=w)
                    ins = nc.vector.tensor_reduce(total[:, at:at + a], sq, AX.X, ALU.add)
                    g.vlink(ins)
                    g.vlink(nc.vector.tensor_scalar(mean[:, at:at + a], total[:, at:at + a], 1.0 / w, EPS,
                                                    ALU.mult, ALU.add))
                    nc.vector.reciprocal(tmp[:, at:at + a], mean[:, at:at + a]).then_inc(
                        (inverse if i == len(items) - 1 else freed).up(), 1)
                    at += a
                dve.wait_ge(*rooted.at(1))
                newton_rstd(g, rstd, mean, tmp)
                at = 0
                for x, gain in items:
                    a, w = x.shape[1], x.shape[2]
                    r = rstd[:, at:at + a].unsqueeze(2).to_broadcast([P, a, w])
                    g.vlink(nc.vector.tensor_tensor(x, x, r, ALU.mult))
                    if gain is not None:
                        gb = gain.unsqueeze(1).to_broadcast([P, a, w])
                        g.vlink(nc.vector.tensor_tensor(x, x, gb, ALU.mult))
                    at += a


def attend(g, name, units, comps, width, out_evac, mask_scale, warm=0):
    nc = g.nc
    U = len(units)
    lag = comps
    names = ("scores", "peak", "probs", "mixed", "turned", "copied", "out", "out_read")
    s_scores, s_peak, s_probs, s_mixed, s_turned, s_copied, s_out, s_read = (g.counter(s) for s in names)
    B = 2
    with ExitStack() as ctx:
        logits = g.sb(name + "_logits", [P, B, comps, BANK], ctx=ctx)
        probs = g.sb(name + "_probs", [P, B, comps, BANK], ctx=ctx)
        probsT = g.sb(name + "_probsT", [P, B, BANK], ctx=ctx)
        st = g.sb(name + "_stats", [P, 4, 4, comps], ctx=ctx)

        with nc.Block() as block:

            @block.sync
            def _(sp):
                g.prefetch(sp, g.taken)

            @block.tensor
            def _(pe):
                def scores(i):
                    un = units[i]
                    if i >= B:
                        pe.wait_ge(*s_peak.at(i - B + 1))
                    for c in range(comps):
                        mm = nc.tensor.matmul(g.psum[:, (i % B) * 2 + c, 0:un["nk"]], un["q"][c], un["k"][c],
                                              start=True, stop=True)
                    mm.then_inc(s_scores.up(), 1)

                def turn(i):
                    un = units[i]
                    pe.wait_ge(*(s_mixed if comps == 2 else s_probs).at(i + 1))
                    if i >= B:
                        pe.wait_ge(*s_copied.at(i - B + 1))
                    for j in range(un["nk"] // P):
                        mm = nc.tensor.transpose(g.psum[:, 4 + i % B, j * P:j * P + P],
                                                 probs[:, i % B, 0, j * P:j * P + P], g.ident[:])
                    mm.then_inc(s_turned.up(), 1)

                def values(i):
                    un = units[i]
                    pe.wait_ge(*s_copied.at(i + 1))
                    if i >= B:
                        pe.wait_ge(*s_read.at(i - B + 1))
                    n = un["nk"] // P
                    for j in range(n):
                        mm = nc.tensor.matmul(g.psum[:, 6 + i % B, 0:width], probsT[:, i % B, j * P:j * P + P],
                                              un["v"][j], start=(j == 0), stop=(j == n - 1))
                    mm.then_inc(s_out.up(), 1)

                def warm_up():
                    for _ in range(warm):
                        nc.tensor.matmul(g.psum[:, 7, :], g.ident[:], g.causal[:, 0:BANK], start=True, stop=True)

                for i in range(U + lag + 1):
                    if i < U:
                        scores(i)
                    if i == 0:
                        warm_up()
                    if 0 <= i - lag < U:
                        turn(i - lag)
                    if i > lag:
                        values(i - lag - 1)

            @block.vector
            def _(dve):
                def peak(i):
                    un = units[i]
                    dve.wait_ge(*s_scores.at(i + 1))
                    if i >= B:
                        dve.wait_ge(*s_probs.at(i - B + 1))
                    for c in range(comps):
                        ins = nc.vector.tensor_tensor_reduce(
                            logits[:, i % B, c, 0:un["nk"]], g.psum[:, (i % B) * 2 + c, 0:un["nk"]], un["bias"],
                            mask_scale, NEG * 10, ALU.add, ALU.max, st[:, i % 4, 0, c:c + 1])
                    g.vlink(ins)
                    nc.vector.tensor_scalar(st[:, i % 4, 1, :], st[:, i % 4, 0, :], -1.0, None,
                                            ALU.mult).then_inc(s_peak.up(), 1)

                def mix(i):
                    un = units[i]
                    dve.wait_ge(*s_probs.at(i + 1))
                    g.vlink(nc.vector.reciprocal(st[:, i % 4, 3, :], st[:, i % 4, 2, :]))
                    if comps == 2:
                        g.vlink(nc.vector.tensor_scalar(st[:, i % 4, 3, 1:2], st[:, i % 4, 3, 1:2], g.neg_lam[:, 0:1],
                                                        None, ALU.mult))
                        p0, p1 = (probs[:, i % B, c, 0:un["nk"]] for c in range(2))
                        g.vlink(nc.vector.tensor_scalar(p0, p0, st[:, i % 4, 3, 0:1], None, ALU.mult))
                        nc.vector.scalar_tensor_tensor(p0, p1, st[:, i % 4, 3, 1:2], p0, ALU.mult,
                                                       ALU.add).then_inc(s_mixed.up(), 1)

                def finish(i):
                    dve.wait_ge(*s_out.at(i + 1))
                    out_evac(units[i], g.psum[:, 6 + i % B, 0:width], st[:, i % 4, 3, 0:1]).then_inc(s_read.up(), 1)

                for i in range(U + lag + 1):
                    if i < U:
                        peak(i)
                    if 1 <= i <= U:
                        mix(i - 1)
                    if i > lag:
                        finish(i - lag - 1)

            @block.scalar
            def _(act):
                def exponent(i):
                    un = units[i]
                    act.wait_ge(*s_peak.at(i + 1))
                    if i >= B:
                        act.wait_ge(*s_turned.at(i - B + 1))
                    if i >= 4:
                        act.wait_ge(*s_read.at(i - 3))
                    for c in range(comps):
                        ins = nc.scalar.activation(probs[:, i % B, c, 0:un["nk"]], logits[:, i % B, c, 0:un["nk"]],
                                                   ACT.Exp, bias=st[:, i % 4, 1, c:c + 1],
                                                   accum_out=st[:, i % 4, 2, c:c + 1])
                    ins.then_inc(s_probs.up(), 1)

                def copy_turned(i):
                    un = units[i]
                    act.wait_ge(*s_turned.at(i + 1))
                    if i >= B:
                        act.wait_ge(*s_out.at(i - B + 1))
                    nc.scalar.activation(probsT[:, i % B, 0:un["nk"]], g.psum[:, 4 + i % B, 0:un["nk"]],
                                         ACT.Copy).then_inc(s_copied.up(), 1)

                for i in range(U + lag):
                    if i < U:
                        exponent(i)
                    if i >= lag:
                        copy_turned(i - lag)


COLS = dict(g_mix=0, g_xattn=16, g_mem=32, g_mlp=48, conv_w=64, pool_scale=76, conv_w_2=80, conv_b_2=100)
COL_ROWS = 104
ROW_GAINS = (("gq_a", 64), ("gk_a", 64), ("gq_b", 64), ("gk_b", 64), ("g_kidx", 64), ("g_sub_a", 128), ("g_kv_b", 256),
             ("gq_x", 256), ("gk_x", 256), ("q_norm_g_2", 64), ("k_norm_g_2", 64))


def spread(w, n):
    return bass.AP(w.tensor, w.offset, [[0, P], [1, n]])


def constants(g):
    nc, t = g.nc, g.t
    g.x = g.sb("x_rows", [P, NT, D])
    g.hT = g.sb("hT", [P, KD, SEQ])
    g.ident = g.sb("ident", [P, P])
    g.causal = g.sb("causal", [P, SEQ])
    g.zeros = g.sb("zeros", [P, MEM])
    g.cols = g.sb("cols", [P, COL_ROWS])
    g.rowg = g.sb("row_gains", [P, sum(n for _, n in ROW_GAINS)])
    g.cos, g.sin = g.sb("cos", [P, NT, 8]), g.sb("sin", [P, NT, 8])
    g.neg_lam = g.sb("neg_lam", [P, 1])
    g.gain = {}
    at = 0
    for name, n in ROW_GAINS:
        g.gain[name] = g.rowg[:, at:at + n]
        at += n
    loaded, x_loaded, made = g.sem("constants_loaded"), g.sem("x_loaded"), g.counter("tables_made")
    turned, zeroed = g.counter("cols_turned"), g.counter("constants_zeroed")
    reduced, sines, expo = g.counter("angles_reduced"), g.counter("sines"), g.counter("lambda_exp")
    inv = (np.float32(500000.0) ** (-np.arange(0, 16, 2, dtype=np.float32) / np.float32(16))).astype(np.float32)
    c1, c2 = 6.28125, 0.0019350051879882812
    c3 = 2 * np.pi - c1 - c2
    with ExitStack() as ctx:
        colrows = g.sb("col_rows", [COL_ROWS, P], ctx=ctx)
        pos = g.sb("positions", [P, NT], I32, ctx=ctx)
        posf = g.sb("positions_f", [P, NT], ctx=ctx)
        freq = g.sb("frequencies", [P, 8], ctx=ctx)
        ang, turns, rest = (g.sb(n, [P, NT, 8], ctx=ctx) for n in ("angle", "turns", "rest"))
        lamv = g.sb("lambda_vectors", [P, 4, 64], ctx=ctx)
        lams = g.sb("lambda_sums", [P, 4], ctx=ctx)
        junk = g.sb("lambda_products", [P, 64], ctx=ctx)
        loads = [
            (colrows[0:16], t["g_mix"].rearrange("l (k p) -> (l k) p", p=P)),
            (colrows[16:32], t["g_xattn"].rearrange("l (k p) -> (l k) p", p=P)),
            (colrows[32:48], t["g_mem"].rearrange("l (k p) -> (l k) p", p=P)),
            (colrows[48:64], t["g_mlp"].rearrange("l (k p) -> (l k) p", p=P)),
            (colrows[64:76], t["conv_w"][0].rearrange("j (k p) -> (j k) p", p=P)),
            (colrows[76:80], t["pool_scale"].rearrange("l (k p) -> (l k) p", p=P)),
            (colrows[80:100], t["conv_w_2"][0].rearrange("j (k p) -> (j k) p", p=P)),
            (colrows[100:104], t["conv_b_2"].rearrange("l (k p) -> (l k) p", p=P)),
            (pos[:], t["positions"][0].rearrange("(t p) -> p t", p=P)),
        ]
        loads += [(g.gain[name], spread(t[name], n)) for name, n in ROW_GAINS]
        loads += [(lamv[:, i, :], spread(t[n], 64)) for i, n in enumerate(("lam_q1", "lam_k1", "lam_q2", "lam_k2"))]
        with nc.Block() as block:

            @block.sync
            def _(sp):
                sp.dma_start(g.x[:], t["x"][0].rearrange("(t p) d -> p t d", p=P)).then_inc(x_loaded, 16)
                with nc.allow_non_contiguous_dma(reason="512 positions, one per partition and tile"):
                    for out, src in loads:
                        sp.dma_start(out, src).then_inc(loaded, 16)
                g.prefetch(sp, 0)
                sp.wait_ge(x_loaded, 16)
                sp.wait_ge(loaded, 16 * len(loads))

            @block.gpsimd
            def _(pool):
                nc.gpsimd.memset(g.zeros[:], 0.0).then_inc(zeroed.up(), 1)
                nc.gpsimd.memset(g.ident[:], 0.0).then_inc(zeroed.up(), 1)
                nc.gpsimd.memset(g.causal[:], 0.0).then_inc(zeroed.up(), 1)
                for i in range(8):
                    nc.gpsimd.memset(freq[:, i:i + 1], float(inv[i])).then_inc(zeroed.up(), 1)
                pool.wait_ge(*zeroed.at(11))
                nc.gpsimd.affine_select(out=g.ident[:], in_=g.ident[:], compare_op=ALU.not_equal, fill=1.0, base=0,
                                        pattern=[[-1, P]], channel_multiplier=1).then_inc(made.up(), 1)
                nc.gpsimd.affine_select(out=g.causal[:], in_=g.causal[:], compare_op=ALU.is_ge, fill=NEG,
                                        base=SEQ - P, pattern=[[-1, SEQ]], channel_multiplier=1).then_inc(made.up(), 1)

            @block.tensor
            def _(pe):
                pe.wait_ge(*made.at(2))
                pe.wait_ge(loaded, 16 * len(loads))
                nc.tensor.transpose(g.psum[:, 0, 0:COL_ROWS], colrows[:], g.ident[0:COL_ROWS, 0:COL_ROWS]).then_inc(
                    turned.up(), 1)

            @block.vector
            def _(dve):
                dve.wait_ge(loaded, 16 * len(loads))
                dve.wait_ge(*zeroed.at(11))
                g.vlink(nc.vector.tensor_copy(posf[:], pos[:]))
                f = freq[:].unsqueeze(1).to_broadcast([P, NT, 8])
                g.vlink(nc.vector.tensor_tensor(ang[:], posf[:].unsqueeze(2).to_broadcast([P, NT, 8]), f, ALU.mult))
                g.vlink(nc.vector.tensor_scalar(turns[:], ang[:], float(1 / (2 * np.pi)), 12582912.0,
                                                ALU.mult, ALU.add))
                g.vlink(nc.vector.tensor_scalar(turns[:], turns[:], -12582912.0, None, ALU.add))
                for c in (c1, c2, c3):
                    g.vlink(nc.vector.scalar_tensor_tensor(ang[:], turns[:], -float(c), ang[:], ALU.mult, ALU.add))
                g.vlink(nc.vector.tensor_scalar(ang[:], ang[:], 3.1415925, -3.1415925, ALU.min, ALU.max))
                g.vlink(nc.vector.scalar_tensor_tensor(rest[:], ang[:], -1.0, ang[:], ALU.mult, ALU.max))
                nc.vector.tensor_scalar(rest[:], rest[:], -1.0, float(np.pi / 2), ALU.mult, ALU.add).then_inc(
                    reduced.up(), 1)
                for i in range(2):
                    ins = nc.vector.tensor_tensor_reduce(junk[:], lamv[:, 2 * i, :], lamv[:, 2 * i + 1, :], 1.0, 0.0,
                                                         ALU.mult, ALU.add, lams[:, i:i + 1])
                    g.vlink(ins)
                nc.vector.tensor_copy(junk[:, 0:2], lams[:, 0:2]).then_inc(reduced.up(), 1)
                dve.wait_ge(*turned.at(1))
                nc.vector.tensor_copy(g.cols[:], g.psum[:, 0, 0:COL_ROWS])
                dve.wait_ge(*expo.at(1))
                nc.vector.scalar_tensor_tensor(g.neg_lam[:], lams[:, 3:4], -0.2, lams[:, 2:3], ALU.add, ALU.subtract)

            @block.scalar
            def _(act):
                act.wait_ge(*reduced.at(2))
                nc.scalar.activation(g.sin[:], ang[:], ACT.Sin)
                nc.scalar.activation(g.cos[:], rest[:], ACT.Sin).then_inc(sines.up(), 1)
                nc.scalar.activation(lams[:, 2:4], junk[:, 0:2], ACT.Exp).then_inc(expo.up(), 1)


def rope(g, name, items):
    nc = g.nc
    with ExitStack() as ctx:
        tmp = [g.sb(f"{name}_tmp{i}", [P, NT * 8 * 8], ctx=ctx) for i in range(4)]
        with nc.Block() as block:

            @block.sync
            def _(sp):
                g.prefetch(sp, g.taken)

            @block.vector
            def _(dve):
                for x in items:
                    h = x.shape[2]
                    for t in range(NT):
                        x1, x2 = x[:, t, :, 0:8], x[:, t, :, 8:16]
                        c = g.cos[:, t, :].unsqueeze(1).to_broadcast([P, h, 8])
                        s = g.sin[:, t, :].unsqueeze(1).to_broadcast([P, h, 8])
                        o = 64 * t
                        v = [a[:, o:o + h * 8].rearrange("p (h d) -> p h d", d=8) for a in tmp]
                        nc.vector.tensor_tensor(v[0], x1, c, ALU.mult)
                        nc.vector.tensor_tensor(v[1], x2, s, ALU.mult)
                        nc.vector.tensor_tensor(v[2], x2, c, ALU.mult)
                        g.vlink(nc.vector.tensor_tensor(v[3], x1, s, ALU.mult))
                        nc.vector.tensor_tensor(x1, v[0], v[1], ALU.subtract)
                        g.vlink(nc.vector.tensor_tensor(x2, v[2], v[3], ALU.add))


def heads(x, w):
    return x.rearrange("p t (h d) -> p (t h) d", d=w)


def add_to_x(g):
    def evac(eng, b, m, ps, n):
        xs = g.x[:, m, b * BANK:b * BANK + n]
        return eng.tensor_tensor(xs, ps, xs, ALU.add)
    return evac


def col(g, name, l, k=KD):
    return g.cols[:, COLS[name] + l * k:COLS[name] + (l + 1) * k]


def memory_keys(g, l, kT, v):
    nc, t = g.nc, g.t
    with ExitStack() as ctx:
        mem = g.sb(f"mem{l}", [P, 2, D], ctx=ctx)
        krow = g.sb(f"mem_keys{l}", [P, 2, BANK], ctx=ctx)
        s = g.sem(f"mem_loaded{l}")
        with nc.Block() as block:

            @block.sync
            def _(sp):
                sp.dma_start(mem[:], t["mem"][0].rearrange("(t p) d -> p t d", p=P)).then_inc(s, 16)
                g.prefetch(sp, g.taken)
                sp.wait_ge(s, 16)

        norm_transpose(g, f"mem_norm{l}", mem[:], 2, g.hT, gain_col=col(g, "g_mem", l))
        project(g, f"mem_kv{l}", 2, g.hT, lambda eng, b, m, ps, n: copy(eng, nc, (krow, v)[b][:, m, :], ps),
                ntok=MEM, engines="va")
        head_norm(g, f"mem_knorm{l}", [(heads(krow[:], P), g.gain["gk_x"][:, l * P:l * P + P])])
        transpose_rows(g, f"mem_kT{l}", [(kT[:, h, :], [krow[:, i, h * P:h * P + P] for i in range(2)])
                                         for h in range(4)])


def cross_attention(g, l, kT, v):
    nc = g.nc
    norm_transpose(g, f"x_norm{l}", g.x[:], NT, g.hT, gain_col=col(g, "g_xattn", l))
    with ExitStack() as ctx:
        q = g.sb(f"x_q{l}", [P, NT, BANK], ctx=ctx)
        y = g.sb(f"x_y{l}", [P, NT, BANK], ctx=ctx)
        project(g, f"x_qproj{l}", 1, g.hT, lambda eng, b, m, ps, n: copy(eng, nc, q[:, m, :], ps), engines="va")
        head_norm(g, f"x_qnorm{l}", [(heads(q[:], P), g.gain["gq_x"][:, l * P:l * P + P])])
        transpose_rows(g, f"x_qT{l}", [(g.hT[:, h, :], [q[:, i, h * P:h * P + P] for i in range(NT)])
                                       for h in range(4)])
        units = [dict(q=[g.hT[:, h, i * P:i * P + P]], k=[kT[:, h, :]], nk=MEM, bias=g.zeros[:],
                      v=[v[:, j, h * P:h * P + P] for j in range(2)], out=y[:, i, h * P:h * P + P])
                 for h in range(4) for i in range(NT)]
        attend(g, f"x_att{l}", units, 1, P,
               lambda un, ps, r: nc.vector.tensor_scalar(un["out"], ps, r, None, ALU.mult), float(P) ** -0.5)
        transpose_rows(g, f"x_yT{l}", [(g.hT[:, h, :], [y[:, i, h * P:h * P + P] for i in range(NT)])
                                       for h in range(4)])
        project(g, f"x_out{l}", 2, g.hT, add_to_x(g))


def mlp(g, l, beside=None):
    nc = g.nc
    norm_transpose(g, f"m_norm{l}", g.x[:], NT, g.hT, gain_col=col(g, "g_mlp", l))
    with ExitStack() as ctx:
        u = g.sb(f"m_u{l}", [P, FF // P, SEQ], ctx=ctx)

        def squared_relu(eng, b, m, ps, n):
            o = u[:, b * 4 + m, :]
            if eng is nc.scalar:
                g.alink(nc.scalar.activation(o, ps, ACT.Relu))
                return nc.scalar.activation(o, o, ACT.Square)
            g.vlink(nc.vector.tensor_scalar(o, ps, 0.0, None, ALU.max))
            return nc.vector.tensor_tensor(o, o, o, ALU.mult)

        if beside:
            with ExitStack() as c2:
                project(g, f"m_up{l}", FF // BANK, g.hT, squared_relu, cols=True, engines="a", beside=beside(c2))
        else:
            project(g, f"m_up{l}", FF // BANK, g.hT, squared_relu, cols=True, engines="va")
        project(g, f"m_down{l}", 8, u, add_to_x(g), kgroups=4)


def index_select(g, qiT, kiT, wi, bias, scratch, small, topk=P):
    nc = g.nc
    scored, relued, read = g.counter("scores"), g.counter("scores_relu"), g.counter("relu_read")
    tiles = range(1, NT)
    units = [(i, h) for h in range(4) for i in tiles]
    starts = {1: 0, 2: 2 * P, 3: 5 * P}
    isc = {i: scratch[0][:, i - 1, 0:(i + 1) * P] for i in tiles}
    rel = scratch[1]
    work = {1: rel[:, 0, 0:2 * P], 2: rel[:, 1, 0:3 * P], 3: scratch[0][:, 3, :]}
    top = {i: small[:, 8 * i - 8:8 * i] for i in tiles}
    cnt = {i: small[:, 23 + i:24 + i] for i in tiles}

    def tensor(pe):
        for u, (i, h) in enumerate(units):
            p0, nk = 64 * (h % 2), (i + 1) * P
            if u >= 8:
                pe.wait_ge(*relued.at(u - 7))
            nc.tensor.matmul(g.psum[:, u % 8, 0:nk], qiT[p0:p0 + 64, h // 2, i * P:i * P + P],
                             kiT[p0:p0 + 64, 0:nk], start=True, stop=True).then_inc(scored.up(), 1)
        pe.wait_ge(*relued.at(len(units)))

    def scalar(act):
        for u, (i, h) in enumerate(units):
            nk = (i + 1) * P
            act.wait_ge(*scored.at(u + 1))
            if u >= 2:
                act.wait_ge(*read.at(u - 1))
            nc.scalar.activation(rel[:, u % 2, 0:nk], g.psum[:, u % 8, 0:nk], ACT.Relu).then_inc(relued.up(), 1)

    def vector(dve):
        for u, (i, h) in enumerate(units):
            dve.wait_ge(*relued.at(u + 1))
            s, r = isc[i], rel[:, u % 2, 0:(i + 1) * P]
            w = wi[:, i, h:h + 1]
            if h == 0:
                ins = nc.vector.tensor_scalar(s, r, w, None, ALU.mult)
            else:
                dve.wait_ge(*read.at(u - 2))
                ins = nc.vector.scalar_tensor_tensor(s, r, w, s, ALU.mult, ALU.add)
            ins.then_inc(read.up(), 1)
        dve.wait_ge(*read.at(len(units)))

        marks = {i: 0 for i in tiles}

        def step(make):
            for i in tiles:
                if marks[i]:
                    dve.wait_ge(g.dve_sem, marks[i])
                marks[i] = g.vmark(make(i))

        tt, ts, stt = nc.vector.tensor_tensor, nc.vector.tensor_scalar, nc.vector.scalar_tensor_tensor
        step(lambda i: tt(isc[i], isc[i], g.causal[:, (NT - 1 - i) * P:SEQ], ALU.add))
        for r8 in range(topk // 8):
            src = work if r8 else isc
            step(lambda i: nc.vector.max(top[i], src[i]))
            if r8 < topk // 8 - 1:
                step(lambda i: nc.vector.match_replace(work[i], top[i], src[i], -3e38))
        run = {i: bias[:, starts[i]:starts[i] + (i + 1) * P] for i in tiles}
        step(lambda i: ts(work[i], isc[i], top[i][:, 7:8], None, ALU.is_gt, ALU.add, cnt[i]))
        step(lambda i: ts(isc[i], isc[i], top[i][:, 7:8], None, ALU.is_equal))
        step(lambda i: ts(cnt[i], cnt[i], -1.0, float(topk), ALU.mult, ALU.add))
        step(lambda i: nc.vector.tensor_tensor_scan(run[i], isc[i], isc[i], 0.0, ALU.add, ALU.bypass))
        step(lambda i: stt(isc[i], run[i], cnt[i], isc[i], ALU.is_le, ALU.mult))
        step(lambda i: tt(work[i], work[i], isc[i], ALU.add))
        step(lambda i: ts(work[i], work[i], -NEG, NEG, ALU.mult, ALU.add))
        step(lambda i: tt(run[i], work[i], g.causal[:, (NT - 1 - i) * P:SEQ], ALU.min))

    return tensor, scalar, vector


def even_mixer(g):
    nc = g.nc
    norm_transpose(g, "e_norm", g.x[:], NT, g.hT, gain_col=col(g, "g_mix", 0))
    with ExitStack() as ctx:
        va, vb, qb, kb = (g.sb("e_" + n, [P, NT, BANK], ctx=ctx) for n in ("va", "vb", "qb", "kb"))
        bias = g.sb("e_bias", [P, 1152], ctx=ctx)
        QTb, KTb = g.sb("e_QTb", [P, 4, SEQ], ctx=ctx), g.sb("e_KTb", [P, 4, SEQ], ctx=ctx)
        QTa, KTa = g.hT[:, 0:4, :], g.hT[:, 4:8, :]
        with ExitStack() as c2:
            qa, ka, cq = (g.sb("e_" + n, [P, NT, BANK], ctx=c2) for n in ("qa", "ka", "cq"))
            kw = g.sb("e_kw", [P, NT, 68], ctx=c2)
            wi, small = g.sb("e_wi", [P, NT, 4], ctx=c2), g.sb("e_index_small", [P, 27], ctx=c2)
            qiT, kiT = g.sb("e_qiT", [P, 2, SEQ], ctx=c2), g.sb("e_kiT", [P, SEQ], ctx=c2)
            ckT, ki2 = KTb[:, 2:4, :], KTb[:, 0, :].rearrange("p (t c) -> p t c", t=NT)

            def split(x):
                return x.rearrange("p t (h d) -> p t h d", d=64)

            project(g, "e_in_index", 2, g.hT, lambda eng, b, m, ps, n: copy(eng, nc, (kw, cq)[b][:, m, :], ps),
                    engines="va")
            head_norm(g, "e_inorm", [(cq[:, :, 0:256], g.gain["g_kv_b"]), (kw[:, :, 0:64], g.gain["g_kidx"])])
            rope(g, "e_irope", [split(cq[:, :, 256:512]), kw[:, :, 0:64].unsqueeze(2)])
            with nc.Block() as block:

                @block.vector
                def _(dve):
                    nc.vector.tensor_copy(ki2[:, :, 0:64], kw[:, :, 0:64])
                    nc.vector.tensor_copy(ki2[:, :, 64:128], kw[:, :, 0:64])
                    nc.vector.tensor_scalar(wi[:], kw[:, :, 64:68], 4 ** -0.5 * 64 ** -0.5, None, ALU.mult)

            transpose_rows(g, "e_iT", [(dst[:, k, :], [cq[:, i, a + k * P:a + k * P + P] for i in range(NT)])
                                       for dst, a in ((ckT, 0), (qiT, 256)) for k in range(2)] +
                           [(kiT[:], [ki2[:, i, :] for i in range(NT)])])
            dest = [qa, ka, va, qb, kb, vb]
            project(g, "e_in", 6, [g.hT] * 4 + [ckT] * 2, lambda eng, b, m, ps, n: copy(eng, nc, dest[b][:, m, :], ps),
                    engines="a", beside=index_select(g, qiT, kiT, wi, bias, (QTb, KTb), small))
            head_norm(g, "e_hnorm", [(heads(qa[:], 64), g.gain["gq_a"]), (heads(ka[:], 64), g.gain["gk_a"]),
                                     (heads(qb[:], 64), g.gain["gq_b"]), (heads(kb[:], 64), g.gain["gk_b"])])
            rope(g, "e_rope", [split(qa[:]), split(ka[:]), split(qb[:]), split(kb[:])])
            transpose_rows(g, "e_T", [(dst[:, k, :], [src[:, i, k * P:k * P + P] for i in range(NT)])
                                      for dst, src in ((QTa, qa), (KTa, ka), (QTb, qb), (KTb, kb)) for k in range(4)])
        with ExitStack() as c2:
            ya, yb = (g.sb("e_" + n, [P, NT, BANK], ctx=c2) for n in ("ya", "yb"))

            def causal(i):
                return g.causal[:, (NT - 1 - i) * P:SEQ]

            units = [dict(q=[QTa[64 * c:64 * c + 64, h, i * P:i * P + P] for c in range(2)],
                          k=[KTa[64 * c:64 * c + 64, h, 0:(i + 1) * P] for c in range(2)], nk=(i + 1) * P,
                          bias=causal(i), v=[va[:, j, h * P:h * P + P] for j in range(i + 1)],
                          out=ya[:, i, h * P:h * P + P]) for h in range(4) for i in range(NT)]
            attend(g, "e_attA", units, 2, P, lambda un, ps, r: nc.vector.tensor_copy(un["out"], ps), 64 ** -0.5, warm=5)
            offs = [0, 0, 256, 640]
            units = [dict(q=[QTb[64 * (h % 2):64 * (h % 2) + 64, h // 2, i * P:i * P + P]],
                          k=[KTb[64 * (h % 2):64 * (h % 2) + 64, h // 2, 0:(i + 1) * P]], nk=(i + 1) * P,
                          bias=causal(0) if i == 0 else bias[:, offs[i]:offs[i] + (i + 1) * P],
                          v=[vb[:, j, h * 64:h * 64 + 64] for j in range(i + 1)],
                          out=yb[:, i, h * 64:h * 64 + 64]) for h in range(8) for i in range(NT)]
            attend(g, "e_attB", units, 1, 64,
                   lambda un, ps, r: nc.vector.tensor_scalar(un["out"], ps, r, None, ALU.mult), 64 ** -0.5, warm=5)
            gs = g.sb("e_gsub", [P, P], ctx=c2)
            with nc.Block() as block:

                @block.vector
                def _(dve):
                    nc.vector.tensor_scalar(gs[:], g.gain["g_sub_a"], 0.8, None, ALU.mult)

            head_norm(g, "e_onorm", [(heads(ya[:], P), gs[:])])
            transpose_rows(g, "e_yT", [(g.hT[:, 4 * s + k, :], [(ya, yb)[s][:, i, k * P:k * P + P]
                                                               for i in range(NT)]) for s in range(2)
                                       for k in range(4)])
            project(g, "e_out", 2, g.hT, add_to_x(g))


def odd_mixer(g):
    nc, t = g.nc, g.t
    norm_transpose(g, "o_norm", g.x[:], NT, g.hT, gain_col=col(g, "g_mix", 1))
    with ExitStack() as ctx:
        gb, u, z, cv, sm = (g.sb("o_" + n, [P, NT, SEQ], ctx=ctx) for n in ("gb", "u", "z", "conv", "sums"))
        wp = g.sb("o_wpool", [P, 4, P], ctx=ctx)
        rc = g.sb("o_rcount", [P, 16], ctx=ctx)

        def evac(eng, b, m, ps, n):
            if b == 2:
                if m == 0:
                    g.vlink(nc.vector.tensor_copy(rc[:, 0:1], g.zeros[:, 0:1]))
                return eng.tensor_tensor(u[:, m, :], ps, u[:, m, :], ALU.mult)
            return eng.tensor_copy({0: gb, 1: u, 3: z}[b][:, m, :], ps)

        project(g, "o_in", 4, g.hT, evac, cols=True)
        wl = g.sem("w_pool_loaded")
        cnt, pooled, mixed = (g.counter(n) for n in ("counts", "pooled", "pool_mixed"))
        yT = g.hT
        with nc.Block() as block:

            @block.sync
            def _(sp):
                sp.dma_start(wp[:], t["w_pool"][0].rearrange("g c d -> c g d")).then_inc(wl, 16)
                g.prefetch(sp, g.taken)

            @block.gpsimd
            def _(pool):
                for i in range(16):
                    nc.gpsimd.memset(rc[:, i:i + 1], 1.0 / (i + 1)).then_inc(cnt.up(), 1)

            @block.vector
            def _(dve):
                dve.wait_ge(*cnt.at(16))
                for m in range(4):
                    w = 2 ** (m + 1)
                    src, s = z[:, m, :], 1
                    bufs = [sm[:, m, :], cv[:, m, :]]
                    k = 0
                    while s < w:
                        dst = bufs[k % 2]
                        nc.vector.tensor_copy(dst[:, 0:s], src[:, 0:s])
                        g.vlink(nc.vector.tensor_tensor(dst[:, s:SEQ], src[:, s:SEQ], src[:, 0:SEQ - s], ALU.add))
                        src, s, k = dst, 2 * s, k + 1
                    o = bufs[k % 2]
                    g.vlink(nc.vector.tensor_tensor(o[:, 0:w], src[:, 0:w], rc[:, 0:w], ALU.mult))
                    g.vlink(nc.vector.tensor_tensor(o[:, 0:w], o[:, 0:w], z[:, m, 0:w], ALU.subtract))
                    g.vlink(nc.vector.scalar_tensor_tensor(o[:, w:SEQ], src[:, w:SEQ], 1.0 / w, z[:, m, w:SEQ],
                                                           ALU.mult, ALU.subtract))
                    nc.vector.tensor_copy(z[:, m, :], o).then_inc(pooled.up(), 1)
                dve.wait_ge(*pooled.at(4))
                for m in range(4):
                    c, um = cv[:, m, :], u[:, m, :]
                    w = [g.cols[:, COLS["conv_w"] + 4 * j + m:COLS["conv_w"] + 4 * j + m + 1] for j in range(3)]
                    g.vlink(nc.vector.tensor_scalar(c, um, w[2], None, ALU.mult))
                    for j in (1, 0):
                        d = 2 - j
                        g.vlink(nc.vector.scalar_tensor_tensor(c[:, d:SEQ], um[:, 0:SEQ - d], w[j], c[:, d:SEQ],
                                                               ALU.mult, ALU.add))
                    nc.vector.tensor_tensor(yT[:, m, :], gb[:, m, :], c, ALU.mult)
                for m in range(4):
                    dve.wait_ge(*mixed.at(m + 1))
                    ps = g.cols[:, COLS["pool_scale"] + m:COLS["pool_scale"] + m + 1]
                    nc.vector.tensor_scalar(yT[:, 4 + m, :], g.psum[:, m, :], ps, None, ALU.mult)

            @block.tensor
            def _(pe):
                pe.wait_ge(wl, 16)
                for m in range(4):
                    pe.wait_ge(*pooled.at(m + 1))
                    nc.tensor.matmul(g.psum[:, m, :], wp[:, m, :], z[:, m, :], start=True, stop=True).then_inc(
                        mixed.up(), 1)

        project(g, "o_out", 2, g.hT, add_to_x(g))


def first_block(g):
    for l in range(2):
        with ExitStack() as ctx:
            kT, v = g.sb(f"x_kT{l}", [P, 4, MEM], ctx=ctx), g.sb(f"x_v{l}", [P, 2, BANK], ctx=ctx)
            memory_keys(g, l, kT, v)
            if l == 0:
                even_mixer(g)
            else:
                odd_mixer(g)
            cross_attention(g, l, kT, v)
        if l == 0:
            mlp(g, l)
        else:
            mod = g.sb("mod", [P, 6 * D])
            mlp(g, l, lambda ctx: modulation_parts(g, ctx, mod))
    return mod


def shape_constants():
    dist = np.arange(1024) - 511
    n = np.abs(dist)
    half, exact = 16, 8
    ratio = np.log(np.maximum(n, 1).astype(np.float32) / exact) / np.float32(np.log(1024 / exact))
    large = np.minimum(exact + (ratio * (half - exact)).astype(np.int32), half - 1)
    bucket = np.where(dist > 0, half, 0) + np.where(n < exact, n, large)
    hot = (bucket[None, :] == np.arange(32)[:, None]).astype(np.float32)
    count = sum(((n % d == 0) & (n <= 64 * d)).astype(np.float64) for d in (1, 4, 16))
    logs = np.where(count > 0, 8 * np.log(np.maximum(count, 1)), NEG).astype(np.float32)
    return {"bucket_hot": hot, "window_logs": logs}


def modulation_parts(g, ctx, mod):
    nc, t = g.nc, g.t
    quarter = 6 * D // 4
    c_loaded, bias_loaded, zeroed = g.sem("c_loaded"), g.sem("ada_bias_loaded"), g.counter("mod_zeroed")
    silued, added = g.counter("c_silu"), g.counter("mod_added")
    w_loaded = [g.sem(f"ada_loaded_{i}") for i in range(2)]
    c, cs = g.sb("c_col", [P, KD], ctx=ctx), g.sb("c_silu", [P, KD], ctx=ctx)
    w = g.sb("ada_rows", [P, 2, quarter], ctx=ctx)
    rows = t["w_ada_2"][0].rearrange("(k p) n -> p k n", p=P)
    chunks = [(k, h) for h in range(4) for k in range(KD)]

    def tensor(pe):
        pass

    def scalar(act):
        act.wait_ge(c_loaded, 16)
        nc.scalar.activation(cs[:], c[:], ACT.Silu).then_inc(silued.up(), 1)

    def vector(dve):
        dve.wait_ge(*silued.at(1))
        dve.wait_ge(bias_loaded, 16)
        for n, (k, h) in enumerate(chunks):
            dve.wait_ge(w_loaded[n % 2], 16 * (n // 2 + 1))
            if n:
                dve.wait_ge(*added.at(n))
            o = mod[:, h * quarter:(h + 1) * quarter]
            nc.vector.scalar_tensor_tensor(o, w[:, n % 2, :], cs[:, k:k + 1], o, ALU.mult, ALU.add).then_inc(
                added.up(), 1)

    def gpsimd(pool):
        with nc.allow_non_contiguous_dma(reason="1024 values, one per partition and chunk"):
            pool.dma_start(c[:], t["c_2"][0].rearrange("(k p) -> p k", p=P)).then_inc(c_loaded, 16)
        nc.gpsimd.memset(mod[:], 0.0).then_inc(zeroed.up(), 1)
        pool.wait_ge(*zeroed.at(1))
        pool.dma_start(mod[0:1, :], t["b_ada_2"]).then_inc(bias_loaded, 16)
        for n, (k, h) in enumerate(chunks):
            if n >= 2:
                pool.wait_ge(*added.at(n - 1))
            pool.dma_start(w[:, n % 2, :], rows[:, k, h * quarter:(h + 1) * quarter]).then_inc(w_loaded[n % 2], 16)

    return tensor, scalar, vector, gpsimd


def modulation(g, mod):
    nc, t = g.nc, g.t
    loaded, filled, moved = g.sem("norm_gains_loaded"), g.counter("ones_filled"), g.counter("mod_moved")
    summed = g.counter("mod_summed")
    with ExitStack() as ctx:
        gains = g.sb("norm_rows", [P, 2, D], ctx=ctx)
        ones = g.sb("ones", [P, P], ctx=ctx)
        with nc.Block() as block:

            @block.sync
            def _(sp):
                sp.dma_start(gains[:, 0, :], spread(t["norm1_g_2"], D)).then_inc(loaded, 16)
                sp.dma_start(gains[:, 1, :], spread(t["norm2_g_2"], D)).then_inc(loaded, 16)
                g.prefetch(sp, g.taken)

            @block.gpsimd
            def _(pool):
                nc.gpsimd.memset(ones[:], 1.0).then_inc(filled.up(), 1)

            @block.tensor
            def _(pe):
                pe.wait_ge(*filled.at(1))
                for b in range(12):
                    if b >= 8:
                        pe.wait_ge(*moved.at(b - 7))
                    nc.tensor.matmul(g.psum[:, b % 8, :], ones[:], mod[:, b * BANK:b * BANK + BANK], start=True,
                                     stop=True).then_inc(summed.up(), 1)

            @block.vector
            def _(dve):
                dve.wait_ge(loaded, 32)
                for b in range(12):
                    dve.wait_ge(*summed.at(b + 1))
                    o, part = mod[:, b * BANK:b * BANK + BANK], b // 2
                    if part % 3 == 1:
                        gain = gains[:, part // 3, (b % 2) * BANK:(b % 2) * BANK + BANK]
                        ins = nc.vector.scalar_tensor_tensor(o, g.psum[:, b % 8, :], 1.0, gain, ALU.add, ALU.mult)
                    else:
                        ins = nc.vector.tensor_copy(o, g.psum[:, b % 8, :])
                    ins.then_inc(moved.up(), 1)


def gate_rows(g, xT, aT, enT, mrow):
    nc, t = g.nc, g.t
    loaded = g.sem("gates_loaded")
    packed, gated, logf, exped, lned, scanned, turned = (g.counter("gate_" + n) for n in (
        "packed", "gated", "logf", "exped", "lned", "scanned", "turned"))
    first = t["w_in_2"][0][:, 1024:1040].rearrange("(k p) n -> p k n", p=P)
    with ExitStack() as ctx:
        w, wp = g.sb("gate_w", [P, KD, 16], ctx=ctx), g.sb("gate_wp", [P, KD, P], ctx=ctx)
        bias = g.sb("gate_bias", [P, 1], ctx=ctx)
        pre = g.sb("gate_pre", [P, SEQ], ctx=ctx)
        f, e, cum, a, nm = (g.sb("gate_" + n, [64, SEQ], ctx=ctx) for n in ("f", "e", "cum", "a", "nm"))
        zeroed = g.counter("gate_zeroed")
        with nc.Block() as block:

            @block.sync
            def _(sp):
                sp.wait_ge(*zeroed.at(1))
                sp.dma_start(w[:], first).then_inc(loaded, 16)
                with nc.allow_non_contiguous_dma(reason="four biases of four bytes each"):
                    for i, (name, d) in enumerate((("b_igate_2", 0), ("b_igate_2", 1), ("b_fgate_2", 0),
                                                   ("b_fgate_2", 1))):
                        sp.dma_start(bias[32 * i:32 * i + 4, :],
                                     t[name][0, d].rearrange("(h o) -> h o", o=1)).then_inc(loaded, 16)
                g.prefetch(sp, g.taken)

            @block.vector
            def _(dve):
                g.vlink(nc.vector.memset(wp[:], 0.0))
                nc.vector.memset(bias[:], 0.0).then_inc(zeroed.up(), 1)
                dve.wait_ge(loaded, 80)
                for i, c in enumerate((0, 8, 4, 12)):
                    ins = nc.vector.tensor_copy(wp[:, :, 32 * i:32 * i + 4], w[:, :, c:c + 4])
                ins.then_inc(packed.up(), 1)
                dve.wait_ge(*gated.at(1))
                g.vlink(nc.vector.tensor_scalar(pre[:], g.psum[:, 0, :], bias[:, 0:1], None, ALU.add))
                g.vlink(nc.vector.tensor_copy(f[:], pre[64:128, :]))
                nc.vector.scalar_tensor_tensor(e[:], f[:], -1.0, f[:], ALU.mult, ALU.max).then_inc(logf.up(), 1)
                dve.wait_ge(*lned.at(1))
                g.vlink(nc.vector.scalar_tensor_tensor(f[:], f[:], 0.0, e[:], ALU.min, ALU.subtract))
                g.vlink(nc.vector.tensor_tensor_scan(cum[0:32, :], f[0:32, :], f[0:32, :], 0.0, ALU.add, ALU.bypass))
                g.vlink(nc.vector.tensor_tensor_scan(cum[32:64, ::-1], f[32:64, ::-1], f[32:64, ::-1], 0.0, ALU.add,
                                                     ALU.bypass))
                g.vlink(nc.vector.tensor_tensor(a[:], pre[0:64, :], cum[:], ALU.subtract))
                g.vlink(nc.vector.tensor_tensor_scan(mrow[0:32, :], a[0:32, :], a[0:32, :], 0.0, ALU.max, ALU.bypass))
                g.vlink(nc.vector.tensor_tensor_scan(mrow[32:64, ::-1], a[32:64, ::-1], a[32:64, ::-1], 0.0, ALU.max,
                                                     ALU.bypass))
                nc.vector.scalar_tensor_tensor(nm[:], cum[:], -1.0, mrow[:], ALU.mult, ALU.subtract).then_inc(
                    scanned.up(), 1)
                dve.wait_ge(*turned.at(1))
                nc.vector.tensor_copy(aT[:], g.psum[:, 1, 0:4 * 64].rearrange("p (t h) -> p t h", t=4))

            @block.scalar
            def _(act):
                act.wait_ge(*logf.at(1))
                g.alink(nc.scalar.activation(e[:], e[:], ACT.Exp, scale=-1.0))
                nc.scalar.activation(e[:], e[:], ACT.Ln, bias=1.0).then_inc(lned.up(), 1)
                act.wait_ge(*turned.at(2))
                nc.scalar.activation(enT[:], g.psum[:, 2, 0:4 * 64].rearrange("p (t h) -> p t h", t=4), ACT.Exp)

            @block.tensor
            def _(pe):
                pe.wait_ge(*packed.at(1))
                for k in range(KD):
                    mm = nc.tensor.matmul(g.psum[:, 0, :], wp[:, k, :], xT[:, k, :], start=(k == 0), stop=(k == KD - 1))
                mm.then_inc(gated.up(), 1)
                pe.wait_ge(*scanned.at(1))
                for bank, src in ((1, a), (2, nm)):
                    for i in range(4):
                        mm = nc.tensor.transpose(g.psum[:, bank, i * 64:i * 64 + 64], src[:, i * P:i * P + P],
                                                 g.ident[0:64, 0:64])
                    mm.then_inc(turned.up(), 1)


def mlstm_inputs(g, xmT, xcT, qT, kT, v):
    nc, t = g.nc, g.t
    loaded = g.sem("blocks_loaded")
    built, summed, silued, made, moved = (g.counter("mx_" + n) for n in ("built", "summed", "silued", "made", "moved"))
    with ExitStack() as ctx:
        wl = g.sb("block_w", [P, 3, 4, 4], ctx=ctx)
        bd = g.sb("block_diag", [P, 3, 4, P], ctx=ctx)
        with nc.Block() as block:

            @block.sync
            def _(sp):
                for i, n in enumerate(("w_q_blk_2", "w_k_blk_2", "w_v_blk_2")):
                    sp.dma_start(wl[:, i], t[n][0].rearrange("(h g) i j -> (g i) h j", h=4)).then_inc(loaded, 16)
                g.prefetch(sp, g.taken)

            @block.gpsimd
            def _(pool):
                pool.wait_ge(loaded, 48)
                for i in range(3):
                    for h in range(4):
                        o = bd[:, i, h].rearrange("p (b j) -> p b j", j=4)
                        src = wl[:, i, h].unsqueeze(1).to_broadcast([P, 32, 4])
                        g.plink(nc.gpsimd.affine_select(out=o, in_=src, compare_op=ALU.is_ge, fill=0.0, base=0,
                                                        pattern=[[-4, 32], [0, 4]], channel_multiplier=1))
                        nc.gpsimd.affine_select(out=o, in_=o, compare_op=ALU.is_ge, fill=0.0, base=3,
                                                pattern=[[4, 32], [0, 4]], channel_multiplier=-1).then_inc(
                            built.up(), 1)

            @block.vector
            def _(dve):
                for m in range(4):
                    x, c = xmT[:, m, :], xcT[:, m, :]
                    w = [g.cols[:, COLS["conv_w_2"] + 4 * j + m:COLS["conv_w_2"] + 4 * j + m + 1] for j in range(5)]
                    g.vlink(nc.vector.tensor_scalar(c, x, w[2], None, ALU.mult))
                    for j in (0, 1, 3, 4):
                        d = j - 2
                        co, xi = (c[:, -d:SEQ], x[:, 0:SEQ + d]) if d < 0 else (c[:, 0:SEQ - d], x[:, d:SEQ])
                        ins = nc.vector.scalar_tensor_tensor(co, xi, w[j], co, ALU.mult, ALU.add)
                        if j < 4:
                            g.vlink(ins)
                    ins.then_inc(summed.up(), 1)
                g.vlink(nc.vector.memset(v[:, :, :, P:P + 1], 1.0))
                for u in range(12):
                    dve.wait_ge(*made.at(u + 1))
                    h, ps = u // 3, g.psum[:, u % 8, :]
                    if u % 3 == 0:
                        ins = nc.vector.tensor_copy(qT[:, h, :], ps)
                    elif u % 3 == 1:
                        ins = nc.vector.tensor_scalar(kT[:, h, :], ps, float(P) ** -0.5, None, ALU.mult)
                    else:
                        ins = nc.vector.tensor_copy(v[:, :, h, 0:P], ps.rearrange("p (t e) -> p t e", e=P))
                    ins.then_inc(moved.up(), 1)

            @block.scalar
            def _(act):
                for m in range(4):
                    act.wait_ge(*summed.at(m + 1))
                    b = COLS["conv_b_2"] + m
                    nc.scalar.activation(xcT[:, m, :], xcT[:, m, :], ACT.Silu, bias=g.cols[:, b:b + 1]).then_inc(
                        silued.up(), 1)

            @block.tensor
            def _(pe):
                pe.wait_ge(*built.at(12))
                for u in range(12):
                    h, what = u // 3, u % 3
                    if u >= 8:
                        pe.wait_ge(*moved.at(u - 7))
                    pe.wait_ge(*silued.at(h + 1))
                    if what < 2:
                        mm = nc.tensor.matmul(g.psum[:, u % 8, :], bd[:, what, h, :], xcT[:, h, :], start=True,
                                              stop=True)
                    else:
                        for j in range(4):
                            mm = nc.tensor.matmul(g.psum[:, u % 8, j * P:j * P + P], xmT[:, h, j * P:j * P + P],
                                                  bd[:, 2, h, :], start=True, stop=True)
                    mm.then_inc(made.up(), 1)


def mlstm_scan(g, qT, kT, v, aT, enT, mrow, spare, hr):
    nc = g.nc
    s_s, s_m, s_diff, s_exp, s_w, s_mask, s_num, s_fin = (g.counter("ml_" + n) for n in (
        "scores", "mrow", "diff", "exp", "weighted", "masked", "num", "finished"))
    units = [(h, d) for h in range(4) for d in range(2)]

    def span(d, j):
        return (j * P, SEQ) if d == 0 else (0, (j + 1) * P)

    with ExitStack() as ctx:
        e = g.sb("ml_e", [P, 3, SEQ], ctx=ctx)
        w = [spare, g.sb("ml_w", [P, NT, SEQ], ctx=ctx)]
        den = g.sb("ml_den", [P, 2, NT], ctx=ctx)
        with nc.Block() as block:

            @block.sync
            def _(sp):
                g.prefetch(sp, g.taken)

            @block.tensor
            def _(pe):
                def numerator(n):
                    h, d = units[n]
                    pe.wait_ge(*s_mask.at(4 * n + 4))
                    if n >= 1:
                        pe.wait_ge(*s_fin.at(n))
                    for tt in range(NT):
                        js = range(0, tt + 1) if d == 0 else range(tt, NT)
                        o = g.psum[:, 6 + tt // 2, (tt % 2) * 256:(tt % 2) * 256 + P + 1]
                        for j in js:
                            mm = nc.tensor.matmul(o, w[n % 2][:, j, tt * P:tt * P + P], v[:, j, h, :],
                                                  start=(j == js[0]), stop=(j == js[-1]))
                    mm.then_inc(s_num.up(), 1)

                for n, (h, d) in enumerate(units):
                    if d == 0:
                        if n:
                            pe.wait_ge(*s_w.at(4 * n))
                        for j in range(NT):
                            mm = nc.tensor.matmul(g.psum[:, j, :], kT[:, h, j * P:j * P + P], qT[:, h, :],
                                                  start=True, stop=True)
                        mm.then_inc(s_s.up(), 1)
                    r = 32 * d + h
                    if n >= 2:
                        pe.wait_ge(*s_diff.at(4 * (n - 1)))
                    nc.tensor.matmul(g.psum[:, 4 + n % 2, :], g.ident[0:64, r:r + 1].to_broadcast([64, P]), mrow[:],
                                     start=True, stop=True).then_inc(s_m.up(), 1)
                    if n:
                        numerator(n - 1)
                numerator(len(units) - 1)

            @block.vector
            def _(dve):
                def difference(s):
                    n, j = s // 4, s % 4
                    h, d = units[n]
                    a, z = span(d, j)
                    dve.wait_ge(*s_m.at(n + 1))
                    if s >= 3:
                        dve.wait_ge(*s_w.at(s - 2))
                    r = 32 * d + h
                    nc.vector.tensor_scalar(e[:, s % 3, a:z], g.psum[:, 4 + n % 2, a:z], aT[:, j, r:r + 1], 0.0,
                                            ALU.subtract, ALU.max).then_inc(s_diff.up(), 1)

                def weigh(s):
                    n, j = s // 4, s % 4
                    h, d = units[n]
                    a, z = span(d, j)
                    dve.wait_ge(*s_exp.at(s + 1))
                    dve.wait_ge(*s_s.at(h + 1))
                    if n >= 2:
                        dve.wait_ge(*s_num.at(n - 1))
                    nc.vector.tensor_tensor(w[n % 2][:, j, a:z], e[:, s % 3, a:z], g.psum[:, j, a:z],
                                            ALU.mult).then_inc(s_w.up(), 1)

                def finish(n):
                    h, d = units[n]
                    r = 32 * d + h
                    dve.wait_ge(*s_num.at(n + 1))
                    sums = [g.psum[:, 6 + tt // 2, (tt % 2) * 256 + P:(tt % 2) * 256 + P + 1] for tt in range(NT)]
                    for tt in range(NT):
                        ins = nc.vector.scalar_tensor_tensor(den[:, 0, tt:tt + 1], sums[tt], -1.0,
                                                             enT[:, tt, r:r + 1], ALU.mult, ALU.max)
                    g.vlink(ins)
                    for tt in range(NT):
                        ins = nc.vector.tensor_tensor(den[:, 0, tt:tt + 1], sums[tt], den[:, 0, tt:tt + 1], ALU.max)
                    g.vlink(ins)
                    g.vlink(nc.vector.reciprocal(den[:, 1, :], den[:, 0, :]))
                    for tt in range(NT):
                        c = (tt % 2) * 256
                        o, num = hr[:, tt, h * P:h * P + P], g.psum[:, 6 + tt // 2, c:c + P]
                        if d == 0:
                            ins = nc.vector.tensor_scalar(o, num, den[:, 1, tt:tt + 1], None, ALU.mult)
                        else:
                            ins = nc.vector.scalar_tensor_tensor(o, num, den[:, 1, tt:tt + 1], o, ALU.mult, ALU.add)
                    ins.then_inc(s_fin.up(), 1)
                    dve.wait_ge(*s_fin.at(n + 1))

                for s in range(4 * len(units) + 1):
                    new_head = s % 8 == 0
                    if s >= 1 and new_head:
                        weigh(s - 1)
                    if s < 4 * len(units):
                        difference(s)
                    if s >= 1 and not new_head:
                        weigh(s - 1)
                    if s % 4 == 0 and s >= 8:
                        finish(s // 4 - 2)
                finish(len(units) - 1)

            @block.scalar
            def _(act):
                for s in range(4 * len(units)):
                    a, z = span(units[s // 4][1], s % 4)
                    act.wait_ge(*s_diff.at(s + 1))
                    nc.scalar.activation(e[:, s % 3, a:z], e[:, s % 3, a:z], ACT.Exp, scale=-1.0).then_inc(
                        s_exp.up(), 1)

            @block.gpsimd
            def _(pool):
                for s in range(4 * len(units)):
                    n, j = s // 4, s % 4
                    pool.wait_ge(*s_w.at(s + 1))
                    b = w[n % 2][:, j, j * P:j * P + P]
                    sign = 1 if units[n][1] == 0 else -1
                    nc.gpsimd.affine_select(out=b, in_=b, compare_op=ALU.is_ge, fill=0.0, base=0,
                                            pattern=[[sign, P]], channel_multiplier=-sign).then_inc(s_mask.up(), 1)


def mlstm(g, xmT, o, hr):
    nc, t = g.nc, g.t
    with ExitStack() as ctx:
        xcT = g.sb("xcT", [P, 4, SEQ], ctx=ctx)
        with ExitStack() as c2:
            aT, enT = g.sb("aT", [P, NT, 64], ctx=c2), g.sb("enT", [P, NT, 64], ctx=c2)
            mrow = g.sb("mrow", [64, SEQ], ctx=c2)
            gate_rows(g, g.hT, aT, enT, mrow)
            v = g.sb("ml_v", [P, NT, 4, P + 1], ctx=c2)
            qT, kT = g.hT[:, 0:4, :], g.hT[:, 4:8, :]
            mlstm_inputs(g, xmT, xcT, qT, kT, v)
            mlstm_scan(g, qT, kT, v, aT, enT, mrow, xmT, hr)
        head_norm(g, "ml_norm", [(heads(hr[:], P), None)])
        xc = g.sb("xc_rows", [P, NT, BANK], ctx=ctx)
        transpose_rows(g, "ml_xc", [(xc[:, i, :], [xcT[:, m, i * P:i * P + P] for m in range(4)])
                                    for i in range(NT)])
        rows = g.sb("ml_rows", [P, 2, BANK], ctx=ctx)
        loaded, gated = g.sem("ml_rows_loaded"), g.counter("sigmoid")
        with nc.Block() as block:

            @block.sync
            def _(sp):
                sp.dma_start(rows[:, 0, :], spread(t["mlstm_norm_g_2"], BANK)).then_inc(loaded, 16)
                sp.dma_start(rows[:, 1, :], spread(t["mlstm_skip_2"], BANK)).then_inc(loaded, 16)
                g.prefetch(sp, g.taken)

            @block.scalar
            def _(act):
                nc.scalar.activation(o, o, ACT.Sigmoid).then_inc(gated.up(), 1)

            @block.vector
            def _(dve):
                dve.wait_ge(loaded, 32)
                gain, skip = (rows[:, i, :].unsqueeze(1).to_broadcast([P, NT, BANK]) for i in range(2))
                nc.vector.tensor_tensor(xc[:], xc[:], skip, ALU.mult)
                g.vlink(nc.vector.tensor_tensor(hr[:], hr[:], gain, ALU.mult))
                g.vlink(nc.vector.tensor_tensor(hr[:], hr[:], xc[:], ALU.add))
                dve.wait_ge(*gated.at(1))
                nc.vector.tensor_tensor(hr[:], hr[:], o, ALU.mult)


def distance_tables(g):
    nc, t = g.nc, g.t
    table = nc.dram_tensor("distance_table", (8, 1024), F32, kind="Internal").ap()
    g.distances = nc.dram_tensor("distance_copies", (8, P, 1024), F32, kind="Internal").ap()
    loaded, written = g.sem("distance_loaded"), g.sem("distance_written")
    g.copied = g.sem("distance_copied")
    summed, added = g.counter("distance_summed"), g.counter("distance_added")
    with ExitStack() as ctx:
        hot, rb = g.sb("bucket_hot", [32, 1024], ctx=ctx), g.sb("rel_bias", [32, 8], ctx=ctx)
        logs, row = g.sb("window_logs", [8, 1024], ctx=ctx), g.sb("distance_row", [8, 1024], ctx=ctx)
        with nc.Block() as block:

            @block.sync
            def _(sp):
                sp.dma_start(hot[:], t["bucket_hot"]).then_inc(loaded, 16)
                sp.dma_start(rb[:], t["rel_bias_2"]).then_inc(loaded, 16)
                w = t["window_logs"]
                sp.dma_start(logs[:], bass.AP(w.tensor, w.offset, [[0, 8], [1, 1024]])).then_inc(loaded, 16)
                sp.wait_ge(*added.at(2))
                sp.dma_start(table, row[:]).then_inc(written, 16)
                sp.wait_ge(written, 16)
                src = bass.AP(table.tensor, table.offset, [[1024, 8], [0, P], [1, 1024]])
                sp.dma_start(g.distances, src).then_inc(g.copied, 16)

            @block.tensor
            def _(pe):
                pe.wait_ge(loaded, 48)
                for c in range(2):
                    nc.tensor.matmul(g.psum[0:8, c, :], rb[:], hot[:, c * BANK:c * BANK + BANK], start=True,
                                     stop=True).then_inc(summed.up(), 1)

            @block.vector
            def _(dve):
                for c in range(2):
                    dve.wait_ge(*summed.at(c + 1))
                    a, z = c * BANK, c * BANK + BANK
                    nc.vector.scalar_tensor_tensor(row[:, a:z], g.psum[0:8, c, :], 8.0, logs[:, a:z], ALU.mult,
                                                   ALU.add).then_inc(added.up(), 1)


def load_distances(g, bias):
    nc = g.nc
    with nc.Block() as block:

        @block.sync
        def _(sp):
            sp.wait_ge(g.copied, 16)
            for h in range(8):
                src = bass.AP(g.distances.tensor, g.distances[h].offset + 127, [[1023, P], [1, 896]])
                sp.dma_start(bias[:, h, :], src).then_inc(g.bias_loaded, 16)
            g.prefetch(sp, g.taken)


def route(g, hot, slots_gated):
    nc, t = g.nc, g.t
    E = EXPERTS
    loaded = g.sem("router_loaded")
    s_log, s_pk, s_exp, s_aff, s_turn, s_pos, s_back, s_gh, s_gt, s_mv = (
        g.counter("route_" + n) for n in ("logits", "peak", "exp", "affinity", "turned", "positions", "back", "gated",
                                          "gated_turned", "gated_moved"))
    with ExitStack() as ctx:
        wr, br = g.sb("w_router", [P, KD, E], ctx=ctx), g.sb("b_router", [P, E], ctx=ctx)
        gated = g.sb("slot_gated", [P, NT, E * CAP], ctx=ctx)
        aff = g.sb("affinity", [P, NT, E], ctx=ctx)
        st = g.sb("route_stats", [P, 3, NT], ctx=ctx)
        A, wk, eq, run = (g.sb("route_" + n, [E, SEQ], ctx=ctx) for n in ("a", "work", "equal", "running"))
        top, cnt = g.sb("route_top", [E, 8], ctx=ctx), g.sb("route_count", [E, 1], ctx=ctx)
        pos = g.sb("route_pos", [P, NT, E], ctx=ctx)
        slot = g.sb("slot_numbers", [P, CAP], ctx=ctx)
        numbered = g.counter("route_numbered")
        with nc.Block() as block:

            @block.sync
            def _(sp):
                sp.dma_start(wr[:], t["w_router_2"][0].rearrange("(k p) e -> p k e", p=P)).then_inc(loaded, 16)
                sp.dma_start(br[:], spread(t["b_router_2"], E)).then_inc(loaded, 16)
                g.prefetch(sp, g.taken)

            @block.gpsimd
            def _(pool):
                nc.gpsimd.iota(slot[:], [[1, CAP]], base=0, channel_multiplier=0,
                               allow_small_or_imprecise_dtypes=True).then_inc(numbered.up(), 1)

            @block.tensor
            def _(pe):
                pe.wait_ge(loaded, 32)
                for i in range(NT):
                    for k in range(KD):
                        mm = nc.tensor.matmul(g.psum[:, i, 0:E], g.hT[:, k, i * P:i * P + P], wr[:, k, :],
                                              start=(k == 0), stop=(k == KD - 1))
                mm.then_inc(s_log.up(), 1)
                pe.wait_ge(*s_aff.at(1))
                for i in range(NT):
                    mm = nc.tensor.transpose(g.psum[0:E, 4, i * P:i * P + P], aff[:, i, :], g.ident[:])
                mm.then_inc(s_turn.up(), 1)
                pe.wait_ge(*s_pos.at(1))
                for i in range(NT):
                    mm = nc.tensor.transpose(g.psum[:, 5, i * E:i * E + E], run[:, i * P:i * P + P],
                                             g.ident[0:E, 0:E])
                mm.then_inc(s_back.up(), 1)
                pe.wait_ge(*s_gh.at(1))
                for u in range(8):
                    if u >= 2:
                        pe.wait_ge(*s_mv.at(u - 1))
                    for i in range(NT):
                        mm = nc.tensor.transpose(g.psum[:, 6 + u % 2, i * P:i * P + P], gated[:, i, u * P:u * P + P],
                                                 g.ident[:])
                    mm.then_inc(s_gt.up(), 1)

            @block.scalar
            def _(act):
                act.wait_ge(*s_pk.at(1))
                for i in range(NT):
                    ins = nc.scalar.activation(aff[:, i, :], aff[:, i, :], ACT.Exp, bias=st[:, 1, i:i + 1],
                                               accum_out=st[:, 2, i:i + 1])
                g.alink(ins)
                nc.scalar.activation(br[:, 0:1], br[:, 0:1], ACT.Copy).then_inc(s_exp.up(), 1)

            @block.vector
            def _(dve):
                dve.wait_ge(*s_log.at(1))
                for i in range(NT):
                    ins = nc.vector.tensor_tensor_reduce(aff[:, i, :], g.psum[:, i, 0:E], br[:], 1.0, NEG * 10,
                                                         ALU.add, ALU.max, st[:, 0, i:i + 1])
                g.vlink(ins)
                nc.vector.tensor_scalar(st[:, 1, :], st[:, 0, :], -1.0, None, ALU.mult).then_inc(s_pk.up(), 1)
                dve.wait_ge(*s_exp.at(1))
                g.vlink(nc.vector.reciprocal(st[:, 0, :], st[:, 2, :]))
                r = st[:, 0, :].unsqueeze(2).to_broadcast([P, NT, E])
                nc.vector.tensor_tensor(aff[:], aff[:], r, ALU.mult).then_inc(s_aff.up(), 1)
                dve.wait_ge(*s_turn.at(1))
                g.vlink(nc.vector.tensor_copy(A[:], g.psum[0:E, 4, :]))
                src = A[:]
                for r8 in range(CAP // 8):
                    g.vlink(nc.vector.max(top[:], src))
                    if r8 < CAP // 8 - 1:
                        g.vlink(nc.vector.match_replace(wk[:], top[:], src, -1.0))
                        src = wk[:]
                thr = top[:, 7:8]
                g.vlink(nc.vector.tensor_scalar(wk[:], A[:], thr, None, ALU.is_gt, ALU.add, cnt[:]))
                g.vlink(nc.vector.tensor_scalar(eq[:], A[:], thr, None, ALU.is_equal))
                g.vlink(nc.vector.tensor_scalar(cnt[:], cnt[:], -1.0, float(CAP), ALU.mult, ALU.add))
                g.vlink(nc.vector.tensor_tensor_scan(run[:], eq[:], eq[:], 0.0, ALU.add, ALU.bypass))
                g.vlink(nc.vector.scalar_tensor_tensor(eq[:], run[:], cnt[:], eq[:], ALU.is_le, ALU.mult))
                g.vlink(nc.vector.tensor_tensor(wk[:], wk[:], eq[:], ALU.add))
                g.vlink(nc.vector.tensor_tensor_scan(eq[:], wk[:], wk[:], 0.0, ALU.add, ALU.bypass))
                g.vlink(nc.vector.tensor_tensor(eq[:], eq[:], wk[:], ALU.mult))
                nc.vector.tensor_scalar(run[:], eq[:], -1.0, None, ALU.add).then_inc(s_pos.up(), 1)
                dve.wait_ge(*s_back.at(1))
                g.vlink(nc.vector.tensor_copy(pos[:], g.psum[:, 5, 0:NT * E].rearrange("p (t e) -> p t e", e=E)))
                dve.wait_ge(*numbered.at(1))
                for i in range(NT):
                    o = hot[:, i, :].rearrange("p (e s) -> p e s", s=CAP)
                    ins = nc.vector.tensor_tensor(o, slot[:].unsqueeze(1).to_broadcast([P, E, CAP]),
                                                  pos[:, i, :].unsqueeze(2).to_broadcast([P, E, CAP]), ALU.is_equal)
                g.vlink(ins)
                for i in range(NT):
                    o, h = (a[:, i, :].rearrange("p (e s) -> p e s", s=CAP) for a in (gated, hot))
                    ins = nc.vector.tensor_tensor(o, h, aff[:, i, :].unsqueeze(2).to_broadcast([P, E, CAP]), ALU.mult)
                ins.then_inc(s_gh.up(), 1)
                for u in range(8):
                    dve.wait_ge(*s_gt.at(u + 1))
                    nc.vector.tensor_copy(slots_gated[:, u, :], g.psum[:, 6 + u % 2, :]).then_inc(s_mv.up(), 1)


def experts(g, h2, hot, slots_gated, spare, gate2):
    nc, t = g.nc, g.t
    pairs, nf = EXPERTS // 2, FE // BANK
    per = 4 * nf + 8
    base, g0 = g.tiles, g.taken
    wg, wu, wd = (t[n].rearrange("a e (k p) n -> (a e) p k n", p=P) for n in ("w_gate_2", "w_up_2", "w_down_2"))
    names = ("gathered", "x", "silu", "hidden", "turned", "copied", "y", "back", "added")
    s_tmp = g.counter("ex_scaled")
    first = [g.counter("ex_" + n) for n in names]
    slot_of = [(g0 + j) % RING for j in range(per)]
    landed_at = [16 * ((g0 + j) // RING + 1) for j in range(per)]

    with ExitStack() as ctx:
        xc = g.sb("ex_x", [P, KD, P], ctx=ctx)
        sg = g.sb("ex_slots", [P, SEQ], ctx=ctx)
        y = g.sb("ex_y", [P, D], ctx=ctx)
        tmp = g.sb("ex_tmp", [P, 2, BANK], ctx=ctx)
        hT = spare[:, 0:FE].rearrange("p (f s) -> p f s", s=P)
        hid, act_g = (spare[:, a:a + 2 * BANK].rearrange("p (b n) -> p b n", b=2) for a in (FE, FE + 2 * BANK))

        with nc.Block() as block:

            @block.gpsimd
            def _(pool):
                for q in range(2 * len(first)):
                    nc.gpsimd.memset(hid[:, 0, q:q + 1], 0.0).then_inc(first[q // 2].up(), 1)
                nc.gpsimd.memset(y[:], 0.0)
                nc.gpsimd.memset(sg[:], 0.0)

        s_gat, s_x, s_silu, s_hid, s_turn, s_copy, s_y, s_back, s_add = (g.counter("ex_" + n) for n in names)
        with nc.Block() as block:

            @block.sync
            def _(sp):
                def load(i, j):
                    sp.wait_ge(g.tiles_done, i * per + (base + j + 1 - RING))
                    if j < 4 * nf:
                        b, what, e = j // 4, (j // 2) % 2, j % 2
                        src = (wg, wu)[what][i * 2 + e, :, :, b * BANK:b * BANK + BANK]
                    else:
                        jj = j - 4 * nf
                        b, kg, e = jj // 4, (jj // 2) % 2, jj % 2
                        src = wd[i * 2 + e, :, kg * KD:kg * KD + KD, b * BANK:b * BANK + BANK]
                    dst = g.ring[:, slot_of[j], :].rearrange("p (k n) -> p k n", k=KD)
                    sp.dma_start(dst, src).then_inc(g.landed[slot_of[j]], 16)

                for j in range(RING, per):
                    load(0, j)
                with sp.Fori(1, pairs) as i:
                    for j in range(per):
                        load(i, j)

            @block.tensor
            def _(pe):
                def pair_of_groups(i, j, bank, lhs, start, stop):
                    ws = [g.ring[:, slot_of[j + e], :].rearrange("p (k n) -> p k n", k=KD) for e in range(2)]
                    for e in range(2):
                        pe.wait_ge(g.landed[slot_of[j + e]], i * (16 * per // RING) + landed_at[j + e])
                    for k in range(KD):
                        for e in range(2):
                            mm = nc.tensor.matmul(g.psum[64 * e:64 * e + 64, bank, :], lhs(k)[:, 64 * e:64 * e + 64],
                                                  ws[e][:, k, :], start=(start and k == 0), stop=(stop and k == KD - 1))
                            if k == KD - 1:
                                mm.then_inc(g.tiles_done, 1)

                def turn(i, b):
                    pe.wait_ge(s_hid.sem, i * nf + (s_hid.base + b + 1))
                    if b >= 2:
                        pe.wait_ge(s_copy.sem, i * nf + (s_copy.base + b - 1))
                    for c in range(4):
                        mm = nc.tensor.transpose(g.psum[:, 4 + b % 2, c * P:c * P + P], hid[:, b % 2, c * P:c * P + P],
                                                 g.ident[:])
                    mm.then_inc(s_turn.up(), 1)

                def gather(i):
                    for q in range(2):
                        for k in range(4 * q, 4 * q + 4):
                            for tt in range(NT):
                                mm = nc.tensor.matmul(g.psum[:, 4 + q, (k % 4) * P:(k % 4) * P + P],
                                                      h2[:, tt, k * P:k * P + P], hot[:, tt, bass.ds(i * P, P)],
                                                      start=(tt == 0), stop=(tt == NT - 1))
                        mm.then_inc(s_gat.up(), 1)

                def scatter(i, u):
                    if u >= 2:
                        pe.wait_ge(s_tmp.sem, i * 2 * NT + (s_tmp.base + u - 1))
                    tt, c = u // 2, u % 2
                    nc.tensor.matmul(g.psum[:, 6 + u % 2, :], sg[:, tt * P:tt * P + P], y[:, c * BANK:c * BANK + BANK],
                                     start=True, stop=True).then_inc(s_back.up(), 1)

                def pair(i, last):
                    pe.wait_ge(s_x.sem, i * 2 + (s_x.base + 2))
                    pe.wait_ge(s_y.sem, i * 2 + s_y.base)
                    for b in range(nf):
                        if b >= 2:
                            pe.wait_ge(s_hid.sem, i * nf + (s_hid.base + b - 1))
                        pair_of_groups(i, 4 * b, (b % 2) * 2, lambda k: xc[:, k, :], True, True)
                        scatter(i, 2 * b)
                        pair_of_groups(i, 4 * b + 2, (b % 2) * 2 + 1, lambda k: xc[:, k, :], True, True)
                        scatter(i, 2 * b + 1)
                        if b:
                            turn(i, b - 1)
                    turn(i, nf - 1)
                    pe.wait_ge(s_copy.sem, i * nf + (s_copy.base + nf))
                    pe.wait_ge(s_tmp.sem, i * 2 * NT + (s_tmp.base + 2 * NT))
                    for b in range(2):
                        for kg in range(2):
                            pair_of_groups(i, 4 * nf + 4 * b + 2 * kg, 6 + b, lambda k: hT[:, kg * KD + k, :],
                                           kg == 0, kg == 1)
                        if b == 0 and not last:
                            gather(i + 1)

                gather(0)
                with pe.Fori(0, pairs - 1) as i:
                    pair(i, False)
                pair(pairs - 1, True)
                pe.wait_ge(s_y.sem, pairs * 2 + s_y.base)
                for u in range(2 * NT):
                    scatter(pairs, u)

            @block.scalar
            def _(act):
                def copied(i, b):
                    act.wait_ge(s_turn.sem, i * nf + (s_turn.base + b + 1))
                    nc.scalar.activation(hT[:, 4 * b:4 * b + 4, :],
                                         g.psum[:, 4 + b % 2, :].rearrange("p (c s) -> p c s", c=4),
                                         ACT.Copy).then_inc(s_copy.up(), 1)

                with act.Fori(0, pairs) as i:
                    for b in range(nf):
                        act.wait_ge(g.tiles_done, i * per + (base + 4 * b + 2))
                        act.wait_ge(s_hid.sem, i * nf + (s_hid.base + b - 1))
                        nc.scalar.activation(act_g[:, b % 2, :], g.psum[:, (b % 2) * 2, :], ACT.Silu).then_inc(
                            s_silu.up(), 1)
                        if b:
                            copied(i, b - 1)
                    copied(i, nf - 1)

            @block.vector
            def _(dve):
                def move_gathered(i):
                    for q in range(2):
                        dve.wait_ge(s_gat.sem, i * 2 + (s_gat.base + q + 1))
                        nc.vector.tensor_copy(xc[:, 4 * q:4 * q + 4, :],
                                              g.psum[:, 4 + q, :].rearrange("p (c s) -> p c s", c=4)).then_inc(
                            s_x.up(), 1)

                def add(i, u):
                    tt, c = u // 2, u % 2
                    dve.wait_ge(s_back.sem, i * 2 * NT + (s_back.base + u + 1))
                    dve.wait_ge(s_add.sem, i * 2 * NT + (s_add.base + u - 1))
                    nc.vector.tensor_tensor(tmp[:, u % 2, :], g.psum[:, 6 + u % 2, :],
                                            gate2[:, c * BANK:c * BANK + BANK], ALU.mult).then_inc(s_tmp.up(), 1)
                    dve.wait_ge(s_tmp.sem, i * 2 * NT + (s_tmp.base + u + 1))
                    xs = g.x[:, tt, c * BANK:c * BANK + BANK]
                    nc.vector.tensor_tensor(xs, tmp[:, u % 2, :], xs, ALU.add).then_inc(s_add.up(), 1)

                def pair(i, last):
                    for b in range(nf):
                        add(i, 2 * b)
                        dve.wait_ge(s_silu.sem, i * nf + (s_silu.base + b + 1))
                        dve.wait_ge(g.tiles_done, i * per + (base + 4 * b + 4))
                        dve.wait_ge(s_turn.sem, i * nf + (s_turn.base + b - 1))
                        nc.vector.tensor_tensor(hid[:, b % 2, :], g.psum[:, (b % 2) * 2 + 1, :], act_g[:, b % 2, :],
                                                ALU.mult).then_inc(s_hid.up(), 1)
                        add(i, 2 * b + 1)
                    for b in range(2):
                        dve.wait_ge(g.tiles_done, i * per + (base + 4 * nf + 4 * b + 4))
                        if b == 0:
                            nc.vector.tensor_copy(sg[:].unsqueeze(1), slots_gated[:, bass.ds(i, 1), :])
                        nc.vector.tensor_copy(y[:, b * BANK:b * BANK + BANK], g.psum[:, 6 + b, :]).then_inc(
                            s_y.up(), 1)
                        if b == 0 and not last:
                            move_gathered(i + 1)

                move_gathered(0)
                with dve.Fori(0, pairs - 1) as i:
                    pair(i, False)
                pair(pairs - 1, True)
                for u in range(2 * NT):
                    add(pairs, u)


def prefetch_experts(g):
    wg, wu = (g.t[n].rearrange("a e (k p) n -> (a e) p k n", p=P) for n in ("w_gate_2", "w_up_2"))
    g.groups += [(w[e, :, :, 0:BANK], KD, BANK) for w in (wg, wu) for e in range(2)]


def write_out(g, out):
    nc = g.nc
    done = g.sem("out_written")
    rows = out[0].rearrange("(t p) d -> p t d", p=P)
    with nc.Block() as block:

        @block.sync
        def _(sp):
            sp.dma_start(rows[:, 0:2, :], g.x[:, 0:2, :]).then_inc(done, 16)
            sp.dma_start(rows[:, 2:4, :], g.x[:, 2:4, :]).then_inc(done, 16)
            sp.wait_ge(done, 32)


def second_block(g, out, mod):
    nc = g.nc
    shift1, gain1, gate1, shift2, gain2, gate2 = (mod[:, i * D:i * D + D] for i in range(6))
    modulation(g, mod)
    norm_transpose(g, "s_norm", g.x[:], NT, g.hT, gain_row=gain1, shift_row=shift1)
    with ExitStack() as ctx:
        aq, ak, av, hr = (g.sb("s_" + n, [P, NT, BANK], ctx=ctx) for n in ("aq", "ak", "av", "hr"))
        with ExitStack() as c2:
            xmT = g.sb("s_xmT", [P, NT, SEQ], ctx=c2)
            o = mod[:, 0:2 * D].rearrange("p (t n) -> p t n", t=NT)
            project(g, "s_xm", 1, g.hT, lambda eng, b, m, ps, n: copy(eng, nc, xmT[:, m, :], ps), cols=True,
                    engines="va")
            dest = [o, aq, ak, av]
            project(g, "s_rows", 4, g.hT, lambda eng, b, m, ps, n: copy(eng, nc, dest[b][:, m, :], ps), engines="va")
            mlstm(g, xmT, o, hr)
        bias = g.sb("s_bias", [P, 8, 896], ctx=ctx)
        g.bias_loaded = g.sem("distance_bias_loaded")
        load_distances(g, bias)
        head_norm(g, "s_qk", [(heads(aq[:], 64), g.gain["q_norm_g_2"]), (heads(ak[:], 64), g.gain["k_norm_g_2"])])
        QT, KT = g.hT[:, 0:4, :], g.hT[:, 4:8, :]
        transpose_rows(g, "s_T", [(dst[:, k, :], [src[:, i, k * P:k * P + P] for i in range(NT)])
                                  for dst, src in ((QT, aq), (KT, ak)) for k in range(4)])
        ya = aq
        with nc.Block() as block:

            @block.sync
            def _(sp):
                sp.wait_ge(g.bias_loaded, 16 * 8)

        units = [dict(q=[QT[64 * (h % 2):64 * (h % 2) + 64, h // 2, i * P:i * P + P]],
                      k=[KT[64 * (h % 2):64 * (h % 2) + 64, h // 2, :]], nk=SEQ,
                      bias=bias[:, h, 384 - P * i:896 - P * i], v=[av[:, j, h * 64:h * 64 + 64] for j in range(NT)],
                      out=ya[:, i, h * 64:h * 64 + 64]) for h in range(8) for i in range(NT)]
        attend(g, "s_att", units, 1, 64,
               lambda un, ps, r: nc.vector.tensor_scalar(un["out"], ps, r, None, ALU.mult), 0.125, warm=5)
        transpose_rows(g, "s_yT", [(g.hT[:, 4 * s + k, :], [(hr, ya)[s][:, i, k * P:k * P + P] for i in range(NT)])
                                   for s in range(2) for k in range(4)])
        tmp = g.sb("s_tmp", [P, 2, BANK], ctx=ctx)

        def gated_add(eng, b, m, ps, n):
            g.vlink(eng.tensor_tensor(tmp[:, m % 2, :], ps, gate1[:, b * BANK:b * BANK + BANK], ALU.mult))
            xs = g.x[:, m, b * BANK:b * BANK + BANK]
            return eng.tensor_tensor(xs, tmp[:, m % 2, :], xs, ALU.add)

        project(g, "s_out", 2, g.hT, gated_add)
    with ExitStack() as ctx:
        h2 = g.sb("h2_rows", [P, NT, D], ctx=ctx)
        hot = g.sb("slot_hot", [P, NT, EXPERTS * CAP], ctx=ctx)
        norm_transpose(g, "r_norm", g.x[:], NT, g.hT, gain_row=gain2, shift_row=shift2, keep=h2)
        route(g, hot, g.hT)
        experts(g, h2, hot, g.hT, mod[:, 0:4 * D], gate2)
        write_out(g, out)


def build(nc, t, out):
    with ExitStack() as ctx:
        g = Program(nc, t, ctx)
        g.groups = weight_plan(t)
        prefetch_experts(g)
        constants(g)
        distance_tables(g)
        mod = first_block(g)
        second_block(g, out, mod)


_INS = ['x', 'mem', 'positions', 'g_mix', 'g_xattn', 'g_mem', 'g_mlp', 'wq_x', 'wkv_x', 'gq_x', 'gk_x', 'wo_x', 'w_up',
        'w_down', 'w_in_e', 'gq_a', 'gk_a', 'lam_q1', 'lam_k1', 'lam_q2', 'lam_k2', 'g_sub_a', 'g_kv_b', 'w_kv_up_b',
        'gq_b', 'gk_b', 'g_kidx', 'w_out_e', 'w_in_o', 'conv_w', 'w_pool', 'pool_scale', 'w_out_o', 'c_2', 'w_ada_2',
        'b_ada_2', 'norm1_g_2', 'w_in_2', 'conv_w_2', 'conv_b_2', 'w_q_blk_2', 'w_k_blk_2', 'w_v_blk_2', 'b_igate_2',
        'b_fgate_2', 'mlstm_norm_g_2', 'mlstm_skip_2', 'q_norm_g_2', 'k_norm_g_2', 'rel_bias_2', 'w_out_2',
        'norm2_g_2', 'w_router_2', 'b_router_2', 'w_gate_2', 'w_up_2', 'w_down_2']


def kernel(**inputs):
    import numpy as _np
    import concourse.bacc as _bacc
    from concourse import mybir as _mybir
    from concourse.bass_utils import run_bass_kernel_spmd as _run

    nc = _bacc.Bacc("TRN2", target_bir_lowering=False, num_devices=1)
    arrays, t = {}, {}
    for name in _INS:
        a = _np.ascontiguousarray(inputs[name])
        arrays[f"in_{name}"] = a
        t[name] = nc.dram_tensor(f"in_{name}", a.shape, _mybir.dt.from_np(a.dtype), kind="ExternalInput").ap()
    out = nc.dram_tensor("out", (1, SEQ, D), _mybir.dt.float32, kind="ExternalOutput").ap()
    for name, value in shape_constants().items():
        arrays[f"in_{name}"] = value
        t[name] = nc.dram_tensor(f"in_{name}", value.shape, _mybir.dt.float32, kind="ExternalInput").ap()
    build(nc, t, out)
    r = _run(nc, [arrays], core_ids=[0])
    return r.results[0]["out"]
```
